# Optimizing a Trainium2 kernel written in Bass

```python
import math
import numpy as np
import jax
import jax.numpy as jnp
from jax import lax

D_MODEL = 2048
BATCH = 1
SEQ = 256
DEPTH = 1
DEC_BATCH = 8
DEC_SEQ = 4
PAST_LEN = 2048
PAGE_SIZE = 128

N_BRANCH = 3
BRANCH_W = 3 * D_MODEL // 8
DK_A = 128
DV_A = 128
H_A = BRANCH_W // DV_A
CONV_W = 4
CHUNK_A = 64
DK_B = 64
DV_B = 128
H_B = BRANCH_W // DV_B
GLA_RANK = 16
GLA_NORMALIZER = 16.0
CHUNK_B = 16
N_C = 64
H_C = BRANCH_W // N_C
DECAY_LORA = 64
AAA_LORA = 64
GATE_LORA = 128
GN_EPS = 64e-5
D_FF = 5504
NORM_EPS = 1e-6

QKV_A = 2 * H_A * DK_A + H_A * DV_A
A_COLS = (QKV_A, H_A * DV_A, H_A, H_A)
B_COLS = (H_B * DK_B, H_B * DK_B, H_B * DV_B, H_B * DV_B, GLA_RANK)
C_COLS = (BRANCH_W, BRANCH_W, BRANCH_W, DECAY_LORA, AAA_LORA, GATE_LORA)
N_A = sum(A_COLS)
N_B = sum(B_COLS)
N_CC = sum(C_COLS)
N_GATE = N_BRANCH * D_MODEL
IN_COLS = (N_A, N_B, N_CC, N_GATE)
N_IN = sum(IN_COLS)

kernel_name = 'hybrid_gdn_gla_rwkv7_macaron_step'

def _split(x, sizes):
    return jnp.split(x, np.cumsum(sizes)[:-1].tolist(), axis=-1)

def _heads(x, h):
    return x.reshape(x.shape[:2] + (h, -1))

def _rmsnorm(x, g):
    xf = x.astype(jnp.float32)
    y = xf * lax.rsqrt(jnp.mean(xf * xf, axis=-1, keepdims=True) + NORM_EPS)
    return (y * g.astype(jnp.float32)).astype(x.dtype)

def _head_rmsnorm(o, g):
    return o * lax.rsqrt(jnp.mean(o * o, axis=-1, keepdims=True) + NORM_EPS) * g.astype(jnp.float32)

def _l2norm(x):
    return x * lax.rsqrt(jnp.sum(x * x, axis=-1, keepdims=True) + 1e-6)

def _swiglu(x, w_up, w_down):
    gate, up = jnp.split(x @ w_up, 2, axis=-1)
    return (jax.nn.silu(gate) * up) @ w_down

def _to_chunks(x, c):
    b, t = x.shape[:2]
    pad = (-t) % c
    x = jnp.pad(x, [(0, 0), (0, pad)] + [(0, 0)] * (x.ndim - 2))
    x = x.reshape((b, (t + pad) // c, c) + x.shape[2:])
    return jnp.moveaxis(x, 3, 1)

def _from_chunks(o, t):
    b, h, n, c, v = o.shape
    return jnp.moveaxis(o, 1, 3).reshape(b, n * c, h, v)[:, :t]

def _gated_delta_chunked(q, k, v, g, beta, s0):
    t = q.shape[1]
    c = min(CHUNK_A, t)
    q, k, v, g, beta = (_to_chunks(a, c) for a in (q, k, v, g, beta))
    gc = jnp.cumsum(g, axis=-1)
    causal = jnp.tril(jnp.ones((c, c), dtype=bool))
    strict = jnp.tril(jnp.ones((c, c), dtype=bool), -1)
    diff = gc[..., :, None] - gc[..., None, :]
    decay = jnp.where(causal, jnp.exp(jnp.where(causal, diff, 0.0)), 0.0)
    kb = k * beta[..., None]
    vb = v * beta[..., None]
    lower = jnp.where(strict, jnp.einsum('bhnik,bhnjk->bhnij', kb, k) * decay, 0.0)
    eye = jnp.eye(c, dtype=q.dtype)
    tmat = lax.linalg.triangular_solve(eye + lower, jnp.broadcast_to(eye, lower.shape),
                                       left_side=True, lower=True)
    u_base = tmat @ vb
    w_k = tmat @ (kb * jnp.exp(gc)[..., None])
    attn = jnp.einsum('bhnik,bhnjk->bhnij', q, k) * decay
    q_dec = q * jnp.exp(gc)[..., None]
    k_dec = k * jnp.exp(gc[..., -1:] - gc)[..., None]
    g_last = jnp.exp(gc[..., -1])

    def step(s, xs):
        u_b, wk, at, qd, kd, gl = xs
        u = u_b - jnp.einsum('bhck,bhkv->bhcv', wk, s)
        o = jnp.einsum('bhck,bhkv->bhcv', qd, s) + jnp.einsum('bhij,bhjv->bhiv', at, u)
        s = gl[..., None, None] * s + jnp.einsum('bhck,bhcv->bhkv', kd, u)
        return s, o

    xs = tuple(jnp.moveaxis(a, 2, 0) for a in (u_base, w_k, attn, q_dec, k_dec, g_last))
    s, o = lax.scan(step, s0, xs)
    return _from_chunks(jnp.moveaxis(o, 0, 2), t), s

def _gla_chunked(q, k, v, gk, s0):
    t = q.shape[1]
    c = min(CHUNK_B, t)
    q, k, v, gk = (_to_chunks(a, c) for a in (q, k, v, gk))
    bc = jnp.cumsum(gk, axis=-2)
    q_in = q * jnp.exp(bc)
    k_in = k * jnp.exp(-bc)
    causal = jnp.tril(jnp.ones((c, c), dtype=bool))
    attn = jnp.where(causal, jnp.einsum('bhnik,bhnjk->bhnij', q_in, k_in), 0.0)
    o_intra = attn @ v
    k_dec = k * jnp.exp(bc[..., -1:, :] - bc)
    a_last = jnp.exp(bc[..., -1, :])

    def step(s, xs):
        qi, kd, vv, al = xs
        o = jnp.einsum('bhck,bhkv->bhcv', qi, s)
        s = al[..., None] * s + jnp.einsum('bhck,bhcv->bhkv', kd, vv)
        return s, o

    xs = tuple(jnp.moveaxis(a, 2, 0) for a in (q_in, k_dec, v, a_last))
    s, o_inter = lax.scan(step, s0, xs)
    return _from_chunks(o_intra + jnp.moveaxis(o_inter, 0, 2), t), s

def _rwkv7_scan(r, w, k, v, a, b, s0):
    def step(s, xs):
        rt, wt, kt, vt, at, bt = xs
        sa = jnp.einsum('bhvk,bhk->bhv', s, at)
        s = s * wt[:, :, None, :] + sa[..., None] * bt[:, :, None, :] + vt[..., None] * kt[:, :, None, :]
        return s, jnp.einsum('bhvk,bhk->bhv', s, rt)

    xs = tuple(jnp.moveaxis(z, 1, 0) for z in (r, w, k, v, a, b))
    s, o = lax.scan(step, s0, xs)
    return jnp.moveaxis(o, 0, 1), s

def _mixer(xn, s_gdn, conv_buf, s_gla, s_rwkv, shift_buf, p):
    bsz, t, _ = xn.shape
    dt = xn.dtype
    f32 = jnp.float32
    pa, pb, pc, pg = _split(xn @ p['w_in'], IN_COLS)

    qkv, z_a, b_a, a_a = _split(pa, A_COLS)
    full = jnp.concatenate([conv_buf.astype(dt), qkv], axis=1)
    conv = sum(full[:, j:j + t] * p['conv_a'][j] for j in range(CONV_W))
    new_conv = full[:, t:]
    q_a, k_a, v_a = _split(jax.nn.silu(conv.astype(f32)), (H_A * DK_A, H_A * DK_A, H_A * DV_A))
    q_a = _l2norm(_heads(q_a, H_A)) * DK_A ** -0.5
    k_a = _l2norm(_heads(k_a, H_A))
    beta = jax.nn.sigmoid(b_a.astype(f32))
    g_a = -jnp.exp(p['a_log'].astype(f32)) * jax.nn.softplus(a_a.astype(f32) + p['dt_bias'].astype(f32))
    o_a, s_gdn = _gated_delta_chunked(q_a, k_a, _heads(v_a, H_A), g_a, beta, s_gdn.astype(f32))
    y_a = (_head_rmsnorm(o_a, p['gdn_norm']) * jax.nn.silu(_heads(z_a.astype(f32), H_A))).reshape(bsz, t, BRANCH_W)

    q_b, k_b, v_b, og_b, gk_low = _split(pb, B_COLS)
    gk = jax.nn.log_sigmoid((gk_low @ p['gla_gk_up'] + p['gla_gk_bias']).astype(f32)) / GLA_NORMALIZER
    o_b, s_gla = _gla_chunked(_heads(q_b.astype(f32), H_B) * DK_B ** -0.5, _heads(k_b.astype(f32), H_B),
                              _heads(v_b.astype(f32), H_B), _heads(gk, H_B), s_gla.astype(f32))
    y_b = (_head_rmsnorm(o_b, p['gla_norm']) * jax.nn.silu(_heads(og_b.astype(f32), H_B))).reshape(bsz, t, BRANCH_W)

    prev = jnp.concatenate([shift_buf.astype(dt), pc[:, :-1]], axis=1)
    new_shift = pc[:, t - 1:]
    xc = pc + (prev - pc) * p['rwkv_mu']
    r_c, k_c, v_c, w_low, a_low, g_low = _split(xc, C_COLS)
    w_log = -jax.nn.softplus(-(p['rwkv_w0'] + jnp.tanh(w_low) @ p['rwkv_w_up']).astype(f32)) - 0.5
    decay = jnp.exp(-jnp.exp(w_log))
    a_c = jax.nn.sigmoid((p['rwkv_a0'] + a_low @ p['rwkv_a_up']).astype(f32))
    g_c = (jax.nn.sigmoid(g_low) @ p['rwkv_g_up']).astype(f32)
    k_c = k_c.astype(f32)
    kk = _l2norm(_heads(k_c * p['rwkv_k_k'].astype(f32), H_C))
    k_c = _heads(k_c * (1.0 + (a_c - 1.0) * p['rwkv_k_a'].astype(f32)), H_C)
    r_c = _heads(r_c.astype(f32), H_C)
    v_c = _heads(v_c.astype(f32), H_C)
    o_c, s_rwkv = _rwkv7_scan(r_c, _heads(decay, H_C), k_c, v_c, -kk, kk * _heads(a_c, H_C), s_rwkv.astype(f32))
    mu = jnp.mean(o_c, axis=-1, keepdims=True)
    var = jnp.mean(jnp.square(o_c - mu), axis=-1, keepdims=True)
    o_c = ((o_c - mu) * lax.rsqrt(var + GN_EPS)).reshape(bsz, t, BRANCH_W) * p['rwkv_ln_w'].astype(f32) + p['rwkv_ln_b'].astype(f32)
    bonus = jnp.sum(r_c * k_c * p['rwkv_r_k'].astype(f32).reshape(H_C, N_C), axis=-1, keepdims=True) * v_c
    y_c = (o_c + bonus.reshape(bsz, t, BRANCH_W)) * g_c

    ys = jnp.stack([y_a, y_b, y_c], axis=2).astype(dt)
    gates = jax.nn.sigmoid(pg.astype(f32)).astype(dt).reshape(bsz, t, N_BRANCH, D_MODEL)
    merged = jnp.sum(gates * jnp.einsum('btnw,nwd->btnd', ys, p['w_branch']), axis=2)
    return merged @ p['w_out'], (s_gdn, new_conv, s_gla, s_rwkv, new_shift)

def _trunk(x, s_gdn, conv_buf, s_gla, s_rwkv, shift_buf, weights, norm_final):
    new = ([], [], [], [], [])
    for l in range(DEPTH):
        p = {name: arr[l] for name, arr in weights.items()}
        h = x + 0.5 * _swiglu(_rmsnorm(x, p['norm_ff1']), p['w_ff1_up'], p['w_ff1_down'])
        m, st = _mixer(_rmsnorm(h, p['norm_mix']), s_gdn[l], conv_buf[l], s_gla[l], s_rwkv[l], shift_buf[l], p)
        h = h + m
        x = h + 0.5 * _swiglu(_rmsnorm(h, p['norm_ff2']), p['w_ff2_up'], p['w_ff2_down'])
        for lst, s in zip(new, st):
            lst.append(s.astype(x.dtype))
    return (_rmsnorm(x, norm_final),) + tuple(jnp.stack(lst) for lst in new)

def setup_inputs(seed: int = 0) -> dict:
    key = jax.random.key(seed)
    ks = iter(jax.random.split(key, 48))
    f32 = jnp.float32
    L = DEPTH

    def nrm(shape, scale):
        return jax.random.normal(next(ks), shape, f32) * scale

    def gain(shape):
        return 1.0 + nrm(shape, 0.1)

    def unif(shape, lo, hi):
        return jax.random.uniform(next(ks), shape, f32, lo, hi)

    dt_init = jnp.exp(unif((L, H_A), math.log(1e-3), math.log(1e-1)))
    return {
        'x_prompt': nrm((BATCH, SEQ, D_MODEL), 1.0),
        'x_sample': nrm((DEC_BATCH, DEC_SEQ, D_MODEL), 1.0),
        'state_gdn': nrm((L, DEC_BATCH, H_A, DK_A, DV_A), 0.1),
        'state_gdn_conv': nrm((L, DEC_BATCH, CONV_W - 1, QKV_A), 1.0),
        'state_gla': nrm((L, DEC_BATCH, H_B, DK_B, DV_B), 1.0),
        'state_rwkv': nrm((L, DEC_BATCH, H_C, N_C, N_C), 0.5),
        'state_rwkv_shift': nrm((L, DEC_BATCH, 1, N_CC), 1.0),
        'w_in': nrm((L, D_MODEL, N_IN), D_MODEL ** -0.5),
        'conv_a': nrm((L, CONV_W, QKV_A), CONV_W ** -0.5),
        'a_log': jnp.log(unif((L, H_A), 1.0, 16.0)),
        'dt_bias': dt_init + jnp.log(-jnp.expm1(-dt_init)),
        'gdn_norm': gain((L, DV_A)),
        'gla_gk_up': nrm((L, GLA_RANK, H_B * DK_B), GLA_RANK ** -0.5),
        'gla_gk_bias': nrm((L, H_B * DK_B), 0.1),
        'gla_norm': gain((L, DV_B)),
        'rwkv_mu': unif((L, N_CC), 0.0, 1.0),
        'rwkv_w0': unif((L, BRANCH_W), -6.0, -1.0),
        'rwkv_w_up': nrm((L, DECAY_LORA, BRANCH_W), 0.5 * DECAY_LORA ** -0.5),
        'rwkv_a0': nrm((L, BRANCH_W), 0.1),
        'rwkv_a_up': nrm((L, AAA_LORA, BRANCH_W), AAA_LORA ** -0.5),
        'rwkv_g_up': nrm((L, GATE_LORA, BRANCH_W), GATE_LORA ** -0.5),
        'rwkv_k_k': 0.85 + nrm((L, BRANCH_W), 0.05),
        'rwkv_k_a': 1.0 + nrm((L, BRANCH_W), 0.05),
        'rwkv_r_k': nrm((L, BRANCH_W), 0.1),
        'rwkv_ln_w': gain((L, BRANCH_W)),
        'rwkv_ln_b': nrm((L, BRANCH_W), 0.01),
        'w_branch': nrm((L, N_BRANCH, BRANCH_W, D_MODEL), BRANCH_W ** -0.5),
        'w_out': nrm((L, D_MODEL, D_MODEL), D_MODEL ** -0.5),
        'norm_ff1': gain((L, D_MODEL)),
        'w_ff1_up': nrm((L, D_MODEL, 2 * D_FF), D_MODEL ** -0.5),
        'w_ff1_down': nrm((L, D_FF, D_MODEL), D_FF ** -0.5),
        'norm_mix': gain((L, D_MODEL)),
        'norm_ff2': gain((L, D_MODEL)),
        'w_ff2_up': nrm((L, D_MODEL, 2 * D_FF), D_MODEL ** -0.5),
        'w_ff2_down': nrm((L, D_FF, D_MODEL), D_FF ** -0.5),
        'norm_final': gain((D_MODEL,)),
    }

def reference(x_prompt, x_sample, state_gdn, state_gdn_conv, state_gla, state_rwkv, state_rwkv_shift,
              w_in, conv_a, a_log, dt_bias, gdn_norm, gla_gk_up, gla_gk_bias, gla_norm,
              rwkv_mu, rwkv_w0, rwkv_w_up, rwkv_a0, rwkv_a_up, rwkv_g_up, rwkv_k_k, rwkv_k_a, rwkv_r_k,
              rwkv_ln_w, rwkv_ln_b, w_branch, w_out, norm_ff1, w_ff1_up, w_ff1_down, norm_mix,
              norm_ff2, w_ff2_up, w_ff2_down, norm_final):
    weights = dict(w_in=w_in, conv_a=conv_a, a_log=a_log, dt_bias=dt_bias, gdn_norm=gdn_norm,
                   gla_gk_up=gla_gk_up, gla_gk_bias=gla_gk_bias, gla_norm=gla_norm,
                   rwkv_mu=rwkv_mu, rwkv_w0=rwkv_w0, rwkv_w_up=rwkv_w_up, rwkv_a0=rwkv_a0,
                   rwkv_a_up=rwkv_a_up, rwkv_g_up=rwkv_g_up, rwkv_k_k=rwkv_k_k, rwkv_k_a=rwkv_k_a,
                   rwkv_r_k=rwkv_r_k, rwkv_ln_w=rwkv_ln_w, rwkv_ln_b=rwkv_ln_b, w_branch=w_branch,
                   w_out=w_out, norm_ff1=norm_ff1, w_ff1_up=w_ff1_up, w_ff1_down=w_ff1_down,
                   norm_mix=norm_mix, norm_ff2=norm_ff2, w_ff2_up=w_ff2_up, w_ff2_down=w_ff2_down)

    def zeros_like_state(s):
        return jnp.zeros((DEPTH, BATCH) + s.shape[2:], x_prompt.dtype)

    y_prompt, gdn_p, conv_p, gla_p, rwkv_p, shift_p = _trunk(
        x_prompt, zeros_like_state(state_gdn), zeros_like_state(state_gdn_conv), zeros_like_state(state_gla),
        zeros_like_state(state_rwkv), zeros_like_state(state_rwkv_shift), weights, norm_final)
    y_sample, gdn_s, conv_s, gla_s, rwkv_s, shift_s = _trunk(
        x_sample, state_gdn, state_gdn_conv, state_gla, state_rwkv, state_rwkv_shift, weights, norm_final)
    return (y_prompt, y_sample, gdn_p, gdn_s, conv_p, conv_s, gla_p, gla_s, rwkv_p, rwkv_s, shift_p, shift_s)


_drawn_inputs = setup_inputs


def setup_inputs(seed=0):
    import zlib

    import numpy as np

    out = dict(_drawn_inputs(seed))
    spreads = {}
    factors = {'rwkv_ln_b': 8.0}
    for name, (base, spread) in spreads.items():
        noise = np.random.default_rng([zlib.crc32(name.encode()), seed]).standard_normal(out[name].shape)
        drawn = base * np.exp(spread * noise) if base else spread * noise
        out[name] = jnp.asarray(drawn.astype(out[name].dtype))
    for name, factor in factors.items():
        out[name] = (out[name] * factor).astype(out[name].dtype)
    return out
```

```python
import math
from contextlib import ExitStack

import concourse.bass as bass
from concourse import mybir

F32 = mybir.dt.float32
F32R = mybir.dt.float32r
ALU = mybir.AluOpType
ACT = mybir.ActivationFunctionType
ADD, SUB, MUL = ALU.add, ALU.subtract, ALU.mult

P = 128
D = 2048
KD = D // P
TP, NSEQ, TS = 256, 8, 4
NT = TP + NSEQ * TS
FF = 5504
FT = FF // P
HALVES = (22, 21)
BW = 768
BT = BW // P
RANK, DLORA = 16, 64
N_A, N_B, N_C = 3084, 2320, 2560
COL_BA, COL_B, COL_LOW, COL_C = 3072, N_A, N_A + 2304, N_A + N_B
COL_GATE = N_A + N_B + N_C
EPS = 1e-6
GN_EPS = 64e-5
CP, CS = 32, TS
BLOCKS = ((0, 128, CP), (128, 128, CP), (256, 32, CS))
GAP = 3
SEQW = TP + GAP
PW = SEQW + NSEQ * (TS + GAP)
CW = (TP // CP) * (CP + 1) + NSEQ * (CS + 1)
RING = 4
SLOT = 1024
AHEAD = 2

R_FF1, R_MIX, R_FF2, R_FIN, R_MU, R_W0, R_A0, R_KK, R_KA, R_RK, R_LNW, R_LNB, R_GDN, R_GLA = (
    0, 16, 32, 48, 64, 84, 90, 96, 102, 108, 114, 120, 126, 127)
R_BIAS = 72


def plan():
    ph = []

    def add(name, per_body, times, groups):
        ph.append(dict(name=name, n=per_body, times=times, groups=groups))

    def ff(f):
        for h, tiles in enumerate(HALVES):
            add(f"up{f}{h}", 8, tiles // 2, 2)
            if tiles % 2:
                add(f"up{f}{h}t", 4, 1, 1)
            add(f"down{f}{h}", tiles, 2, 4)

    ff(0)
    add("low", 4, 1, 1)
    add("inC", 8, 5, 2)
    add("inA", 8, 6, 2)
    add("inB", 8, 4, 2)
    add("inBt", 4, 1, 1)
    add("branch", 36, 4, 6)
    add("out", 8, 4, 2)
    ff(1)
    use, group = [0] * RING, 2
    for p in ph:
        p["base"] = list(use)
        p["per"] = [len(range(q, p["n"], RING)) for q in range(RING)]
        p["group0"] = group
        use = [u + p["times"] * c for u, c in zip(use, p["per"])]
        group += p["times"] * p["groups"]
    return {p["name"]: p for p in ph}


PLAN = plan()
ORDER = list(PLAN)


def build(nc, i, o):
    ctx = ExitStack()
    with ctx:
        base = (nc.sbuf_base + 63) // 64 * 64

        class Map:

            def __init__(self, at, end):
                self.at, self.end = (at + 31) // 32 * 32, end

            def __call__(self, name, shape, dt=F32):
                t = nc.alloc_sbuf_tensor_at(name, shape, dt, offset=self.at)
                n = 4
                for s in shape[1:]:
                    n *= s
                self.at += (n + 31) // 32 * 32
                assert self.at <= self.end, (name, self.at, self.end)
                return t

        fixed = Map(base, nc.sbuf_usable_end)
        x = fixed("x", [P, KD, NT])
        xh = fixed("xh", [P, KD, NT], F32R)
        xl = fixed("xl", [P, KD, NT], F32R)
        raw = fixed("raw", [P, RING, SLOT])
        hi = fixed("hi", [P, RING, SLOT], F32R)
        lo = fixed("lo", [P, RING, SLOT], F32R)
        ident = fixed("ident", [P, P])
        ones = fixed("ones", [P, P])
        ones64 = fixed("ones64", [P, P])
        par1 = fixed("par1", [P, P])
        par2 = fixed("par2", [P, 75])
        low = fixed("low", [P, 2, NT])
        mk = []
        for w, c in ((P, CP), (32, CS)):
            mk.append({k: fixed(f"mask_{k}{w}", [w, w]) for k in
                       ("ui",
                        "us",
                        "same",
                        "l16",
                        "off")})
        seqmask = fixed("seqmask", [32, NSEQ])
        notlead = fixed("notlead", [P, CW])
        smA = fixed("smA", [P, 2, 6])
        arena0 = fixed.at
        y_at = nc.sbuf_usable_end // 64 * 64 - 3 * BT * NT * 4

        hid = Map(arena0, y_at)
        hidh = hid("hidh", [P, HALVES[0], NT], F32R)
        hidl = hid("hidl", [P, HALVES[0], NT], F32R)
        stage = Map(arena0, nc.sbuf_usable_end)
        xrow = stage("xrow", [P, 3, D])
        prow = stage("prow", [P, 2, P])
        ymap = Map(y_at, nc.sbuf_usable_end)
        ybuf = ymap("ybuf", [P, 3 * BT, NT])
        YB, YA, YC = 0, BT, 2 * BT
        ysp = Map(arena0, y_at)
        yh = ysp("yh", [P, 3 * BT, NT], F32R)
        yl = ysp("yl", [P, 3 * BT, NT], F32R)
        mmap = Map(y_at, nc.sbuf_usable_end)
        merged = mmap("merged", [P, KD, NT])
        tmp = Map(hid.at, y_at)
        work = tmp("work", [P, 2, NT])
        prodt = tmp("prodt", [P, 2, NT])
        sq = tmp("sq", [P, 2, NT])
        rstd = tmp("rstd", [P, NT])
        normed = tmp("normed", [P, 2, NT])

        ps = ctx.enter_context(nc.psum_tensor("ps", [P, 8, 512], F32))

        sems = {}

        def sem(name):
            if name not in sems:
                sems[name] = ctx.enter_context(nc.semaphore(name))
            return sems[name]

        landed = [sem(f"landed{q}") for q in range(RING)]
        hi_ready = [sem(f"hi_ready{q}") for q in range(RING)]
        lo_ready = [sem(f"lo_ready{q}") for q in range(RING)]
        multiplied = [sem(f"multiplied{q}") for q in range(RING)]
        acc_empty = sem("acc_empty")
        gate_ready = sem("gate_ready")
        hid_hi, hid_lo = sem("hid_hi"), sem("hid_lo")

        w_in = i["w_in"][0].rearrange("(k p) n -> p k n", p=P)
        w_up = [i[n][0].rearrange("(k p) (c n) -> p k c n", p=P, c=2) for n in ("w_ff1_up", "w_ff2_up")]
        w_down = [i[n][0].rearrange("(k p) n -> p k n", p=P) for n in ("w_ff1_down", "w_ff2_down")]
        w_branch = i["w_branch"][0].rearrange("b (k p) n -> p b k n", p=P)
        w_out = i["w_out"][0].rearrange("(k p) n -> p k n", p=P)
        w_low = i["w_in"][0][:, COL_BA:COL_BA + 2 * (COL_LOW - COL_BA)].rearrange(
            "(k p) (c n) -> p k c n", p=P, c=2)

        def source(name, s, it):
            if name.startswith("up"):
                f, h = int(name[2]), int(name[3])
                m = h * HALVES[0] + (HALVES[h] - 1 if name.endswith("t") else 2 * it + s // 4)
                return w_up[f][:, 4 * (s % 4):4 * (s % 4) + 4, :, bass.ds(m * P, P)], 4
            if name.startswith("down"):
                f, h = int(name[4]), int(name[5])
                return it * 1024, 1
            if name == "low":
                return w_low[:, 4 * s:4 * s + 4, :, 0:P], 4
            k = 4 * (s % 4)
            if name.startswith("in"):
                g = 8 if name.endswith("t") else 2 * it + s // 4
                c0 = {"A": 0, "B": COL_B, "C": COL_C}[name[2]]
                return w_in[:, k:k + 4, bass.ds(g * 256 + c0, 256)], 4
            if name == "out":
                return w_out[:, k:k + 4, bass.ds((2 * it + s // 4) * 256, 256)], 4
            pair, n, r = s // 18, s // 6 % 3, s % 6
            if r < 4:
                return w_in[:, 4 * r:4 * r + 4, bass.ds((2 * it + pair) * 256 + COL_GATE + n * D, 256)], 4
            return w_branch[:, n, 3 * (r - 4):3 * (r - 4) + 3, bass.ds((2 * it + pair) * 256, 256)], 3

        def use(p, s, it):
            q = s % RING
            return it * p["per"][q] + (p["base"][q] + s // RING)

        def ahead(p, s, it):
            s += AHEAD
            if s < p["n"]:
                return s % RING, use(p, s, it)
            s -= p["n"]
            return s, it * p["per"][s] + (p["base"][s] + p["per"][s])

        def turns(eng, p, body, unrolled=False):
            if p["times"] == 1 or unrolled:
                for it in range(p["times"]):
                    body(it)
            else:
                with eng.Fori(0, p["times"]) as it:
                    body(it)

        LAST = ORDER[-1]

        def sp_program(sp):
            for b, (t0, n, _) in enumerate(BLOCKS):
                src = i["x_prompt"][0][t0:t0 + n] if b < 2 else i["x_sample"].rearrange("b t d -> (b t) d")
                sp.dma_start(xrow[0:n, b, :], src).then_inc(sem("x_landed"), 16)
            for name in ORDER:
                p = PLAN[name]

                def body(it):
                    for s in range(p["n"]):
                        q = s % RING
                        src, kk = source(name, s, it)
                        if kk > 1 and len(src.shape) == 4:
                            dst = raw[:, q, :].rearrange("p (k c n) -> p k c n", k=kk, c=2)
                            parts = [(dst[:, :, c, :], src[:, :, c, :]) for c in range(2)]
                        elif kk == 1:
                            f, h = int(name[4]), int(name[5])
                            parts = [(raw[:, q, c:c + 512],
                                      w_down[f][:, h * HALVES[0] + s, bass.ds(it * 1024 + c, 512)])
                                     for c in (0, 512)]
                        else:
                            dst = raw[:, q, 0:kk * 256].rearrange("p (k n) -> p k n", k=kk)
                            parts = [(dst[:, a:b, :], src[:, a:b, :]) for a, b in ((kk // 2, kk), (0, kk // 2))]
                        sp.wait_ge(lo_ready[q], use(p, s, it) + 1)
                        for dst, src in parts:
                            sp.dma_start(dst, src).then_inc(landed[q], 16)

                turns(sp, p, body)
            for b, (t0, n, _) in enumerate(BLOCKS):
                dst = o["y_prompt"][0][t0:t0 + n] if b < 2 else o["y_sample"].rearrange("b t d -> (b t) d")
                sp.wait_ge(sem("rows_out"), 4 * (b + 1))
                sp.dma_start(dst, xrow[0:n, b, :]).then_inc(sem("stored"), 16)
            sp.wait_ge(sem("stored"), 48)

        def pe_program(pe):
            def three(out, q, col, rh, rl, start, stop):
                w, wl = hi[:, q, col:col + P], lo[:, q, col:col + P]
                pe.matmul(out, w, rh, start=start, stop=False)
                pe.matmul(out, w, rl, start=False, stop=False)
                return pe.matmul(out, wl, rh, start=False, stop=stop)

            def phase(name):
                p = PLAN[name]
                down, br = name.startswith("down"), name == "branch"
                pe.wait_ge(acc_empty, p["group0"])

                def body(it):
                    for s in range(p["n"]):
                        q = s % RING
                        pe.wait_ge(lo_ready[q], use(p, s, it) + 2)
                        if down:
                            for m in range(8):
                                g = it * 4 + (p["group0"] + m // 2)
                                if s == 0 and m % 2 == 0:
                                    pe.wait_ge(acc_empty, g - 3)
                                mm = three(ps[:, m, 0:NT], q, m * P, hidh[:, s, :], hidl[:, s, :],
                                           s == 0, s == p["n"] - 1)
                            mm.then_inc(multiplied[q], 1)
                            continue
                        size = 6 if br else 4
                        g, r = s // size, s % size
                        G = it * p["groups"] + (p["group0"] + g)
                        if r == 0:
                            pe.wait_ge(acc_empty, G - 1)
                        if br and r >= 4:
                            y0 = (YA, YB, YC)[g % 3] + 3 * (r - 4)
                            for k in range(3):
                                for c in range(2):
                                    mm = three(ps[:, g % 2 * 4 + 2 + c, 0:NT], q, (2 * k + c) * P,
                                               yh[:, y0 + k, :], yl[:, y0 + k, :],
                                               r == 4 and k == 0, r == 5 and k == 2)
                        else:
                            for k in range(4):
                                for c in range(2):
                                    mm = three(ps[:, g % 2 * (4 if br else 2) + c, 0:NT], q,
                                               (2 * k + c) * P, xh[:, 4 * r + k, :], xl[:, 4 * r + k, :],
                                               r == 0 and k == 0, r == 3 and k == 3)
                        mm.then_inc(multiplied[q], 1)

                turns(pe, p, body)

            pe_setup(pe)
            for name in ORDER:
                if name in ("up00", "low", "up10"):
                    n = ("up00", "low", "up10").index(name)
                    pe_norm(pe, n)
                    pe.wait_ge(sem("xn_ready"), KD * (n + 1))
                if name == "out":
                    pe.wait_ge(sem("merged_ready"), KD)
                if name in ("inA", "inB", "branch"):
                    pe.wait_ge(sem("mixer_done"), ("inA", "inB", "branch").index(name) + 1)
                if name.startswith("down"):
                    pe.wait_ge(hid_lo, hidden_before(name))
                phase(name)
                if name == "inC":
                    pe_mixC(pe)
                if name == "inA":
                    pe_mixA(pe)
                if name == "inBt":
                    pe_mixB(pe)
            pe_norm(pe, 3)
            for b, (t0, n, _) in enumerate(BLOCKS):
                for kq in range(4):
                    r = 4 * b + kq
                    pe.wait_ge(sem("final_ready"), 4 * (kq + 1))
                    if r >= 4:
                        pe.wait_ge(sem("rows_out"), r - 3)
                    for k in range(4):
                        mm = pe.transpose(ps[0:n, 4 + r % 4, k * P:(k + 1) * P],
                                          x[:, 4 * kq + k, t0:t0 + n], ident[:, :])
                    mm.then_inc(sem("final_turned"), 1)

        def hidden_before(name):
            f, h = int(name[4]), int(name[5])
            return f * FT + (HALVES[0] if h == 0 else FT)

        def pe_setup(pe):
            for q in range(RING):
                pe.nop().then_inc(multiplied[q], 1)
            pe.wait_ge(sem("consts"), 1)
            pe.wait_ge(sem("prow_landed"), PROWS * 16)
            pe.transpose(ps[:, 0, 0:P], prow[:, 0, :], ident[:, :])
            pe.transpose(ps[:, 1, 0:75], prow[0:75, 1, :], ident[0:75, 0:75]).then_inc(sem("par_turned"), 1)
            pe.wait_ge(sem("x_landed"), 48)
            for b, (t0, n, _) in enumerate(BLOCKS):
                for kq in range(4):
                    r = 4 * b + kq
                    if r >= 4:
                        pe.wait_ge(sem("x_copied"), r - 3)
                    for k in range(4):
                        mm = pe.transpose(ps[:, 2 + r % 4, k * P:k * P + n],
                                          xrow[0:n, b, (4 * kq + k) * P:(4 * kq + k + 1) * P],
                                          ident[0:n, 0:n])
                    mm.then_inc(sem("x_turned"), 1)

        def pe_norm(pe, n):
            for k in range(KD):
                pe.wait_ge(sem("sq_ready"), n * KD + k + 1)
                pe.matmul(ps[:, 7, 0:NT], ones[:, :], sq[:, k % 2, :], start=k == 0,
                          stop=k == KD - 1).then_inc(sem("sq_used"), 1)

        def act_program(act):
            def split(place):
                q, u = place
                act.wait_ge(landed[q], (u + 1) * 32)
                act.wait_ge(multiplied[q], u + 1)
                act.activation(hi[:, q, :], raw[:, q, :], ACT.Copy).then_inc(hi_ready[q], 1)

            def phase(name):
                p = PLAN[name]
                size = {"up": 4, "do": p["n"], "br": 6}.get(name[0:2], 4)

                def body(it):
                    for s in range(p["n"]):
                        q = s % RING
                        if not (name == LAST and it == 1 and s + AHEAD >= p["n"]):
                            split(ahead(p, s, it))
                        if (s + 1) % size:
                            continue
                        g = s // size
                        G = it * p["groups"] + (p["group0"] + g)
                        if name.startswith("up"):
                            act.wait_ge(multiplied[q], use(p, s, it) + 2)
                            act.activation(work[:, 0, :], ps[:, g % 2 * 2, 0:NT],
                                           ACT.Silu).then_inc(gate_ready, 1)
                            act.wait_ge(acc_empty, G + 1)
                            m = HALVES[int(name[3])] - 1 if name.endswith("t") else it * 2 + g
                            act.activation(hidh[:, bass.ds(m, 1), :], prodt[:, 0:1, :],
                                           ACT.Copy).then_inc(hid_hi, 1)
                        if name == "branch":
                            act.wait_ge(multiplied[q], use(p, s, it) + 2)
                            act.wait_ge(acc_empty, G)
                            act.activation(work[:, :, :], ps[:, g % 2 * 4:g % 2 * 4 + 2, 0:NT],
                                           ACT.Sigmoid).then_inc(gate_ready, 1)

                turns(act, p, body, name == LAST)

            act_setup(act)
            for s in range(AHEAD):
                split((s, 0))
            act_norm(act, 0)
            for name in ORDER:
                if name == "low":
                    act_norm(act, 1)
                if name == "up10":
                    act_norm(act, 2)
                if name == "out":
                    act.wait_ge(sem("gated"), 2 * KD // 2)
                    act_split(act, merged, xh, KD, sem("merged_hi"))
                phase(name)
                if name == "inC":
                    act_mixC(act)
                if name == "inA":
                    act_mixA(act)
                if name == "inBt":
                    act_mixB(act)
            act_norm(act, 3)

        def act_split(act, src, dst, n, done):
            for k in range(n):
                act.activation(dst[:, k, :], src[:, k, :], ACT.Copy).then_inc(done, 1)

        def act_setup(act):
            pass

        def act_norm(act, n):
            groups = (2, PLAN["low"]["group0"], PLAN["up10"]["group0"],
                      PLAN[LAST]["group0"] + 8)[n]
            act.wait_ge(acc_empty, groups)
            if n == 0:
                act.wait_ge(sem("x_copied"), 12)
            for k in range(KD):
                if n or k > 1:
                    act.wait_ge(sem("sq_used"), n * KD + k - 1)
                act.activation(sq[:, k % 2, :], x[:, k, :], ACT.Square).then_inc(sem("sq_ready"), 1)
            act.wait_ge(sem("ms_ready"), n + 1)
            act.activation(rstd[:, :], rstd[:, :], ACT.Sqrt).then_inc(sem("root_ready"), 1)
            if n == 3:
                return
            for k in range(KD):
                act.wait_ge(sem("normed_ready"), n * KD + k + 1)
                act.activation(xh[:, k, :], normed[:, k % 2, :], ACT.Copy).then_inc(sem("xn_hi"), 1)

        def dve_program(dve):
            def split(place):
                q, u = place
                dve.wait_ge(hi_ready[q], u + 1)
                dve.tensor_tensor(lo[:, q, :], raw[:, q, :], hi[:, q, :].bitcast(F32),
                                  SUB).then_inc(lo_ready[q], 1)

            def phase(name):
                p = PLAN[name]
                size = {"up": 4, "do": p["n"], "br": 6}.get(name[0:2], 4)

                def body(it):
                    for s in range(p["n"]):
                        q = s % RING
                        if not (name == LAST and it == 1 and s + AHEAD >= p["n"]):
                            split(ahead(p, s, it))
                        if (s + 1) % size:
                            continue
                        g = s // size
                        G = it * p["groups"] + (p["group0"] + g)
                        if name.startswith("up"):
                            f, h = int(name[2]), int(name[3])
                            m = HALVES[h] - 1 if name.endswith("t") else it * 2 + g
                            F = f * FT + h * HALVES[0] + m
                            dve.wait_ge(multiplied[q], use(p, s, it) + 2)
                            dve.wait_ge(gate_ready, F + (24 * f + 1))
                            dve.tensor_tensor(prodt[:, 0, :], work[:, 0, :], ps[:, g % 2 * 2 + 1, 0:NT],
                                              MUL).then_inc(acc_empty, 1)
                            dve.wait_ge(hid_hi, F + 1)
                            dve.tensor_tensor(hidl[:, bass.ds(m, 1), :], prodt[:, 0:1, :],
                                              hidh[:, bass.ds(m, 1), :].bitcast(F32),
                                              SUB).then_inc(hid_lo, 1)
                        elif name.startswith("down"):
                            dve.wait_ge(multiplied[q], use(p, s, it) + 2)
                            for j in range(4):
                                xx = x[:, bass.ds(it * 8 + 2 * j, 2), :]
                                dve.scalar_tensor_tensor(xx, ps[:, 2 * j:2 * j + 2, 0:NT], 0.5, xx,
                                                         MUL, ADD).then_inc(acc_empty, 1)
                        elif name == "out":
                            dve.wait_ge(multiplied[q], use(p, s, it) + 2)
                            xx = x[:, bass.ds((it * 2 + g) * 2, 2), :]
                            dve.tensor_tensor(xx, ps[:, g % 2 * 2:g % 2 * 2 + 2, 0:NT], xx,
                                              ADD).then_inc(acc_empty, 1)
                        elif name == "low":
                            dve.wait_ge(multiplied[q], use(p, s, it) + 2)
                            dve.tensor_copy(low[:, :, :], ps[:, 0:2, 0:NT]).then_inc(acc_empty, 1)
                        elif name.startswith("in"):
                            m = 16 if name.endswith("t") else (it * 2 + g) * 2
                            dve.wait_ge(multiplied[q], use(p, s, it) + 2)
                            b = g % 2 * 2
                            if name[2] == "B":
                                dve.tensor_copy(proj[:, bass.ds(m, 2), 0:NT],
                                                ps[:, b:b + 2, 0:NT]).then_inc(acc_empty, 1)
                            else:
                                dve.tensor_copy(proj[:, bass.ds(m, 2), GAP:SEQW], ps[:, b:b + 2, 0:TP])
                                for c in range(2):
                                    cp = dve.tensor_copy(
                                        proj[:, bass.ds(m + c, 1), SEQW:PW].rearrange(
                                            "p o (b t) -> p (o b) t", t=GAP + TS)[:, :, GAP:],
                                        ps[:, b + c, TP:NT].rearrange("p (b t) -> p b t", t=TS))
                                cp.then_inc(acc_empty, 1)
                        elif name == "branch":
                            n, m = g % 3, (it * 2 + g // 3) * 2
                            dve.wait_ge(gate_ready, it * 6 + (FT + g + 1))
                            br = ps[:, g % 2 * 4 + 2:g % 2 * 4 + 4, 0:NT]
                            if n == 0:
                                dve.tensor_tensor(merged[:, bass.ds(m, 2), :], work[:, :, :], br,
                                                  MUL).then_inc(acc_empty, 1)
                            else:
                                dve.tensor_tensor(prodt[:, :, :], work[:, :, :], br,
                                                  MUL).then_inc(acc_empty, 1)
                                dve.wait_ge(acc_empty, G + 1)
                                mm = merged[:, bass.ds(m, 2), :]
                                dve.tensor_tensor(mm, mm, prodt[:, :, :], ADD).then_inc(sem("gated"), 1)

                turns(dve, p, body, name == LAST)

            dve_setup(dve)
            for s in range(AHEAD):
                split((s, 0))
            dve_norm(dve, 0)
            for name in ORDER:
                if name == "low":
                    dve_norm(dve, 1)
                if name == "up10":
                    dve_norm(dve, 2)
                if name == "out":
                    for k in range(KD):
                        dve.wait_ge(sem("merged_hi"), k + 1)
                        dve.tensor_tensor(xl[:, k, :], merged[:, k, :], xh[:, k, :].bitcast(F32),
                                          SUB).then_inc(sem("merged_ready"), 1)
                phase(name)
                if name == "inC":
                    dve_mixC(dve)
                if name == "inA":
                    dve_mixA(dve)
                if name == "inBt":
                    dve_mixB(dve)
            dve_norm(dve, 3)
            for b, (t0, n, _) in enumerate(BLOCKS):
                for kq in range(4):
                    r = 4 * b + kq
                    dve.wait_ge(sem("final_turned"), r + 1)
                    dve.tensor_copy(xrow[0:n, b, kq * 512:(kq + 1) * 512],
                                    ps[0:n, 4 + r % 4, :]).then_inc(sem("rows_out"), 1)

        def dve_setup(dve):
            for q in range(RING):
                dve.nop().then_inc(lo_ready[q], 1)
            dve.wait_ge(sem("par_turned"), 1)
            dve.tensor_copy(par1[:, :], ps[:, 0, 0:P]).then_inc(acc_empty, 1)
            dve.tensor_copy(par2[:, :], ps[:, 1, 0:75]).then_inc(acc_empty, 1)
            for b, (t0, n, _) in enumerate(BLOCKS):
                for kq in range(4):
                    r = 4 * b + kq
                    dve.wait_ge(sem("x_turned"), r + 1)
                    dve.tensor_copy(x[:, 4 * kq:4 * kq + 4, t0:t0 + n],
                                    ps[:, 2 + r % 4, :].rearrange("p (k t) -> p k t", k=4)[:, :, 0:n]
                                    ).then_inc(sem("x_copied"), 1)

        def dve_norm(dve, n):
            dve.wait_ge(sem("sq_used"), KD * (n + 1))
            dve.tensor_scalar(rstd[:, :], ps[:, 7, 0:NT], 1.0 / D, EPS, MUL, ADD).then_inc(sem("ms_ready"), 1)
            dve.wait_ge(sem("root_ready"), n + 1)
            dve.reciprocal(rstd[:, :], rstd[:, :]).then_inc(sem("rstd_ready"), 1)
            dve.wait_ge(sem("rstd_ready"), n + 1)
            gain = (R_FF1, R_MIX, R_FF2, R_FIN)[n]
            for k in range(KD):
                if n == 3:
                    dve.scalar_tensor_tensor(x[:, k, :], x[:, k, :], par1[:, gain + k:gain + k + 1],
                                             rstd[:, :], MUL, MUL).then_inc(sem("final_ready"), 1)
                    continue
                if k > 1:
                    dve.wait_ge(sem("xn_ready"), n * KD + k - 1)
                dve.scalar_tensor_tensor(normed[:, k % 2, :], x[:, k, :], par1[:, gain + k:gain + k + 1],
                                         rstd[:, :], MUL, MUL).then_inc(sem("normed_ready"), 1)
                if k:
                    xn_low(dve, n, k - 1)
            if n < 3:
                xn_low(dve, n, KD - 1)

        def xn_low(dve, n, k):
            dve.wait_ge(sem("xn_hi"), n * KD + k + 1)
            dve.tensor_tensor(xl[:, k, :], normed[:, k % 2, :], xh[:, k, :].bitcast(F32),
                              SUB).then_inc(sem("xn_ready"), 1)

        class Steps:
            def __init__(self, eng, name):
                self.eng, self.name, self.n, self.done, self.needed = eng, name, 0, {}, {}

            def link(self, ins):
                self.n += 1
                ins.then_inc(sem(self.name), 1)
                self.eng.wait_ge(sem(self.name), self.n)

            def mark(self, ins, step):
                self.done[step] = self.done.get(step, 0) + 1
                ins.then_inc(sem(step), 1)
                if self.name != "pe_chain":
                    self.eng.wait_ge(sem(step), self.done[step])

            def need(self, step, by=1):
                self.needed[step] = self.needed.get(step, 0) + by
                self.eng.wait_ge(sem(step), self.needed[step])

        steps = {}

        def on(eng, name):
            if name not in steps:
                steps[name] = Steps(eng, name)
            return steps[name]

        y_c = y_at + YC * NT * 4
        y_a = y_at + YA * NT * 4
        proj = Map(arena0, y_c)("proj", [P, 24, PW])
        NEG = -math.exp(-0.5)

        def kind(b):
            t0, n, c = BLOCKS[b]
            return mk[b // 2], n, c, n // c, t0, (0, 4 * (CP + 1), 8 * (CP + 1))[b]

        mapC = Map(arena0 + 20 * PW * 4, y_c)
        csC = mapC("csC", [P, BT, CW])
        kkC = mapC("kkC", [P, BT, NT])
        bbC = mapC("bbC", [P, BT, NT])
        startC = mapC.at

        def recur_tiles(m, n, tag, ft, last):
            t = {}
            for k in ("m16", "off", "mt", "m2", "m2t", "tt"):
                t[k] = m(f"{k}{tag}", [P, 6, n])
            for k in last:
                t[k] = m(f"{k}{tag}", [P, 6, n])
            return t

        def maps_C(n, tag):
            m = Map(startC, y_c)
            t = recur_tiles(m, n, tag, 3, ("nt", "qb", "qk"))
            if n == P:
                f = Map(startC + 3 * 6 * n * 4, y_c)
            else:
                f = m
            for k in ("ri", "ki", "bi", "ai"):
                t[k] = f(k + tag, [P, 3, n])
            f2 = Map(startC + 5 * 6 * n * 4, y_c) if n == P else m
            t["dm"] = f2("dm" + tag, [P, 3, n])
            for k in ("kl", "bl", "rr", "aa"):
                t[k] = m(k + tag, [P, 3, n])
            for k in ("klT", "blT", "aT", "vT"):
                t[k] = m(k + tag, [P, 3, P])
            if n == P:
                f = Map(startC, y_c)
            for k in ("w", "zb", "nv", "z"):
                t[k] = (f if n == P else m)(k + tag, [P, 3, P])
            t["pl"] = m("pl" + tag, [P, 3, 8])
            if n == P:
                t["s"] = m("sC", [P, 2, 3, P])
                t["so"] = f("soC", [P, 3, 64])
            else:
                t["sd"] = m("sdC", [P, NSEQ, P])
                t["s0"] = m("s0C", [P, NSEQ, P])
                t["um"] = m("umC", [32, NSEQ, P])
                t["vm"] = m("vmC", [32, NSEQ, P])
                t["zT"] = m("zTC", [P, 32])
                t["so8"] = m("so8C", [P, NSEQ, 64])
            return t

        preC = Map(startC, y_c)
        wloraC = preC("wloraC", [P, BW])
        gupC = Map(y_c - BW * 4 - 64, y_c)("gupC", [P, BW])
        srowC = preC("srowC", [9, N_C])
        slastC = preC("slastC", [P, 20, 9])
        shA = preC("shA", [P, 2, PW])
        shB = preC("shB", [P, 2, PW])
        sgw = preC("sgw", [P, 2, NT])
        padC = preC("padC", [P, CW])
        sqC = Map(startC, y_c)("sqC", [P, BT, NT])
        tC = [maps_C(P, "Cp"), maps_C(32, "Cs")]
        finC = Map(startC, y_c)
        sqF = finC("sqF", [P, BT, NT])
        rsF = finC("rsF", [P, BT, NT])

        psf = ps[:, :, :].rearrange("p a b -> p (a b)")

        def region(r, n, m, rows=None):
            rows = slice(0, n) if rows is None else rows
            return psf[rows, r * 1024:(r + 1) * 1024].rearrange("p (h t) -> p h t", t=P)[:, 0:6, 0:m]

        def cell(r, q, n, m):
            return ps[0:n, 2 * r + q // 4, q % 4 * P:q % 4 * P + m]

        def parity(r, par, n, m):
            return ps[0:n, 2 * r + par, :].rearrange("p (h t) -> p h t", t=P)[:, 0:3, 0:m]

        def bc(ap, axis, size):
            ap = ap.unsqueeze(axis)
            shape = list(ap.shape)
            shape[axis] = size
            return ap.to_broadcast(shape)

        def pe_solve(pe, t, n):
            e = on(pe, "pe_chain")
            I = ident[0:n, 0:n]
            for q in range(6):
                mm = pe.transpose(cell(2, q, n, n), t["m16"][0:n, q, :], I)
            e.mark(mm, "so_mt")
            e.need("so_mt_kept")

            def square(a, at, second=True):
                for q in range(6):
                    mm = pe.matmul(cell(0, q, n, n), t[at][0:n, q, :], t[a][0:n, q, :], start=True, stop=True)
                if second:
                    for q in range(6):
                        mm = pe.matmul(cell(1, q, n, n), t[a][0:n, q, :], t[at][0:n, q, :], start=True, stop=True)
                return mm

            def extend(a):
                for q in range(6):
                    mm = pe.matmul(cell(2, q, n, n), t[a][0:n, q, :], t["tt"][0:n, q, :], start=True, stop=True)
                return mm

            e.mark(square("m16", "mt", n == P), "so_sq")
            e.need("so_sq_kept")
            if n < P:
                e.mark(extend("m2"), "so_ex")
                e.need("so_ex_kept")
                return
            square("m2", "m2t")
            e.mark(extend("m2"), "so_sq")
            e.need("so_sq_kept")
            square("m16", "mt", False)
            e.mark(extend("m16"), "so_sq")
            e.need("so_sq_kept")
            e.mark(extend("m2"), "so_ex")
            e.need("so_ex_kept")
            for q in range(6):
                pe.transpose(cell(0, q, n, n), t["tt"][0:n, q, :], I)
                mm = pe.matmul(cell(1, q, n, n), t["off"][0:n, q, :], t["tt"][0:n, q, :], start=True, stop=True)
            e.mark(mm, "so_sq")
            e.need("so_sq_kept")
            for q in range(6):
                mm = pe.matmul(cell(2, q, n, n), t["m2t"][0:n, q, :], t["m2"][0:n, q, :], start=True, stop=True)
            e.mark(mm, "so_ex")
            e.need("so_ex_kept")

        def dve_solve(dve, t, n):
            e = on(dve, "dve_chain")
            T = lambda k: t[k][0:n, :, :]
            e.need("so_mt")
            e.link(dve.tensor_copy(T("mt"), region(2, n, n)))
            e.mark(dve.tensor_tensor(T("tt"), T("mt"), bc(ident[0:n, 0:n], 1, 6), ADD), "so_mt_kept")
            e.need("so_sq")
            if n < P:
                e.mark(dve.tensor_copy(T("m2"), region(0, n, n)), "so_sq_kept")
                e.need("so_ex")
                e.mark(dve.tensor_tensor(T("tt"), region(2, n, n), T("tt"), ADD), "so_ex_kept")
                return
            e.link(dve.tensor_copy(T("m2"), region(0, n, n)))
            e.mark(dve.tensor_copy(T("m2t"), region(1, n, n)), "so_sq_kept")
            e.need("so_sq")
            e.link(dve.tensor_copy(T("m16"), region(0, n, n)))
            e.link(dve.tensor_copy(T("mt"), region(1, n, n)))
            e.mark(dve.tensor_tensor(T("tt"), region(2, n, n), T("tt"), ADD), "so_sq_kept")
            e.need("so_sq")
            e.link(dve.tensor_copy(T("m2"), region(0, n, n)))
            e.mark(dve.tensor_tensor(T("tt"), region(2, n, n), T("tt"), ADD), "so_sq_kept")
            e.need("so_ex")
            e.mark(dve.tensor_tensor(T("tt"), region(2, n, n), T("tt"), ADD), "so_ex_kept")
            e.need("so_sq")
            e.link(dve.tensor_copy(T("m2t"), region(0, n, n)))
            e.mark(dve.tensor_copy(T("m2"), region(1, n, n)), "so_sq_kept")
            e.need("so_ex")
            e.mark(dve.tensor_tensor(T("tt"), region(2, n, n), T("tt"), ADD), "so_ex_kept")

        def pool_mixers(pool):
            e = on(pool, "pool_chain2")
            pool.wait_ge(acc_empty, PLAN["inA"]["group0"])
            pool.dma_start(wloraC[0:64, :], i["rwkv_w_up"][0]).then_inc(sem("lora_landed"), 16)
            pool.dma_start(wloraC[64:128, :], i["rwkv_a_up"][0]).then_inc(sem("lora_landed"), 16)
            pool.dma_start(srowC[0:8, :], i["state_rwkv_shift"][0].rearrange("b o n -> (b o) n")).then_inc(sem("lora_landed"), 16)
            e.need("shift_rows")
            pool.dma_start(o["shift_p"][0, 0], srowC[0:1, :]).then_inc(sem("out_stored"), 16)
            pool.dma_start(o["shift_s"][0].rearrange("b o n -> (b o) n"), srowC[1:9, :]).then_inc(sem("out_stored"), 16)
            pool.wait_ge(sem("out_stored"), 32)
            pool.nop().then_inc(sem("shift_stored"), 1)
            stored = 2
            ts = tC[1]
            for g in range(2):
                e.need("C_states")
                for par in range(2):
                    pool.dma_start(o["rwkv_p"][0, 0].rearrange("(p r) v k -> r v p k", r=2)[par][:, 3 * g:3 * g + 3, :],
                                   tC[0]["so"][64 * par:64 * par + 64, :, :]).then_inc(sem("out_stored"), 16)
                stored += 2
                pool.wait_ge(sem("out_stored"), 16 * stored)
                pool.nop().then_inc(sem("C_states_stored"), 1)
            e.need("C_sd_clear")
            for p in range(BT):
                if p:
                    e.need("C_sd_used")
                for par in range(2):
                    pool.dma_start(ts["sd"][64 * par:64 * par + 64, :, 64 * par:64 * par + 64],
                                   i["state_rwkv"][0, :, 2 * p + par].rearrange("b v k -> v b k")).then_inc(sem("C_sd"), 16)
                e.need("C_so8")
                for par in range(2):
                    pool.dma_start(o["rwkv_s"][0, :, 2 * p + par].rearrange("b v k -> v b k"),
                                   ts["so8"][64 * par:64 * par + 64, :, :]).then_inc(sem("out_stored"), 16)
                stored += 2
                pool.wait_ge(sem("out_stored"), 16 * stored)
                pool.nop().then_inc(sem("C_so8_stored"), 1)
            e.need("C_recurred")
            pool.dma_start(gupC[:, :], i["rwkv_g_up"][0]).then_inc(sem("gup_landed"), 16)
            stored = pool_A(pool, e, stored)
            stored = pool_B(pool, e, stored)

        def pe_mixC(pe):
            e = on(pe, "pe_chain")
            pe.wait_ge(acc_empty, PLAN["inA"]["group0"])
            pe.wait_ge(sem("lora_landed"), 48)
            for m in range(20):
                mm = pe.transpose(ps[:, 0, 8 * m:8 * m + 8], srowC[0:8, m * P:(m + 1) * P], ident[0:8, 0:8])
            e.mark(mm, "shift_turned")
            e.need("shift_last")
            for m in range(20):
                mm = pe.transpose(ps[0:9, 1 + m // 4, m % 4 * P:m % 4 * P + P], slastC[:, m, :], ident[:, :])
            e.mark(mm, "last_turned")
            e.need("lora_act")
            e.need("shift_rows")
            for p in range(BT):
                if p > 1:
                    e.need("lora_sig")
                b = 2 * (p % 2)
                pe.matmul(ps[:, b, 0:NT], wloraC[0:64, p * P:(p + 1) * P], proj[0:64, 18, 0:NT], start=True, stop=True)
                mm = pe.matmul(ps[:, b + 1, 0:NT], wloraC[64:128, p * P:(p + 1) * P], proj[64:128, 18, 0:NT], start=True, stop=True)
                e.mark(mm, "lora_mm")
            e.need("lora_sig", 2)
            e.need("hn_sq")
            for p in range(BT):
                mm = pe.matmul(ps[:, p, 0:NT], ones64[:, :], sqC[:, p, :], start=True, stop=True)
            e.mark(mm, "hn_sum")
            e.need("kk_done")
            for b in range(3):
                m, n, c, nch, t0, _ = kind(b)
                t = tC[b // 2]
                for g in range(2):
                    p0 = 3 * g
                    e.need("feat")
                    for r, (l, rh) in enumerate((("ai", "bi"), ("ki", "ai"), ("bi", "ri"), ("ki", "ri"))):
                        for par in range(2):
                            h = slice(64 * par, 64 * par + 64)
                            for p in range(3):
                                mm = pe.matmul(ps[0:n, 2 * r + par, p * P:p * P + n], t[l][h, p, :], t[rh][h, p, :], start=True, stop=True)
                    e.mark(mm, "C_prod")
                    e.need("mats")
                    for k, src in enumerate(("kl", "bl", "aa", None)):
                        for p in range(3):
                            a = t[src][:, p, :] if src else proj[:, 12 + p0 + p, t0:t0 + n]
                            mm = pe.transpose(ps[0:n, k, p * P:(p + 1) * P], a, ident[:, :])
                    e.mark(mm, "C_tok")
                    e.need("C_tok_kept")
                    pe_solve(pe, t, n)
                    for p in range(3):
                        for par in range(2):
                            q, h = 3 * par + p, slice(64 * par, 64 * par + 64)
                            pe.matmul(ps[h, 0, p * P:p * P + n], t["aT"][0:n, p, h], t["tt"][0:n, q, :], start=True, stop=True)
                            mm = pe.matmul(ps[0:n, 2, p * P + 64 * par:p * P + 64 * par + 64], t["nt"][0:n, q, :], t["vT"][0:n, p, h], start=True, stop=True)
                    e.mark(mm, "wz")
                    e.need("wz_kept")
                    for p in range(3):
                        for par in range(2):
                            q, h = 3 * par + p, slice(64 * par, 64 * par + 64)
                            mm = pe.matmul(ps[0:n, 4, p * P + 64 * par:p * P + 64 * par + 64], t["tt"][0:n, q, :], t["nv"][0:n, p, h], start=True, stop=True)
                    e.mark(mm, "C_z")
                    e.need("C_z_kept")
                    if n == P:
                        for j in range(nch):
                            u = slice(CP * j, CP * j + CP)
                            for p in range(3):
                                mm = pe.matmul(ps[u, 0, p * P:(p + 1) * P], t["w"][:, p, u], t["s"][:, g, p, :], start=True, stop=True)
                            e.mark(mm, "sc_z")
                            e.need("sc_z_kept")
                            for p in range(3):
                                oc = slice(p * CP, (p + 1) * CP)
                                pe.matmul(ps[:, 2, oc], t["s"][:, g, p, :], t["rr"][:, p, u], start=True, stop=False, skip_group_check=True)
                                for par in range(2):
                                    q, h = 3 * par + p, slice(64 * par, 64 * par + 64)
                                    pe.matmul(ps[h, 2, oc], t["z"][u, p, h], t["qb"][u, q, u], start=False, stop=False, skip_group_check=True)
                                    pe.matmul(ps[h, 2, oc], t["vT"][u, p, h], t["qk"][u, q, u], start=False, stop=True, skip_group_check=True)
                                pe.matmul(ps[:, 4, p * P:(p + 1) * P], t["blT"][u, p, :], t["z"][u, p, :], start=True, stop=False)
                                mm = pe.matmul(ps[:, 4, p * P:(p + 1) * P], t["klT"][u, p, :], t["vT"][u, p, :], start=False, stop=True)
                            e.mark(mm, "sc_os")
                            e.need("sc_s_kept")
                            e.need("sc_o_kept")
                        if b == 1:
                            for p in range(3):
                                mm = pe.transpose(ps[:, 0, p * P:(p + 1) * P], t["s"][:, g, p, :], ident[:, :])
                            e.mark(mm, "C_s_turned")
                            e.need("C_states")
                    else:
                        for p in range(3):
                            e.eng.wait_ge(sem("C_sd"), 32 * (p0 + p + 1))
                            for k in range(NSEQ):
                                mm = pe.transpose(ps[:, k // 4, k % 4 * P:k % 4 * P + P], t["sd"][:, k, :], ident[:, :])
                            e.mark(mm, "C_s0t")
                            e.need("C_s0_kept")
                            for k in range(NSEQ):
                                u = slice(TS * k, TS * k + TS)
                                pe.matmul(ps[:, 2, u], t["s0"][:, k, :], t["w"][:, p, u], start=True, stop=True)
                                mm = pe.matmul(ps[:, 3, u], t["s0"][:, k, :], t["rr"][:, p, u], start=True, stop=True)
                            e.mark(mm, "ss_z")
                            e.need("ss_zT_kept")
                            e.mark(pe.transpose(ps[0:32, 4, 0:P], t["zT"][:, :], ident[:, :]), "ss_zt")
                            e.need("ss_z_kept")
                            for par in range(2):
                                q, h = 3 * par + p, slice(64 * par, 64 * par + 64)
                                pe.matmul(ps[h, 5, 0:32], t["z"][0:32, p, h], t["qb"][0:32, q, :], start=True, stop=False, skip_group_check=True)
                                pe.matmul(ps[h, 5, 0:32], t["vT"][0:32, p, h], t["qk"][0:32, q, :], start=False, stop=True, skip_group_check=True)
                            for k in range(2):
                                four = slice(4 * k, 4 * k + 4)
                                out = ps[:, 6 + k, :].rearrange("p (b v) -> p b v", v=P)
                                pe.matmul(out, t["blT"][0:32, p, :], t["um"][:, four, :], start=True, stop=False)
                                mm = pe.matmul(out, t["klT"][0:32, p, :], t["vm"][:, four, :], start=False, stop=True)
                            e.mark(mm, "ss_os")
                            e.need("ss_s_kept")
                            for k in range(NSEQ):
                                mm = pe.transpose(ps[:, k // 4, k % 4 * P:k % 4 * P + P], t["s0"][:, k, :], ident[:, :])
                            e.mark(mm, "C_s8t")
                            e.need("C_so8")
            e.need("C_recurred")
            for p in range(BT):
                mm = pe.matmul(ps[:, p, 0:NT], ones64[:, :], ybuf[:, YC + p, :], start=True, stop=True)
            e.mark(mm, "hn_sum")
            e.need("hn_sq")
            for p in range(BT):
                mm = pe.matmul(ps[:, p, 0:NT], ones64[:, :], sqF[:, p, :], start=True, stop=True)
            e.mark(mm, "hn_sum")
            e.need("hn_sq")
            for p in range(BT):
                mm = pe.matmul(ps[:, p, 0:NT], ones64[:, :], sqF[:, p, :], start=True, stop=True)
            e.mark(mm, "hn_sum")
            e.need("gn_bonus_used")
            pe.wait_ge(sem("gup_landed"), 16)
            for p in range(BT):
                mm = pe.matmul(ps[:, p, 0:NT], gupC[:, p * P:(p + 1) * P], proj[:, 19, 0:NT], start=True, stop=True)
            e.mark(mm, "hn_sum")

        def chunks(ap, c):
            return ap.rearrange("p h (j t) -> p h j t", t=c)

        def cums(cs, p0, b, tiles=3):
            _, n, c, nch, _, c0 = kind(b)
            v = cs[:, p0:p0 + tiles, c0:c0 + nch * (c + 1)].rearrange("p h (j t) -> p h j t", t=c + 1)
            rep = lambda k: v[:, :, :, k:k + 1].to_broadcast([P, tiles, nch, c])
            return v[:, :, :, 1:], v[:, :, :, 0:c], rep(c // 2), rep(c), v[:, :, :, c]

        def act_mixC(act):
            e = on(act, "act_chain")
            for k in range(20):
                m = (18, 19)[k] if k < 2 else k - 2
                e.need("shifted")
                e.link(act.activation(proj[:, m, 0:TP], shB[:, k % 2, 0:TP], ACT.Copy))
                e.mark(act.activation(proj[:, m, TP:NT].rearrange("p (b t) -> p b t", t=TS),
                                      shB[:, k % 2, TP:TP + NSEQ * 7].rearrange("p (b t) -> p b t", t=7)[:, :, GAP:],
                                      ACT.Copy), "compact")
            e.link(act.activation(proj[0:64, 18, 0:NT], proj[0:64, 18, 0:NT], ACT.Tanh))
            e.mark(act.activation(proj[:, 19, 0:NT], proj[:, 19, 0:NT], ACT.Sigmoid), "lora_act")
            for p in range(BT):
                b = 2 * (p % 2)
                e.need("lora_mm")
                if p > 1:
                    e.need("sgw_used")
                act.activation(sgw[:, p % 2, :], ps[:, b, 0:NT], ACT.Sigmoid, bias=par1[:, R_W0 + p:R_W0 + p + 1])
                e.mark(act.activation(bbC[:, p, :], ps[:, b + 1, 0:NT], ACT.Sigmoid, bias=par1[:, R_A0 + p:R_A0 + p + 1]), "lora_sig")
            e.need("fin_eps")
            e.link(act.activation(sqC[:, :, :], sqC[:, :, :], ACT.Ln))
            e.mark(act.activation(sqC[:, :, :], sqC[:, :, :], ACT.Exp, scale=-0.5), "fin_rs")
            for b in range(3):
                m, n, c, nch, t0, _ = kind(b)
                t = tC[b // 2]
                for g in range(2):
                    inc, exc, _, _, last = cums(csC, 3 * g, b)
                    e.need("diff")
                    act.activation(t["ri"][:, :, :], t["dm"][:, :, :], ACT.Exp)
                    act.activation(t["ki"][:, :, :], t["dm"][:, :, :], ACT.Exp, scale=-1.0)
                    act.activation(t["ai"][:, :, :], t["ai"][:, :, :], ACT.Exp)
                    act.activation(t["kl"][:, :, :], t["kl"][:, :, :], ACT.Exp)
                    act.activation(chunks(t["rr"][:, :, :], c), inc, ACT.Exp)
                    act.activation(chunks(t["aa"][:, :, :], c), exc, ACT.Exp)
                    e.mark(act.activation(t["pl"][:, :, 0:nch], last, ACT.Exp), "C_exps")
                    e.need("C_tok")
                    for k, dst in enumerate(("klT", "blT", "aT", "vT")):
                        cp = act.activation(t[dst][0:n, :, :], ps[0:n, k, 0:3 * P].rearrange("p (h t) -> p h t", t=P), ACT.Copy)
                    e.mark(cp, "C_tok_kept")
                    if n == P:
                        for j in range(nch):
                            e.need("sc_os")
                            e.mark(act.activation(ybuf[:, YC + 3 * g:YC + 3 * g + 3, t0 + CP * j:t0 + CP * j + CP],
                                                  ps[:, 2, 0:3 * CP].rearrange("p (h t) -> p h t", t=CP), ACT.Copy), "sc_o_kept")
                    else:
                        for p in range(3):
                            e.need("ss_z")
                            e.mark(act.activation(ybuf[:, YC + 3 * g + p, t0:t0 + n], ps[:, 3, 0:32], ACT.Copy), "ss_o_kept")
            act_norm_tail(e, act, "C", sqF)

        def act_norm_tail(e, act, tag, sq_):
            e.need("fin_eps")
            e.link(act.activation(sq_[:, :, :], sq_[:, :, :], ACT.Ln))
            e.mark(act.activation(sq_[:, :, :], sq_[:, :, :], ACT.Exp, scale=-0.5), "fin_rs")

        def dve_mixC(dve):
            e = on(dve, "dve_chain")
            dve.wait_ge(acc_empty, PLAN["inA"]["group0"])
            e.link(dve.memset(proj[:, 0:20, GAP - 1:GAP], 0.0))
            for k in range(GAP - 1):
                e.link(dve.memset(proj[:, 0:20, SEQW:PW].rearrange("p m (b t) -> p m b t", t=7)[:, :, :, k], 0.0))
            e.need("shift_turned")
            e.link(dve.tensor_copy(proj[:, 0:20, SEQW:PW].rearrange("p m (b t) -> p m b t", t=7)[:, :, :, GAP - 1],
                                   ps[:, 0, 0:160].rearrange("p (m b) -> p m b", b=8)))
            e.link(dve.tensor_copy(slastC[:, :, 0:1], proj[:, 0:20, SEQW - 1:SEQW]))
            e.mark(dve.tensor_copy(slastC[:, :, 1:9], proj[:, 0:20, SEQW:PW].rearrange("p m (b t) -> p m b t", t=7)[:, :, :, 6]), "shift_last")
            for k in range(20):
                m = (18, 19)[k] if k < 2 else k - 2
                if k > 1:
                    e.need("compact")
                W = PW - GAP
                e.link(dve.tensor_tensor(shA[:, k % 2, 0:W], proj[:, m, GAP - 1:PW - 1], proj[:, m, GAP:PW], SUB))
                e.mark(dve.scalar_tensor_tensor(shB[:, k % 2, 0:W], shA[:, k % 2, 0:W], par1[:, R_MU + m:R_MU + m + 1],
                                                proj[:, m, GAP:PW], MUL, ADD), "shifted")
            e.need("compact", 2)
            e.need("last_turned")
            e.mark(dve.tensor_copy(srowC[0:9, :], psf[0:9, 512:512 + N_C]), "shift_rows")
            e.link(dve.memset(padC[:, :], 0.0))
            lead = (TP // CP) * (CP + 1)
            for p in range(BT):
                e.need("lora_sig")
                for a, c, lo_, hi_, s0, s1 in ((0, CP, 0, lead, 0, TP), (0, CS, lead, CW, TP, NT)):
                    ins = dve.tensor_scalar(padC[:, lo_:hi_].rearrange("p (j t) -> p j t", t=c + 1)[:, :, 1:],
                                            sgw[:, p % 2, s0:s1].rearrange("p (j t) -> p j t", t=c), NEG, None, MUL)
                    if s0:
                        e.mark(ins, "sgw_used")
                    else:
                        e.link(ins)
                e.link(dve.tensor_tensor_scan(csC[:, p, :], notlead[:, :], padC[:, :], 0.0, MUL, ADD))
                k_ = proj[:, 6 + p, 0:NT]
                e.link(dve.tensor_scalar(kkC[:, p, :], k_, par1[:, R_KK + p:R_KK + p + 1], None, MUL))
                e.link(dve.tensor_scalar(shA[:, 0, 0:NT], bbC[:, p, :], 1.0, par1[:, R_KA + p:R_KA + p + 1], SUB, MUL))
                e.link(dve.scalar_tensor_tensor(k_, shA[:, 0, 0:NT], 1.0, k_, ADD, MUL))
            dve.wait_ge(sem("shift_stored"), 1)
            e.mark(dve.tensor_tensor(sqC[:, :, :], kkC[:, :, :], kkC[:, :, :], MUL), "hn_sq")
            e.need("hn_sum")
            e.mark(dve.tensor_scalar(sqC[:, :, :], ps[:, 0:6, 0:NT], 1e-6, None, ADD), "fin_eps")
            e.need("fin_rs")
            e.link(dve.tensor_tensor(kkC[:, :, :], kkC[:, :, :], sqC[:, :, :], MUL))
            e.mark(dve.tensor_tensor(bbC[:, :, :], bbC[:, :, :], kkC[:, :, :], MUL), "kk_done")
            e.link(dve.memset(tC[0]["s"][:, :, :, :], 0.0))
            for b in range(3):
                m, n, c, nch, t0, _ = kind(b)
                t = tC[b // 2]
                if b == 2:
                    dve.wait_ge(sem("C_states_stored"), 2)
                    e.mark(dve.memset(t["sd"][:, :, :], 0.0), "C_sd_clear")
                for g in range(2):
                    p0 = 3 * g
                    inc, exc, mid, end, _ = cums(csC, p0, b)
                    C = lambda k: chunks(t[k][:, :, :], c)
                    A = lambda k: t[k][:, :, :]
                    e.link(dve.tensor_tensor(C("dm"), inc, mid, SUB))
                    e.link(dve.tensor_tensor(C("ai"), exc, mid, SUB))
                    e.mark(dve.tensor_tensor(C("kl"), end, inc, SUB), "diff")
                    e.need("C_exps")
                    r_, k_ = proj[:, p0:p0 + 3, t0:t0 + n], proj[:, 6 + p0:9 + p0, t0:t0 + n]
                    kk_, bb_ = kkC[:, p0:p0 + 3, t0:t0 + n], bbC[:, p0:p0 + 3, t0:t0 + n]
                    e.link(dve.tensor_tensor(A("ri"), r_, A("ri"), MUL))
                    e.link(dve.tensor_tensor(A("bi"), bb_, A("ki"), MUL))
                    e.link(dve.tensor_tensor(A("ki"), k_, A("ki"), MUL))
                    e.link(dve.scalar_tensor_tensor(A("ai"), kk_, -1.0, A("ai"), MUL, MUL))
                    e.link(dve.tensor_tensor(A("bl"), bb_, A("kl"), MUL))
                    e.link(dve.tensor_tensor(A("kl"), k_, A("kl"), MUL))
                    e.link(dve.tensor_tensor(A("rr"), r_, A("rr"), MUL))
                    e.mark(dve.scalar_tensor_tensor(A("aa"), kk_, -1.0, A("aa"), MUL, MUL), "feat")
                    e.need("C_prod")
                    for par in range(2):
                        q = slice(3 * par, 3 * par + 3)
                        mb = lambda k: bc(m[k][:, :], 1, 3)
                        e.link(dve.tensor_tensor(t["m16"][0:n, q, :], parity(0, par, n, n), mb("l16"), MUL))
                        if n == P:
                            e.link(dve.tensor_tensor(t["off"][0:n, q, :], parity(0, par, n, n), mb("off"), MUL))
                        e.link(dve.tensor_tensor(t["nt"][0:n, q, :], parity(1, par, n, n), mb("us"), MUL))
                        e.link(dve.tensor_tensor(t["qb"][0:n, q, :], parity(2, par, n, n), mb("ui"), MUL))
                        ins = dve.tensor_tensor(t["qk"][0:n, q, :], parity(3, par, n, n), mb("ui"), MUL)
                        if par:
                            e.mark(ins, "mats")
                        else:
                            e.link(ins)
                    dve_solve(dve, t, n)
                    e.need("wz")
                    e.link(dve.tensor_copy(t["w"][:, :, 0:n], ps[:, 0, :].rearrange("p (h t) -> p h t", t=P)[:, 0:3, 0:n]))
                    e.mark(dve.tensor_copy(t["nv"][0:n, :, :], ps[0:n, 2, 0:3 * P].rearrange("p (h t) -> p h t", t=P)), "wz_kept")
                    e.need("C_z")
                    e.mark(dve.tensor_copy(t["zb"][0:n, :, :], ps[0:n, 4, 0:3 * P].rearrange("p (h t) -> p h t", t=P)), "C_z_kept")
                    if n == P:
                        for j in range(nch):
                            u = slice(CP * j, CP * j + CP)
                            e.need("sc_z")
                            e.mark(dve.tensor_tensor(t["z"][u, :, :], ps[u, 0, 0:3 * P].rearrange("p (h t) -> p h t", t=P),
                                                     t["zb"][u, :, :], ADD), "sc_z_kept")
                            e.need("sc_os")
                            for par in range(2):
                                h = slice(64 * par, 64 * par + 64)
                                s = t["s"][h, g, :, h]
                                e.link(dve.tensor_tensor(s, s, t["pl"][h, :, j:j + 1].to_broadcast([64, 3, 64]), MUL))
                                ins = dve.tensor_tensor(s, ps[h, 4, 0:3 * P].rearrange("p (h t) -> p h t", t=P)[:, :, h], s, ADD)
                                if par:
                                    e.mark(ins, "sc_s_kept")
                                else:
                                    e.link(ins)
                        if b == 1:
                            e.need("C_s_turned")
                            if g:
                                dve.wait_ge(sem("C_states_stored"), 1)
                            for par in range(2):
                                h = slice(64 * par, 64 * par + 64)
                                ins = dve.tensor_copy(t["so"][h, :, :], ps[h, 0, 0:3 * P].rearrange("p (h t) -> p h t", t=P)[:, :, h])
                                if par:
                                    e.mark(ins, "C_states")
                                else:
                                    e.link(ins)
                            dve.wait_ge(sem("C_states_stored"), g + 1)
                    else:
                        for p in range(3):
                            e.need("C_s0t")
                            e.mark(dve.tensor_copy(t["s0"][:, :, :], psf[:, 0:1024].rearrange("p (b v) -> p b v", v=P)), "C_s0_kept")
                            dve.nop().then_inc(sem("C_sd_used"), 1)
                            e.need("ss_z")
                            e.mark(dve.tensor_copy(t["zT"][:, :], ps[:, 2, 0:32]), "ss_zT_kept")
                            e.need("ss_zt")
                            e.link(dve.tensor_tensor(t["z"][0:32, p, :], ps[0:32, 4, 0:P], t["zb"][0:32, p, :], ADD))
                            sm = bc(seqmask[:, :], 2, P)
                            e.link(dve.tensor_tensor(t["um"][:, :, :], bc(t["z"][0:32, p, :], 1, NSEQ), sm, MUL))
                            e.mark(dve.tensor_tensor(t["vm"][:, :, :], bc(t["vT"][0:32, p, :], 1, NSEQ), sm, MUL), "ss_z_kept")
                            e.need("ss_os")
                            e.link(dve.tensor_tensor(t["s0"][:, :, :], t["s0"][:, :, :], bc(t["pl"][:, p, :], 2, P), MUL))
                            e.mark(dve.tensor_tensor(t["s0"][:, :, :], psf[:, 3072:4096].rearrange("p (b v) -> p b v", v=P),
                                                     t["s0"][:, :, :], ADD), "ss_s_kept")
                            e.need("ss_o_kept")
                            yy = ybuf[:, YC + p0 + p, t0:t0 + n]
                            e.link(dve.tensor_tensor(yy, ps[:, 5, 0:32], yy, ADD))
                            e.need("C_s8t")
                            if p0 + p:
                                dve.wait_ge(sem("C_so8_stored"), p0 + p)
                            for par in range(2):
                                h = slice(64 * par, 64 * par + 64)
                                ins = dve.tensor_copy(t["so8"][h, :, :], psf[h, 0:1024].rearrange("p (b v) -> p b v", v=P)[:, :, h])
                                if par:
                                    e.mark(ins, "C_so8")
                                else:
                                    e.link(ins)
            dve.wait_ge(sem("C_so8_stored"), 6)
            dve.nop().then_inc(sem("C_recurred"), 1)
            Y = ybuf[:, YC:YC + 6, :]
            PS6 = ps[:, 0:6, 0:NT]
            e.need("hn_sum")
            e.link(dve.scalar_tensor_tensor(Y, PS6, -1.0 / 64, Y, MUL, ADD))
            e.mark(dve.tensor_tensor(sqF[:, :, :], Y, Y, MUL), "hn_sq")
            e.need("hn_sum")
            e.mark(dve.tensor_scalar(sqF[:, :, :], PS6, 1.0 / 64, GN_EPS, MUL, ADD), "fin_eps")
            e.need("fin_rs")
            e.link(dve.tensor_tensor(Y, Y, sqF[:, :, :], MUL))
            for p in range(BT):
                e.link(dve.tensor_scalar(Y[:, p, :], Y[:, p, :], par1[:, R_LNW + p:R_LNW + p + 1], par1[:, R_LNB + p:R_LNB + p + 1], MUL, ADD))
                ins = dve.scalar_tensor_tensor(sqF[:, p, :], proj[:, p, 0:NT], par1[:, R_RK + p:R_RK + p + 1], proj[:, 6 + p, 0:NT], MUL, MUL)
                if p < 5:
                    e.link(ins)
                else:
                    e.mark(ins, "hn_sq")
            e.need("hn_sum")
            e.mark(dve.tensor_tensor(sqF[:, :, :], PS6, proj[:, 12:18, 0:NT], MUL), "gn_bonus_used")
            e.link(dve.tensor_tensor(Y, Y, sqF[:, :, :], ADD))
            e.need("hn_sum")
            e.link(dve.tensor_tensor(Y, PS6, Y, MUL))
            dve.nop().then_inc(sem("mixer_done"), 1)

        startA = arena0 + 24 * PW * 4
        preA = Map(startA, y_a)
        rowsA = preA("rowsA", [27, 2304])
        lastA = preA("lastA", [P, 18, 27])
        cvA = preA("cvA", [P, 2, PW])
        sqA = Map(startA, y_a)("sqA", [P, BT, NT])

        def maps_A(n, tag):
            m = Map(startA, y_a)
            t = recur_tiles(m, n, tag, 6, ("dt",))
            al = Map(startA, y_a)
            for k in ("w", "zb", "z"):
                t[k] = (al if n == P else m)(k + tag, [P, 6, P])
            for k in ("gb", "dd"):
                t[k] = (al if n == P else m)(k + tag, [P, 6, P])
            t["eg"] = (al if n == P else m)("eg" + tag, [P, 6, n])
            for k in ("kb", "kd", "vb"):
                t[k] = m(k + tag, [P, 6, P])
            for k in ("ba", "ex"):
                t[k] = m(k + tag, [P, 2, 6])
            for k in ("be", "nb", "g", "gc", "gd"):
                t[k] = m(k + tag, [P, 6])
            t["pl"] = m("pl" + tag, [P, 6, 8])
            if n == P:
                t["s"] = m("sA", [P, 6, P])
            else:
                for k in range(2):
                    t["s0", k] = m(f"s0A{k}", [P, NSEQ, P])
                t["um"] = m("umA", [32, NSEQ, P])
                t["zT"] = m("zTA", [P, 32])
            return t

        tA = [maps_A(P, "Ap"), maps_A(32, "As")]
        finA = Map(startA, y_a)
        sqG = finA("sqG", [P, BT, NT])
        zgG = finA("zgG", [P, BT, NT])

        def pool_A(pool, e, stored):
            pool.wait_ge(sem("mixer_done"), 1)
            pool.dma_start(rowsA[0:24, :], i["state_gdn_conv"][0].rearrange("b j n -> (b j) n")).then_inc(sem("a_landed"), 16)
            for k, name in ((0, "a_log"), (1, "dt_bias")):
                pool.dma_start(smA[:, k, :], i[name][0].partition_broadcast(P)).then_inc(sem("a_landed"), 16)
            e.need("A_rows")
            pool.dma_start(o["conv_p"][0, 0], rowsA[0:3, :]).then_inc(sem("out_stored"), 16)
            pool.dma_start(o["conv_s"][0].rearrange("b j n -> (b j) n"), rowsA[3:27, :]).then_inc(sem("out_stored"), 16)
            stored += 2
            pool.wait_ge(sem("out_stored"), 16 * stored)
            pool.nop().then_inc(sem("A_rows_stored"), 1)
            e.need("state_whole")
            pool.dma_start(o["gdn_p"][0, 0].rearrange("h k v -> k h v"), tA[0]["s"][:, :, :]).then_inc(sem("out_stored"), 16)
            stored += 1
            pool.wait_ge(sem("out_stored"), 16 * stored)
            pool.nop().then_inc(sem("state_stored"), 1)
            return sample_states(pool, e, stored, tA[1], 6, "A",
                                 lambda h: i["state_gdn"][0, :, h].rearrange("b k v -> k b v"),
                                 lambda h: o["gdn_s"][0, :, h].rearrange("b k v -> k b v"))

        def sample_states(pool, e, stored, t, count, tag, src, dst):
            def load(h):
                pool.dma_start(t["s0", h % 2][:, :, :], src(h)).then_inc(sem(f"{tag}_s0_{h % 2}"), 16)

            load(0)
            load(1)
            for h in range(count):
                e.need("s_new")
                pool.dma_start(dst(h), t["s0", h % 2][:, :, :]).then_inc(sem("out_stored"), 16)
                stored += 1
                pool.wait_ge(sem("out_stored"), 16 * stored)
                if h + 2 < count:
                    load(h + 2)
            pool.nop().then_inc(sem("s_stored"), 1)
            return stored

        def pe_mixA(pe):
            e = on(pe, "pe_chain")
            pe.wait_ge(acc_empty, PLAN["inB"]["group0"])
            pe.wait_ge(sem("a_landed"), 48)
            for m in range(18):
                mm = pe.transpose(ps[:, 0, 24 * m:24 * m + 24], rowsA[0:24, m * P:(m + 1) * P], ident[0:24, 0:24])
            e.mark(mm, "A_hist")
            e.need("A_last")
            for m in range(18):
                mm = pe.transpose(ps[0:27, 1 + m // 4, m % 4 * P:m % 4 * P + P], lastA[:, m, :], ident[:, :])
            e.mark(mm, "A_last_turned")
            for half in range(2):
                e.need("hn_sq")
                for h in range(6):
                    mm = pe.matmul(ps[:, h, 0:NT], ones[:, :], sqA[:, h, :], start=True, stop=True)
                e.mark(mm, "hn_sum")
            e.need("A_normed")
            for b in range(3):
                m, n, c, nch, t0, _ = kind(b)
                t = tA[b // 2]
                cols = slice(t0, t0 + n)
                e.mark(pe.transpose(ps[0:n, 0, 0:12], low[0:12, 0, cols], ident[0:12, 0:12]), "A_ba")
                e.need("A_g")
                pe.matmul(ps[0:n, 1, 0:6], m["ui"][:, :], t["g"][0:n, :], start=True, stop=True)
                pe.matmul(ps[0:n, 1, 8:14], m["same"][:, :], t["g"][0:n, :], start=True, stop=True)
                for h in range(6):
                    mm = pe.matmul(cell(1, h, P, n), t["gb"][0:n, h, :], m["ui"][:, :], start=True, stop=True)
                e.mark(mm, "A_gc")
                e.need("A_exps")
                for h in range(6):
                    q_, k_, v_ = proj[:, h, cols], proj[:, 6 + h, cols], proj[:, 12 + h, cols]
                    pe.matmul(cell(0, h, n, n), k_, k_, start=True, stop=True)
                    pe.matmul(cell(1, h, n, n), k_, q_, start=True, stop=True)
                    pe.transpose(cell(2, h, n, P), k_, ident[:, :])
                    mm = pe.transpose(cell(3, h, n, P), v_, ident[:, :])
                e.mark(mm, "A_prod")
                e.need("mats")
                pe_solve(pe, t, n)
                for h in range(6):
                    pe.matmul(cell(0, h, P, n), t["kb"][0:n, h, :], t["tt"][0:n, h, :], start=True, stop=True)
                    mm = pe.matmul(cell(1, h, n, P), t["tt"][0:n, h, :], t["vb"][0:n, h, :], start=True, stop=True)
                e.mark(mm, "wz")
                e.need("wz_kept")
                if n == P:
                    for j in range(nch):
                        u = slice(CP * j, CP * j + CP)
                        for h in range(6):
                            mm = pe.matmul(ps[u, h // 4, h % 4 * P:h % 4 * P + P], t["w"][:, h, u], t["s"][:, h, :], start=True, stop=True)
                        e.mark(mm, "sc_z")
                        e.need("sc_z_kept")
                        for h in range(6):
                            oc = slice(h * CP, (h + 1) * CP)
                            pe.matmul(ps[:, 4, oc], t["s"][:, h, :], proj[:, h, t0 + CP * j:t0 + CP * j + CP], start=True, stop=False)
                            pe.matmul(ps[:, 4, oc], t["z"][u, h, :], t["dt"][u, h, u], start=False, stop=True)
                            mm = pe.matmul(cell(1, h, P, P), t["kd"][u, h, :], t["z"][u, h, :], start=True, stop=True)
                        e.mark(mm, "sc_os")
                        e.need("sc_s_kept")
                        e.need("sc_o_kept")
                else:
                    for h in range(6):
                        pe.wait_ge(sem(f"A_s0_{h % 2}"), 16 * (h // 2 + 1))
                        s0 = t["s0", h % 2]
                        for k in range(NSEQ):
                            u = slice(TS * k, TS * k + TS)
                            pe.matmul(ps[:, 2, u], s0[:, k, :], t["w"][:, h, u], start=True, stop=True)
                            mm = pe.matmul(ps[:, 3, u], s0[:, k, :], proj[:, h, t0 + TS * k:t0 + TS * k + TS], start=True, stop=True)
                        e.mark(mm, "ss_z")
                        e.need("ss_zT_kept")
                        e.mark(pe.transpose(ps[0:32, 4, 0:P], t["zT"][:, :], ident[:, :]), "ss_zt")
                        e.need("ss_z_kept")
                        pe.matmul(ps[:, 5, 0:32], t["z"][0:32, h, :], t["dt"][0:32, h, :], start=True, stop=True)
                        for k in range(2):
                            mm = pe.matmul(ps[:, 6 + k, :].rearrange("p (b v) -> p b v", v=P), t["kd"][0:32, h, :],
                                           t["um"][:, 4 * k:4 * k + 4, :], start=True, stop=True)
                        e.mark(mm, "ss_os")
                        e.need("ss_s_kept")
            pe_head_norm(e, pe, "A", sqG)

        def pe_head_norm(e, pe, tag, sq_):
            e.need("hn_sq")
            for h in range(6):
                mm = pe.matmul(ps[:, h, 0:NT], ones[:, :], sq_[:, h, :], start=True, stop=True)
            e.mark(mm, "hn_sum")

        def act_mixA(act):
            e = on(act, "act_chain")
            act.wait_ge(sem("a_landed"), 48)
            e.link(act.activation(smA[:, 0, :], smA[:, 0, :], ACT.Exp))
            for m in range(18):
                e.need("A_conv")
                e.link(act.activation(proj[:, m, 0:TP], cvA[:, m % 2, 0:TP], ACT.Silu))
                e.mark(act.activation(proj[:, m, TP:NT].rearrange("p (b t) -> p b t", t=TS),
                                      cvA[:, m % 2, SEQW:PW].rearrange("p (b t) -> p b t", t=7)[:, :, 0:TS],
                                      ACT.Silu), "A_silu")
            for half in range(2):
                e.need("fin_eps")
                e.link(act.activation(sqA[:, :, :], sqA[:, :, :], ACT.Ln))
                e.mark(act.activation(sqA[:, :, :], sqA[:, :, :], ACT.Exp, scale=-0.5), "fin_rs")
            for b in range(3):
                m, n, c, nch, t0, _ = kind(b)
                t = tA[b // 2]
                e.need("A_ba_kept")
                e.link(act.activation(t["ex"][0:n, :, :], t["ex"][0:n, :, :], ACT.Exp, scale=-1.0))
                e.mark(act.activation(t["be"][0:n, :], t["ex"][0:n, 1, :], ACT.Ln, bias=ones[0:n, 0:1]), "A_ln")
                e.need("A_dd")
                act.activation(t["eg"][:, :, :], region(1, n, n, slice(0, P)), ACT.Exp)
                act.activation(t["pl"][:, :, 0:nch], region(1, n, n, slice(0, P)).rearrange("p h (j t) -> p h j t", t=c)[:, :, :, c - 1], ACT.Exp)
                act.activation(t["dt"][0:n, :, :], t["dt"][0:n, :, :], ACT.Exp)
                act.activation(t["dd"][0:n, :, 0:n], t["dd"][0:n, :, 0:n], ACT.Exp, scale=-1.0)
                act.activation(t["gc"][0:n, :], t["gc"][0:n, :], ACT.Exp)
                e.mark(act.activation(t["gd"][0:n, :], t["gd"][0:n, :], ACT.Exp), "A_exps")
                if n == P:
                    for j in range(nch):
                        e.need("sc_os")
                        e.mark(act.activation(ybuf[:, YA:YA + 6, t0 + CP * j:t0 + CP * j + CP],
                                              ps[:, 4, 0:6 * CP].rearrange("p (h t) -> p h t", t=CP), ACT.Copy), "sc_o_kept")
                else:
                    for h in range(6):
                        e.need("ss_z")
                        e.mark(act.activation(ybuf[:, YA + h, t0:t0 + n], ps[:, 3, 0:32], ACT.Copy), "ss_o_kept")
            e.need("A_fin")
            e.link(act.activation(zgG[:, :, 0:TP], proj[:, 18:24, GAP:SEQW], ACT.Silu))
            for h in range(6):
                e.link(act.activation(zgG[:, h, TP:NT].rearrange("p (b t) -> p b t", t=TS),
                                      proj[:, 18 + h, SEQW:PW].rearrange("p (b t) -> p b t", t=7)[:, :, GAP:], ACT.Silu))
            act_norm_tail(e, act, "A", sqG)

        def dve_mixA(dve):
            e = on(dve, "dve_chain")
            dve.wait_ge(acc_empty, PLAN["inB"]["group0"])
            e.link(dve.memset(proj[:, 0:18, 0:GAP], 0.0))
            e.need("A_hist")
            for m in range(18):
                e.link(dve.tensor_copy(proj[:, m, SEQW:PW].rearrange("p (b t) -> p b t", t=7)[:, :, 0:GAP],
                                       ps[:, 0, 24 * m:24 * m + 24].rearrange("p (b t) -> p b t", t=GAP)))
            e.link(dve.tensor_copy(lastA[:, :, 0:GAP], proj[:, 0:18, TP:SEQW]))
            for m in range(18):
                ins = dve.tensor_copy(lastA[:, m, GAP:27].rearrange("p (b t) -> p b t", t=GAP),
                                      proj[:, m, SEQW:PW].rearrange("p (b t) -> p b t", t=7)[:, :, TS:])
                if m < 17:
                    e.link(ins)
                else:
                    e.mark(ins, "A_last")
            W = PW - GAP
            for m in range(18):
                if m > 1:
                    e.need("A_silu")
                cv = cvA[:, m % 2, 0:W]
                tap = lambda j: par2[:, j * 18 + m:j * 18 + m + 1]
                e.link(dve.tensor_scalar(cv, proj[:, m, 0:W], tap(0), None, MUL))
                for j in (1, 2):
                    e.link(dve.scalar_tensor_tensor(cv, proj[:, m, j:j + W], tap(j), cv, MUL, ADD))
                e.mark(dve.scalar_tensor_tensor(cv, proj[:, m, 3:3 + W], tap(3), cv, MUL, ADD), "A_conv")
            e.need("A_silu", 2)
            e.need("A_last_turned")
            e.mark(dve.tensor_copy(rowsA[0:27, :], psf[0:27, 512:512 + 2304]), "A_rows")
            dve.wait_ge(sem("A_rows_stored"), 1)
            for half in range(2):
                v = proj[:, 6 * half:6 * half + 6, 0:NT]
                e.mark(dve.tensor_tensor(sqA[:, :, :], v, v, MUL), "hn_sq")
                e.need("hn_sum")
                e.mark(dve.tensor_scalar(sqA[:, :, :], ps[:, 0:6, 0:NT], 1e-6, None, ADD), "fin_eps")
                e.need("fin_rs")
                if half:
                    e.mark(dve.tensor_tensor(v, v, sqA[:, :, :], MUL), "A_normed")
                else:
                    e.link(dve.tensor_tensor(v, v, sqA[:, :, :], MUL))
                    e.link(dve.tensor_scalar(v, v, 128 ** -0.5, None, MUL))
            e.link(dve.tensor_scalar(smA[:, 0, :], smA[:, 0, :], -1.0, None, MUL))
            e.link(dve.memset(tA[0]["s"][:, :, :], 0.0))
            for b in range(3):
                m, n, c, nch, t0, _ = kind(b)
                t = tA[b // 2]
                if b == 2:
                    dve.nop().then_inc(sem("state_whole"), 1)
                    dve.wait_ge(sem("state_stored"), 1)
                R = lambda k: t[k][0:n, :]
                T = lambda k: t[k][0:n, :, 0:n]
                e.need("A_ba")
                e.link(dve.tensor_copy(t["ba"][0:n, :, :], ps[0:n, 0, 0:12].rearrange("p (a h) -> p a h", a=2)))
                e.link(dve.tensor_tensor(t["ba"][0:n, 1, :], t["ba"][0:n, 1, :], smA[0:n, 1, :], ADD))
                e.link(dve.tensor_copy(t["ex"][0:n, 0, :], t["ba"][0:n, 0, :]))
                e.mark(dve.scalar_tensor_tensor(t["ex"][0:n, 1, :], t["ba"][0:n, 1, :], -1.0, t["ba"][0:n, 1, :], MUL, ALU.max), "A_ba_kept")
                e.need("A_ln")
                e.link(dve.scalar_tensor_tensor(R("g"), t["ba"][0:n, 1, :], 0.0, R("be"), ALU.max, ADD))
                e.link(dve.tensor_tensor(R("g"), R("g"), smA[0:n, 0, :], MUL))
                e.mark(dve.tensor_copy(t["gb"][0:n, :, :], bc(R("g"), 2, P)), "A_g")
                e.link(dve.tensor_scalar(t["ex"][0:n, 0, :], t["ex"][0:n, 0, :], 1.0, None, ADD))
                e.link(dve.reciprocal(R("be"), t["ex"][0:n, 0, :]))
                e.link(dve.tensor_scalar(R("nb"), R("be"), -1.0, None, MUL))
                e.need("A_gc")
                e.link(dve.tensor_copy(R("gc"), ps[0:n, 1, 0:6]))
                e.link(dve.tensor_tensor(R("gd"), ps[0:n, 1, 8:14], R("gc"), SUB))
                e.link(dve.tensor_tensor(T("dd"), region(1, n, n), bc(R("gc"), 2, n), SUB))
                e.link(dve.tensor_scalar(T("dt"), T("dd"), 0.0, None, ALU.min))
                e.mark(dve.tensor_scalar(T("dd"), T("dd"), 0.0, None, ALU.max), "A_dd")
                e.need("A_exps")
                e.link(dve.tensor_tensor(T("dt"), T("dt"), bc(m["ui"][:, :], 1, 6), MUL))
                e.link(dve.tensor_tensor(T("dd"), T("dd"), bc(R("nb"), 2, n), MUL))
                e.link(dve.tensor_tensor(T("m16"), T("dd"), bc(m["l16"][:, :], 1, 6), MUL))
                if n == P:
                    e.link(dve.tensor_tensor(T("off"), T("dd"), bc(m["off"][:, :], 1, 6), MUL))
                e.link(dve.tensor_tensor(R("nb"), R("nb"), R("gc"), MUL))
                e.need("A_prod")
                e.link(dve.tensor_tensor(T("m16"), region(0, n, n), T("m16"), MUL))
                if n == P:
                    e.link(dve.tensor_tensor(T("off"), region(0, n, n), T("off"), MUL))
                e.link(dve.tensor_tensor(T("dt"), region(1, n, n), T("dt"), MUL))
                e.link(dve.tensor_tensor(t["kb"][0:n, :, :], region(2, n, P), bc(R("nb"), 2, P), MUL))
                e.link(dve.tensor_tensor(t["kd"][0:n, :, :], region(2, n, P), bc(R("gd"), 2, P), MUL))
                e.link(dve.tensor_tensor(t["vb"][0:n, :, :], region(3, n, P), bc(R("be"), 2, P), MUL))
                q_ = proj[:, 0:6, t0:t0 + n]
                e.mark(dve.tensor_tensor(q_, q_, t["eg"][:, :, :], MUL), "mats")
                dve_solve(dve, t, n)
                e.need("wz")
                e.link(dve.tensor_copy(t["w"][:, :, 0:n], region(0, n, n, slice(0, P))))
                e.mark(dve.tensor_copy(t["zb"][0:n, :, :], region(1, n, P)), "wz_kept")
                if n == P:
                    for j in range(nch):
                        u = slice(CP * j, CP * j + CP)
                        e.need("sc_z")
                        e.mark(dve.tensor_tensor(t["z"][u, :, :], region(0, n, P, u), t["zb"][u, :, :], ADD), "sc_z_kept")
                        e.need("sc_os")
                        s = t["s"][:, :, :]
                        e.link(dve.tensor_tensor(s, s, t["pl"][:, :, j:j + 1].to_broadcast([P, 6, P]), MUL))
                        e.mark(dve.tensor_tensor(s, region(1, P, P), s, ADD), "sc_s_kept")
                else:
                    for h in range(6):
                        e.need("ss_z")
                        e.mark(dve.tensor_copy(t["zT"][:, :], ps[:, 2, 0:32]), "ss_zT_kept")
                        e.need("ss_zt")
                        e.link(dve.tensor_tensor(t["z"][0:32, h, :], ps[0:32, 4, 0:P], t["zb"][0:32, h, :], ADD))
                        e.mark(dve.tensor_tensor(t["um"][:, :, :], bc(t["z"][0:32, h, :], 1, NSEQ), bc(seqmask[:, :], 2, P), MUL), "ss_z_kept")
                        e.need("ss_os")
                        s0 = t["s0", h % 2][:, :, :]
                        e.link(dve.tensor_tensor(s0, s0, bc(t["pl"][:, h, :], 2, P), MUL))
                        e.mark(dve.tensor_tensor(s0, psf[:, 3072:4096].rearrange("p (b v) -> p b v", v=P), s0, ADD), "s_new")
                        e.need("ss_o_kept")
                        yy = ybuf[:, YA + h, t0:t0 + n]
                        e.mark(dve.tensor_tensor(yy, ps[:, 5, 0:32], yy, ADD), "ss_s_kept")
            dve.wait_ge(sem("s_stored"), 1)
            dve.nop().then_inc(sem("A_fin"), 1)
            dve_head_norm(e, dve, "A", sqG, zgG[:, :, :], YA, R_GDN)
            dve.nop().then_inc(sem("mixer_done"), 1)

        def dve_head_norm(e, dve, tag, sq_, gate, y0, gain):
            Y = ybuf[:, y0:y0 + 6, :]
            e.mark(dve.tensor_tensor(sq_[:, :, :], Y, Y, MUL), "hn_sq")
            e.need("hn_sum")
            e.mark(dve.tensor_scalar(sq_[:, :, :], ps[:, 0:6, 0:NT], 1.0 / P, EPS, MUL, ADD), "fin_eps")
            e.need("fin_rs")
            e.link(dve.scalar_tensor_tensor(Y, Y, par1[:, gain:gain + 1], sq_[:, :, :], MUL, MUL))
            e.link(dve.tensor_tensor(Y, Y, gate, MUL))

        startB = arena0 + 18 * PW * 4
        mapB = Map(startB, y_at)
        csB = mapB("csB", [P, 3, CW])
        startB = mapB.at
        preB = Map(startB, y_at)
        gkupB = preB("gkupB", [RANK, 384])
        gxB = preB("gxB", [P, 3, NT])
        glB = preB("glB", [P, 3, NT])
        padB = preB("padB", [P, CW])

        def maps_B(n, tag):
            m = Map(startB, y_at)
            t = {"qk": m("qk" + tag, [P, 6, n])}
            for k in ("dm", "ri", "ki", "kl", "rr"):
                t[k] = m(k + tag, [P, 3, n])
            t["klT"] = m("klT" + tag, [P, 3, P])
            t["vT"] = m("vT" + tag, [P, 6, P])
            t["pl"] = m("pl" + tag, [P, 3, 8])
            if n == P:
                t["s"] = m("sB", [P, 3, P])
            else:
                for k in range(2):
                    t["s0", k] = m(f"s0B{k}", [P, NSEQ, P])
                t["vm"] = m("vmB", [32, 2, NSEQ, P])
            return t

        tB = [maps_B(P, "Bp"), maps_B(32, "Bs")]
        sqB = Map(startB, y_at)("sqB", [P, BT, NT])

        def pool_B(pool, e, stored):
            pool.wait_ge(sem("mixer_done"), 2)
            pool.dma_start(gkupB[:, :], i["gla_gk_up"][0]).then_inc(sem("gk_landed"), 16)
            e.need("state_whole")
            for par in range(2):
                pool.dma_start(o["gla_p"][0, 0].rearrange("(p r) k v -> r k p v", r=2)[par],
                               tB[0]["s"][64 * par:64 * par + 64, :, :]).then_inc(sem("out_stored"), 16)
            stored += 2
            pool.wait_ge(sem("out_stored"), 16 * stored)
            pool.nop().then_inc(sem("state_stored"), 2)
            rows = lambda x, p: x[0].rearrange("b h k v -> (h k) b v")[p * P:(p + 1) * P]
            return sample_states(pool, e, stored, tB[1], 3, "B",
                                 lambda p: rows(i["state_gla"], p), lambda p: rows(o["gla_s"], p))

        def pe_mixB(pe):
            e = on(pe, "pe_chain")
            pe.wait_ge(acc_empty, PLAN["branch"]["group0"])
            pe.wait_ge(sem("gk_landed"), 16)
            for p in range(3):
                mm = pe.matmul(ps[:, p, 0:NT], gkupB[:, p * P:(p + 1) * P], low[0:RANK, 1, :], start=True, stop=True)
            e.mark(mm, "B_gk")
            e.need("B_gx")
            for b in range(3):
                m, n, c, nch, t0, _ = kind(b)
                t = tB[b // 2]
                e.need("feat")
                for par in range(2):
                    h = slice(64 * par, 64 * par + 64)
                    for p in range(3):
                        pe.matmul(ps[0:n, par, p * P:p * P + n], t["ki"][h, p, :], t["ri"][h, p, :], start=True, stop=True)
                for p in range(3):
                    mm = pe.transpose(ps[0:n, 2, p * P:(p + 1) * P], t["kl"][:, p, :], ident[:, :])
                for h in range(6):
                    mm = pe.transpose(cell(2, h, n, P), proj[:, 6 + h, t0:t0 + n], ident[:, :])
                e.mark(mm, "B_prod")
                e.need("mats")
                e.need("B_tok_kept")
                if n == P:
                    for j in range(nch):
                        u = slice(CP * j, CP * j + CP)
                        for par in range(2):
                            h = slice(64 * par, 64 * par + 64)
                            for p in range(3):
                                q, oc = 3 * par + p, slice(p * CP, (p + 1) * CP)
                                pe.matmul(ps[:, 6 + par, oc], t["s"][h, p, :], t["rr"][h, p, u], start=True, stop=False)
                                pe.matmul(ps[:, 6 + par, oc], t["vT"][u, 2 * p + par, :], t["qk"][u, q, u], start=False, stop=True)
                                mm = pe.matmul(ps[h, 3, p * P:(p + 1) * P], t["klT"][u, p, h], t["vT"][u, 2 * p + par, :], start=True, stop=True)
                        e.mark(mm, "sc_os")
                        e.need("sc_s_kept")
                        e.need("sc_o_kept")
                else:
                    for p in range(3):
                        pe.wait_ge(sem(f"B_s0_{p % 2}"), 16 * (p // 2 + 1))
                        s0 = t["s0", p % 2]
                        for par in range(2):
                            h, q = slice(64 * par, 64 * par + 64), 3 * par + p
                            for k in range(NSEQ):
                                u = slice(TS * k, TS * k + TS)
                                pe.matmul(ps[:, par, u], s0[h, k, :], t["rr"][h, p, u], start=True, stop=True)
                            pe.matmul(ps[:, 2 + par, 0:32], t["vT"][0:32, 2 * p + par, :], t["qk"][0:32, q, :], start=True, stop=True)
                        e.need("B_vm")
                        for par in range(2):
                            h = slice(64 * par, 64 * par + 64)
                            for k in range(2):
                                mm = pe.matmul(ps[h, 6 + k, :].rearrange("p (b v) -> p b v", v=P), t["klT"][0:32, p, h],
                                               t["vm"][:, par, 4 * k:4 * k + 4, :], start=True, stop=True)
                        e.mark(mm, "B_ss_os")
                        e.need("ss_s_kept")
            pe_head_norm(e, pe, "B", sqB)

        def act_mixB(act):
            e = on(act, "act_chain")
            e.need("B_gx")
            e.link(act.activation(glB[:, :, :], glB[:, :, :], ACT.Exp, scale=-1.0))
            e.mark(act.activation(glB[:, :, :], glB[:, :, :], ACT.Ln, bias=ones[:, 0:1]), "B_gl")
            for b in range(3):
                m, n, c, nch, t0, _ = kind(b)
                t = tB[b // 2]
                inc, _, _, _, last = cums(csB, 0, b)
                e.need("diff")
                act.activation(t["ri"][:, :, :], t["dm"][:, :, :], ACT.Exp)
                act.activation(t["ki"][:, :, :], t["dm"][:, :, :], ACT.Exp, scale=-1.0)
                act.activation(t["kl"][:, :, :], t["kl"][:, :, :], ACT.Exp)
                act.activation(chunks(t["rr"][:, :, :], c), inc, ACT.Exp)
                e.mark(act.activation(t["pl"][:, :, 0:nch], last, ACT.Exp), "B_exps")
                e.need("B_prod")
                act.activation(t["klT"][0:n, :, :], ps[0:n, 2, 0:3 * P].rearrange("p (h t) -> p h t", t=P), ACT.Copy)
                e.mark(act.activation(t["vT"][0:n, :, :], region(2, n, P), ACT.Copy), "B_tok_kept")
                if n == P:
                    for j in range(nch):
                        e.need("sc_os")
                        for par in range(2):
                            ins = act.activation(ybuf[:, YB + par:YB + 6:2, t0 + CP * j:t0 + CP * j + CP],
                                                 ps[:, 6 + par, 0:3 * CP].rearrange("p (h t) -> p h t", t=CP), ACT.Copy)
                        e.mark(ins, "sc_o_kept")
                else:
                    for p in range(3):
                        e.need("B_ss_os")
                        for par in range(2):
                            ins = act.activation(ybuf[:, YB + 2 * p + par, t0:t0 + n], ps[:, par, 0:32], ACT.Copy)
                        e.mark(ins, "B_ss_o")
            e.need("B_fin")
            e.link(act.activation(proj[:, 12:18, 0:NT], proj[:, 12:18, 0:NT], ACT.Silu))
            act_norm_tail(e, act, "B", sqB)
            act.wait_ge(sem("B_whole"), 1)
            act_split(act, ybuf, yh, 3 * BT, sem("y_hi"))

        def dve_mixB(dve):
            e = on(dve, "dve_chain")
            dve.wait_ge(acc_empty, PLAN["branch"]["group0"])
            e.need("B_gk")
            for p in range(3):
                e.link(dve.tensor_scalar(gxB[:, p, :], ps[:, p, 0:NT], par2[:, R_BIAS + p:R_BIAS + p + 1], None, ADD))
            e.mark(dve.scalar_tensor_tensor(glB[:, :, :], gxB[:, :, :], -1.0, gxB[:, :, :], MUL, ALU.max), "B_gx")
            e.need("B_gl")
            e.link(dve.scalar_tensor_tensor(gxB[:, :, :], gxB[:, :, :], 0.0, glB[:, :, :], ALU.min, SUB))
            e.link(dve.memset(padB[:, :], 0.0))
            lead = (TP // CP) * (CP + 1)
            for p in range(3):
                for c, lo_, hi_, s0, s1 in ((CP, 0, lead, 0, TP), (CS, lead, CW, TP, NT)):
                    e.link(dve.tensor_scalar(padB[:, lo_:hi_].rearrange("p (j t) -> p j t", t=c + 1)[:, :, 1:],
                                             gxB[:, p, s0:s1].rearrange("p (j t) -> p j t", t=c), 1.0 / 16, None, MUL))
                e.link(dve.tensor_tensor_scan(csB[:, p, :], notlead[:, :], padB[:, :], 0.0, MUL, ADD))
            e.link(dve.memset(tB[0]["s"][:, :, :], 0.0))
            for b in range(3):
                m, n, c, nch, t0, _ = kind(b)
                t = tB[b // 2]
                if b == 2:
                    dve.nop().then_inc(sem("state_whole"), 1)
                    dve.wait_ge(sem("state_stored"), 2)
                inc, _, mid, end, _ = cums(csB, 0, b)
                C = lambda k: chunks(t[k][:, :, :], c)
                A = lambda k: t[k][:, :, :]
                e.link(dve.tensor_tensor(C("dm"), inc, mid, SUB))
                e.mark(dve.tensor_tensor(C("kl"), end, inc, SUB), "diff")
                e.need("B_exps")
                q_, k_ = proj[:, 0:3, t0:t0 + n], proj[:, 3:6, t0:t0 + n]
                e.link(dve.scalar_tensor_tensor(A("ri"), q_, 64 ** -0.5, A("ri"), MUL, MUL))
                e.link(dve.scalar_tensor_tensor(A("rr"), q_, 64 ** -0.5, A("rr"), MUL, MUL))
                e.link(dve.tensor_tensor(A("ki"), k_, A("ki"), MUL))
                e.mark(dve.tensor_tensor(A("kl"), k_, A("kl"), MUL), "feat")
                e.need("B_prod")
                for par in range(2):
                    ins = dve.tensor_tensor(t["qk"][0:n, 3 * par:3 * par + 3, :], parity(0, par, n, n), bc(m["ui"][:, :], 1, 3), MUL)
                    if par:
                        e.mark(ins, "mats")
                    else:
                        e.link(ins)
                e.need("B_tok_kept")
                if n == P:
                    for j in range(nch):
                        e.need("sc_os")
                        s = t["s"][:, :, :]
                        e.link(dve.tensor_tensor(s, s, t["pl"][:, :, j:j + 1].to_broadcast([P, 3, P]), MUL))
                        e.mark(dve.tensor_tensor(s, ps[:, 3, 0:3 * P].rearrange("p (h t) -> p h t", t=P), s, ADD), "sc_s_kept")
                else:
                    for p in range(3):
                        for par in range(2):
                            ins = dve.tensor_tensor(t["vm"][:, par, :, :], bc(t["vT"][0:32, 2 * p + par, :], 1, NSEQ), bc(seqmask[:, :], 2, P), MUL)
                            if par:
                                e.mark(ins, "B_vm")
                            else:
                                e.link(ins)
                        e.need("B_ss_os")
                        s0 = t["s0", p % 2][:, :, :]
                        e.link(dve.tensor_tensor(s0, s0, bc(t["pl"][:, p, :], 2, P), MUL))
                        e.mark(dve.tensor_tensor(s0, psf[:, 3072:4096].rearrange("p (b v) -> p b v", v=P), s0, ADD), "s_new")
                        e.need("B_ss_o")
                        for par in range(2):
                            yy = ybuf[:, YB + 2 * p + par, t0:t0 + n]
                            ins = dve.tensor_tensor(yy, ps[:, 2 + par, 0:32], yy, ADD)
                            if par:
                                e.mark(ins, "ss_s_kept")
                            else:
                                e.link(ins)
            dve.wait_ge(sem("s_stored"), 2)
            dve.nop().then_inc(sem("B_fin"), 1)
            dve_head_norm(e, dve, "B", sqB, proj[:, 12:18, 0:NT], YB, R_GLA)
            dve.nop().then_inc(sem("B_whole"), 1)
            for k in range(3 * BT):
                dve.wait_ge(sem("y_hi"), k + 1)
                ins = dve.tensor_tensor(yl[:, k, :], ybuf[:, k, :], yh[:, k, :].bitcast(F32), SUB)
                if k < 3 * BT - 1:
                    e.link(ins)
                else:
                    ins.then_inc(sem("mixer_done"), 1)

        vectors = [("norm_ff1", R_FF1, 16), ("norm_mix", R_MIX, 16), ("norm_ff2", R_FF2, 16),
                   ("norm_final", R_FIN, 16), ("rwkv_mu", R_MU, 20), ("rwkv_w0", R_W0, 6),
                   ("rwkv_a0", R_A0, 6), ("rwkv_k_k", R_KK, 6), ("rwkv_k_a", R_KA, 6),
                   ("rwkv_r_k", R_RK, 6), ("rwkv_ln_w", R_LNW, 6), ("rwkv_ln_b", R_LNB, 6),
                   ("gdn_norm", R_GDN, 1), ("gla_norm", R_GLA, 1)]
        PROWS = len(vectors) + 2

        def pool_program(pool):
            made = [0]

            def chain(ins):
                made[0] += 1
                ins.then_inc(sem("pool_chain"), 1)
                pool.wait_ge(sem("pool_chain"), made[0])

            def keep(t, conds, fill=0.0):
                for cond, b0, pattern, mult in conds:
                    chain(pool.affine_select(out=t, in_=t, compare_op=cond, fill=fill, base=b0,
                                             pattern=pattern, channel_multiplier=mult))

            GE = ALU.is_ge
            for name, r, n in vectors:
                v = i[name]
                if len(v.shape) == 2:
                    v = v[0]
                pool.dma_start(prow[r:r + n, 0, :], v.rearrange("(a b) -> a b", b=P)).then_inc(sem("prow_landed"), 16)
            pool.dma_start(prow[0:72, 1, :], i["conv_a"][0].rearrange("j (a b) -> (j a) b", b=P)).then_inc(sem("prow_landed"), 16)
            pool.dma_start(prow[R_BIAS:R_BIAS + 3, 1, :], i["gla_gk_bias"][0].rearrange("(a b) -> a b", b=P)).then_inc(sem("prow_landed"), 16)
            chain(pool.memset(ones[:, :], 1.0))
            chain(pool.memset(ident[:, :], 0.0))
            keep(ident[:, :], [(ALU.not_equal, 0, [[-1, P]], 1)], fill=1.0)
            pool.nop().then_inc(sem("consts"), 1)
            chain(pool.memset(ones64[:, :], 1.0))
            keep(ones64[:, :], [(GE, 0, [[-64, 2], [0, 64]], 1), (GE, 63, [[64, 2], [0, 64]], -1)])
            for m, w, c in ((mk[0], P, CP), (mk[1], 32, CS)):
                for k in m:
                    chain(pool.memset(m[k][:, :], 1.0))
                v = {k: m[k][:, :] for k in m}
                after = (GE, 0, [[-c, w // c], [0, c]], 1)
                before = (GE, c - 1, [[c, w // c], [0, c]], -1)
                keep(v["ui"], [(GE, 0, [[1, w]], -1), after])
                keep(v["us"], [(GE, -1, [[1, w]], -1), after])
                keep(v["same"], [after, before])
                h = min(c, 16)
                keep(v["l16"], [(GE, -1, [[-1, w]], 1), (GE, h - 1, [[h, w // h], [0, h]], -1)])
                keep(v["off"], [(GE, -1, [[-1, w]], 1), before])
                chain(pool.tensor_tensor(v["off"], v["off"], v["l16"], SUB))
            chain(pool.memset(seqmask[:, :], 1.0))
            keep(seqmask[:, :], [(GE, 0, [[-TS, NSEQ]], 1), (GE, TS - 1, [[TS, NSEQ]], -1)])
            chain(pool.memset(notlead[:, :], 1.0))
            lead = (TP // CP) * (CP + 1)
            chain(pool.memset(notlead[:, 0:lead].rearrange("p (c t) -> p c t", t=CP + 1)[:, :, 0:1], 0.0))
            chain(pool.memset(notlead[:, lead:CW].rearrange("p (c t) -> p c t", t=CS + 1)[:, :, 0:1], 0.0))
            pool.nop().then_inc(sem("consts"), 1)
            pool_mixers(pool)

        block = ctx.enter_context(nc.Block())

        @block.sync
        def _(sp):
            sp_program(sp)

        @block.gpsimd
        def _(pool):
            pool_program(pool)

        @block.scalar
        def _(act):
            act_program(act)

        @block.vector
        def _(dve):
            dve_program(dve)

        @block.tensor
        def _(pe):
            pe_program(pe)


INS = ["x_prompt", "x_sample", "state_gdn", "state_gdn_conv", "state_gla", "state_rwkv", "state_rwkv_shift",
       "w_in", "conv_a", "a_log", "dt_bias", "gdn_norm", "gla_gk_up", "gla_gk_bias", "gla_norm",
       "rwkv_mu", "rwkv_w0", "rwkv_w_up", "rwkv_a0", "rwkv_a_up", "rwkv_g_up", "rwkv_k_k", "rwkv_k_a",
       "rwkv_r_k", "rwkv_ln_w", "rwkv_ln_b", "w_branch", "w_out", "norm_ff1", "w_ff1_up", "w_ff1_down",
       "norm_mix", "norm_ff2", "w_ff2_up", "w_ff2_down", "norm_final"]
OUTS = [("y_prompt", (1, TP, D)), ("y_sample", (NSEQ, TS, D)),
        ("gdn_p", (1, 1, 6, 128, 128)), ("gdn_s", (1, NSEQ, 6, 128, 128)),
        ("conv_p", (1, 1, 3, 2304)), ("conv_s", (1, NSEQ, 3, 2304)),
        ("gla_p", (1, 1, 6, 64, 128)), ("gla_s", (1, NSEQ, 6, 64, 128)),
        ("rwkv_p", (1, 1, 12, 64, 64)), ("rwkv_s", (1, NSEQ, 12, 64, 64)),
        ("shift_p", (1, 1, 1, N_C)), ("shift_s", (1, NSEQ, 1, N_C))]


def kernel(**inputs):
    import numpy as np
    import concourse.bacc as bacc
    from concourse.bass_utils import run_bass_kernel_spmd

    nc = bacc.Bacc("TRN2", target_bir_lowering=False, num_devices=1)
    arrays, ins, outs = {}, {}, {}
    for name in INS:
        a = np.ascontiguousarray(inputs[name])
        arrays[f"in_{name}"] = a
        ins[name] = nc.dram_tensor(f"in_{name}", a.shape, mybir.dt.from_np(a.dtype), kind="ExternalInput").ap()
    for name, shape in OUTS:
        outs[name] = nc.dram_tensor(f"out_{name}", shape, F32, kind="ExternalOutput").ap()
    build(nc, ins, outs)
    r = run_bass_kernel_spmd(nc, [arrays], core_ids=[0])
    return tuple(r.results[0][f"out_{name}"] for name, _ in OUTS)
```

```python
import math
from contextlib import ExitStack

import concourse.bass as bass
from concourse import mybir

F32 = mybir.dt.float32
F32R = mybir.dt.float32r
ALU = mybir.AluOpType
ACT = mybir.ActivationFunctionType
ADD, SUB, MUL = ALU.add, ALU.subtract, ALU.mult

P = 128
D = 2048
KD = D // P
TP, NSEQ, TS = 256, 8, 4
NT = TP + NSEQ * TS
FF = 5504
FT = FF // P
HALVES = (22, 21)
BW = 768
BT = BW // P
RANK, DLORA = 16, 64
N_A, N_B, N_C = 3084, 2320, 2560
COL_BA, COL_B, COL_LOW, COL_C = 3072, N_A, N_A + 2304, N_A + N_B
COL_GATE = N_A + N_B + N_C
EPS = 1e-6
GN_EPS = 64e-5
CP, CS = 32, TS
BLOCKS = ((0, 128, CP), (128, 128, CP), (256, 32, CS))
GAP = 3
SEQW = TP + GAP
PW = SEQW + NSEQ * (TS + GAP)
CW = (TP // CP) * (CP + 1) + NSEQ * (CS + 1)
RING = 4
SLOT = 1024
AHEAD = 2

R_FF1, R_MIX, R_FF2, R_FIN, R_MU, R_W0, R_A0, R_KK, R_KA, R_RK, R_LNW, R_LNB, R_GDN, R_GLA = (
    0, 16, 32, 48, 64, 84, 90, 96, 102, 108, 114, 120, 126, 127)
R_BIAS = 72


def plan():
    ph = []

    def add(name, per_body, times, groups):
        ph.append(dict(name=name, n=per_body, times=times, groups=groups))

    def ff(f):
        for h, tiles in enumerate(HALVES):
            add(f"up{f}{h}", 8, tiles // 2, 2)
            if tiles % 2:
                add(f"up{f}{h}t", 4, 1, 1)
            add(f"down{f}{h}", tiles, 2, 4)

    ff(0)
    add("low", 4, 1, 1)
    add("inC", 8, 5, 2)
    add("inA", 8, 6, 2)
    add("inB", 8, 4, 2)
    add("inBt", 4, 1, 1)
    add("gate", 8, 12, 2)
    add("branch", 12, 4, 6)
    add("out", 8, 4, 2)
    ff(1)
    use, group = [0] * RING, 2
    for p in ph:
        p["base"] = list(use)
        p["per"] = [len(range(q, p["n"], RING)) for q in range(RING)]
        p["group0"] = group
        use = [u + p["times"] * c for u, c in zip(use, p["per"])]
        group += p["times"] * p["groups"]
    return {p["name"]: p for p in ph}


PLAN = plan()
ORDER = list(PLAN)
WOVEN = ("inA", "inB", "inBt", "gate")
WOVEN_SLOTS = [(name, it, s) for name in WOVEN for it in range(PLAN[name]["times"])
               for s in range(PLAN[name]["n"])]
GROUPS_A = PLAN["inB"]["group0"] - PLAN["inA"]["group0"]
GROUPS_B = PLAN["gate"]["group0"] - PLAN["inB"]["group0"]
GROUPS_G = PLAN["branch"]["group0"] - PLAN["gate"]["group0"]


def build(nc, i, o):
    ctx = ExitStack()
    with ctx:
        base = (nc.sbuf_base + 63) // 64 * 64

        class Map:

            def __init__(self, at, end):
                self.at, self.end = (at + 31) // 32 * 32, end

            def __call__(self, name, shape, dt=F32):
                t = nc.alloc_sbuf_tensor_at(name, shape, dt, offset=self.at)
                n = 4
                for s in shape[1:]:
                    n *= s
                self.at += (n + 31) // 32 * 32
                assert self.at <= self.end, (name, self.at, self.end)
                return t

        fixed = Map(base, nc.sbuf_usable_end)
        x = fixed("x", [P, KD, NT])
        xh = fixed("xh", [P, KD, NT], F32R)
        xl = fixed("xl", [P, KD, NT], F32R)
        raw = fixed("raw", [P, RING, SLOT])
        hi = fixed("hi", [P, RING, SLOT], F32R)
        lo = fixed("lo", [P, RING, SLOT], F32R)
        ident = fixed("ident", [P, P])
        ones = fixed("ones", [P, P])
        ones64 = fixed("ones64", [P, P])
        par1 = fixed("par1", [P, P])
        par2 = fixed("par2", [P, 75])
        low = fixed("low", [P, 2, NT])
        mk = []
        for w, c in ((P, CP), (32, CS)):
            mk.append({k: fixed(f"mask_{k}{w}", [w, w]) for k in
                       ("ui",
                        "us",
                        "same",
                        "l16",
                        "off")})
        seqmask = fixed("seqmask", [32, NSEQ])
        notlead = fixed("notlead", [P, CW])
        smA = fixed("smA", [P, 2, 6])
        kept = fixed("kept", [P, 2, PW])
        arena0 = fixed.at
        y_at = nc.sbuf_usable_end // 64 * 64 - 3 * BT * NT * 4

        hid = Map(arena0, y_at)
        hidh = hid("hidh", [P, HALVES[0], NT], F32R)
        hidl = hid("hidl", [P, HALVES[0], NT], F32R)
        stage = Map(arena0, nc.sbuf_usable_end)
        xrow = stage("xrow", [P, 3, D])
        prow = stage("prow", [P, 2, P])
        ymap = Map(y_at, nc.sbuf_usable_end)
        ybuf = ymap("ybuf", [P, 3 * BT, NT])
        YB, YA, YC = 0, BT, 2 * BT
        BRANCHES, Y_OF = (0, 2, 1), (YA, YC, YB)
        ysp = Map(y_at - 2 * 3 * BT * NT * 4, y_at)
        yh = ysp("yh", [P, 3 * BT, NT], F32R)
        yl = ysp("yl", [P, 3 * BT, NT], F32R)
        mmap = Map(y_at, nc.sbuf_usable_end)
        merged = mmap("merged", [P, KD, NT])
        tmp = Map(hid.at, y_at)
        work = tmp("work", [P, 2, NT])
        prodt = tmp("prodt", [P, 2, NT])
        sq = tmp("sq", [P, 2, NT])
        rstd = tmp("rstd", [P, NT])
        normed = tmp("normed", [P, 2, NT])
        bmap = Map(arena0, ysp.at)
        gates = bmap("gates", [P, 2, 3, 2 * NT])
        gated = bmap("gatedY", [P, 2, NT])

        projA = nc.dram_tensor("projA", (P, 24, PW), F32, kind="Internal").ap()
        projB = nc.dram_tensor("projB", (P, 18, NT), F32, kind="Internal").ap()
        gatesD = nc.dram_tensor("gatesD", (P, 3, KD * NT), F32, kind="Internal").ap()

        ps = ctx.enter_context(nc.psum_tensor("ps", [P, 8, 512], F32))

        sems = {}

        def sem(name):
            if name not in sems:
                sems[name] = ctx.enter_context(nc.semaphore(name))
            return sems[name]

        landed = [sem(f"landed{q}") for q in range(RING)]
        hi_ready = [sem(f"hi_ready{q}") for q in range(RING)]
        lo_ready = [sem(f"lo_ready{q}") for q in range(RING)]
        multiplied = [sem(f"multiplied{q}") for q in range(RING)]
        acc_empty = sem("acc_empty")
        gate_ready = sem("gate_ready")
        hid_hi, hid_lo = sem("hid_hi"), sem("hid_lo")

        w_in = i["w_in"][0].rearrange("(k p) n -> p k n", p=P)
        w_up = [i[n][0].rearrange("(k p) (c n) -> p k c n", p=P, c=2) for n in ("w_ff1_up", "w_ff2_up")]
        w_down = [i[n][0].rearrange("(k p) n -> p k n", p=P) for n in ("w_ff1_down", "w_ff2_down")]
        w_branch = i["w_branch"][0].rearrange("b (k p) n -> p b k n", p=P)
        w_out = i["w_out"][0].rearrange("(k p) n -> p k n", p=P)
        w_low = i["w_in"][0][:, COL_BA:COL_BA + 2 * (COL_LOW - COL_BA)].rearrange(
            "(k p) (c n) -> p k c n", p=P, c=2)

        def source(name, s, it):
            if name.startswith("up"):
                f, h = int(name[2]), int(name[3])
                m = h * HALVES[0] + (HALVES[h] - 1 if name.endswith("t") else 2 * it + s // 4)
                return w_up[f][:, 4 * (s % 4):4 * (s % 4) + 4, :, bass.ds(m * P, P)], 4
            if name.startswith("down"):
                f, h = int(name[4]), int(name[5])
                return it * 1024, 1
            if name == "low":
                return w_low[:, 4 * s:4 * s + 4, :, 0:P], 4
            k = 4 * (s % 4)
            if name.startswith("in"):
                g = 8 if name.endswith("t") else 2 * it + s // 4
                c0 = {"A": 0, "B": COL_B, "C": COL_C}[name[2]]
                return w_in[:, k:k + 4, bass.ds(g * 256 + c0, 256)], 4
            if name == "out":
                return w_out[:, k:k + 4, bass.ds((2 * it + s // 4) * 256, 256)], 4
            if name == "gate":
                return w_in[:, k:k + 4, bass.ds((2 * it + s // 4) * 256 + COL_GATE, 256)], 4
            pair, n, r = s // 6, BRANCHES[s // 2 % 3], s % 2
            return w_branch[:, n, 3 * r:3 * r + 3, bass.ds((2 * it + pair) * 256, 256)], 3

        def use(p, s, it):
            q = s % RING
            return it * p["per"][q] + (p["base"][q] + s // RING)

        def ahead(p, s, it):
            s += AHEAD
            if s < p["n"]:
                return s % RING, use(p, s, it)
            s -= p["n"]
            return s, it * p["per"][s] + (p["base"][s] + p["per"][s])

        def turns(eng, p, body, unrolled=False):
            if p["times"] == 1 or unrolled:
                for it in range(p["times"]):
                    body(it)
            else:
                first = 0
                if p["name"] in LATE_NORM:
                    body(0)
                    first = 1
                with eng.Fori(first, p["times"]) as it:
                    body(it)

        LAST = ORDER[-1]
        NORMED = ("up00", "low", "up10")
        LATE_NORM = ("up00", "up10")

        def late(name, it, s):
            return name in LATE_NORM and isinstance(it, int) and it == 0 and s == 3
        WOVEN_REST = 4 * len(WOVEN_SLOTS)
        woven = {}

        def woven_units(engine, units):
            at = woven.get(engine, 0)
            woven[engine] = min(at + units, WOVEN_REST)
            return [divmod(u, 4) for u in range(at, woven[engine])]

        def sp_program(sp):
            for b, (t0, n, _) in enumerate(BLOCKS):
                src = i["x_prompt"][0][t0:t0 + n] if b < 2 else i["x_sample"].rearrange("b t d -> (b t) d")
                sp.dma_start(xrow[0:n, b, :], src).then_inc(sem("x_landed"), 16)
            for name in ORDER:
                p = PLAN[name]

                def body(it):
                    for s in range(p["n"]):
                        q = s % RING
                        src, kk = source(name, s, it)
                        if kk > 1 and len(src.shape) == 4:
                            dst = raw[:, q, :].rearrange("p (k c n) -> p k c n", k=kk, c=2)
                            parts = [(dst[:, :, c, :], src[:, :, c, :]) for c in range(2)]
                        elif kk == 1:
                            f, h = int(name[4]), int(name[5])
                            parts = [(raw[:, q, c:c + 512],
                                      w_down[f][:, h * HALVES[0] + s, bass.ds(it * 1024 + c, 512)])
                                     for c in (0, 512)]
                        else:
                            dst = raw[:, q, 0:kk * 256].rearrange("p (k n) -> p k n", k=kk)
                            parts = [(dst[:, a:b, :], src[:, a:b, :]) for a, b in ((kk // 2, kk), (0, kk // 2))]
                        sp.wait_ge(lo_ready[q], use(p, s, it) + 1)
                        for dst, src in parts:
                            sp.dma_start(dst, src).then_inc(landed[q], 16)
                        if name == "branch" and s % 6 == 3:
                            pair = s // 6
                            sp.wait_ge(sem("B_whole"), 1)
                            sp.wait_ge(sem("kept_stored"), 16 * (GROUPS_A + GROUPS_B + GROUPS_G))
                            sp.wait_ge(acc_empty, it * 6 + (p["group0"] + 3 * pair - 3))
                            sp.dma_start(gates[:, pair, :, :],
                                         gatesD[:, :, bass.ds(it * (4 * NT) + 2 * pair * NT, 2 * NT)]).then_inc(sem("gates_landed"), 16)

                turns(sp, p, body)
            for kq in range(4):
                cols = slice(kq * 512, (kq + 1) * 512)
                for b, (t0, n, _) in enumerate(BLOCKS):
                    dst = o["y_prompt"][0][t0:t0 + n] if b < 2 else o["y_sample"].rearrange("b t d -> (b t) d")
                    sp.wait_ge(sem("rows_out"), 3 * kq + b + 1)
                    sp.dma_start(dst[:, cols], xrow[0:n, b, cols]).then_inc(sem("stored"), 16)
            sp.wait_ge(sem("stored"), 12 * 16)

        def pe_program(pe):
            def three(out, q, col, rh, rl, start, stop):
                w, wl = hi[:, q, col:col + P], lo[:, q, col:col + P]
                pe.matmul(out, w, rh, start=start, stop=False)
                pe.matmul(out, w, rl, start=False, stop=False)
                return pe.matmul(out, wl, rh, start=False, stop=stop)

            def phase(name):
                p = PLAN[name]
                down, br = name.startswith("down"), name == "branch"
                pe.wait_ge(acc_empty, p["group0"])

                def body(it):
                    for s in range(p["n"]):
                        q = s % RING
                        pe.wait_ge(lo_ready[q], use(p, s, it) + 2)
                        if down:
                            for m in range(8):
                                g = it * 4 + (p["group0"] + m // 2)
                                if s == 0 and m % 2 == 0:
                                    pe.wait_ge(acc_empty, g - 3)
                                mm = three(ps[:, m, 0:NT], q, m * P, hidh[:, s, :], hidl[:, s, :],
                                           s == 0, s == p["n"] - 1)
                            mm.then_inc(multiplied[q], 1)
                            continue
                        size = 2 if br else 4
                        g, r = s // size, s % size
                        G = it * p["groups"] + (p["group0"] + g)
                        if r == 0:
                            pe.wait_ge(acc_empty, G - 1)
                        if s < 4 and name in NORMED:
                            pe.wait_ge(sem("xn_ready"), KD * NORMED.index(name) + 4 * (s + 1))
                        if name == "out" and s < 4:
                            pe.wait_ge(sem("merged_ready"), 2 * s + 2)
                        if br:
                            y0 = Y_OF[g % 3] + 3 * r
                            if s < 6:
                                pe.wait_ge(sem("y_ready"), 3 * (s + 1))
                            for k in range(3):
                                for c in range(2):
                                    mm = three(ps[:, g % 2 * 2 + c, 0:NT], q, (2 * k + c) * P,
                                               yh[:, y0 + k, :], yl[:, y0 + k, :],
                                               r == 0 and k == 0, r == 1 and k == 2)
                        else:
                            for k in range(4):
                                for c in range(2):
                                    mm = three(ps[:, g % 2 * 2 + c, 0:NT], q,
                                               (2 * k + c) * P, xh[:, 4 * r + k, :], xl[:, 4 * r + k, :],
                                               r == 0 and k == 0, r == 3 and k == 3)
                        mm.then_inc(multiplied[q], 1)
                        if late(name, it, s):
                            pe_norm(pe, NORMED.index(name))

                turns(pe, p, body)

            def weave(units):
                for j, k in woven_units("pe", units):
                    name, it, s = WOVEN_SLOTS[j]
                    p, q, r = PLAN[name], s % RING, s % 4
                    if k == 0 and r == 0:
                        pe.wait_ge(acc_empty, p["group0"] + it * p["groups"] + s // 4)
                    if k == 0:
                        pe.wait_ge(lo_ready[q], use(p, s, it) + 2)
                    for c in range(2):
                        mm = three(ps[:, 6 + c, 0:NT], q, (2 * k + c) * P, xh[:, 4 * r + k, :],
                                   xl[:, 4 * r + k, :], r == 0 and k == 0, r == 3 and k == 3)
                    if k == 3:
                        mm.then_inc(multiplied[q], 1)

            pe_setup(pe)
            for name in ORDER:
                if name == "low":
                    pe_norm(pe, 1)
                if name in WOVEN:
                    continue
                if name.startswith("down"):
                    pe.wait_ge(hid_lo, hidden_before(name))
                phase(name)
                if name == "inC":
                    pe_mixC(pe, weave)
                    pe_mixA(pe, weave)
                    pe_mixB(pe, weave)
                    weave(WOVEN_REST)
            pe_norm(pe, 3)
            for kq in range(4):
                for b, (t0, n, _) in enumerate(BLOCKS):
                    r = 3 * kq + b
                    pe.wait_ge(sem("final_ready"), 4 * (kq + 1))
                    if r >= 4:
                        pe.wait_ge(sem("rows_out"), r - 3)
                    for k in range(4):
                        mm = pe.transpose(ps[0:n, r % 4, k * P:(k + 1) * P],
                                          x[:, 4 * kq + k, t0:t0 + n], ident[:, :])
                    mm.then_inc(sem("final_turned"), 1)

        def hidden_before(name):
            f, h = int(name[4]), int(name[5])
            return f * FT + (HALVES[0] if h == 0 else FT)

        def pe_setup(pe):
            for q in range(RING):
                pe.nop().then_inc(multiplied[q], 1)
            pe.wait_ge(sem("consts"), 1)
            pe.wait_ge(sem("prow_landed"), PROWS * 16)
            pe.transpose(ps[:, 0, 0:P], prow[:, 0, :], ident[:, :])
            pe.transpose(ps[:, 1, 0:75], prow[0:75, 1, :], ident[0:75, 0:75]).then_inc(sem("par_turned"), 1)
            pe.wait_ge(sem("x_landed"), 48)
            for b, (t0, n, _) in enumerate(BLOCKS):
                for kq in range(4):
                    r = 4 * b + kq
                    if r >= 4:
                        pe.wait_ge(sem("x_copied"), r - 3)
                    for k in range(4):
                        mm = pe.transpose(ps[:, 2 + r % 4, k * P:k * P + n],
                                          xrow[0:n, b, (4 * kq + k) * P:(4 * kq + k + 1) * P],
                                          ident[0:n, 0:n])
                    mm.then_inc(sem("x_turned"), 1)

        def pe_norm(pe, n):
            for k in range(KD):
                pe.wait_ge(sem("sq_ready"), n * KD + k + 1)
                pe.matmul(ps[:, 7, 0:NT], ones[:, :], sq[:, k % 2, :], start=k == 0,
                          stop=k == KD - 1).then_inc(sem("sq_used"), 1)

        def act_program(act):
            def split(place):
                q, u = place
                act.wait_ge(landed[q], (u + 1) * 32)
                act.wait_ge(multiplied[q], u + 1)
                act.activation(hi[:, q, :], raw[:, q, :], ACT.Copy).then_inc(hi_ready[q], 1)

            def phase(name):
                p = PLAN[name]
                size = {"up": 4, "do": p["n"], "br": 2}.get(name[0:2], 4)

                def body(it):
                    for s in range(p["n"]):
                        q = s % RING
                        if not (name == LAST and it == 1 and s + AHEAD >= p["n"]):
                            split(ahead(p, s, it))
                        if (s + 1) % size:
                            continue
                        g = s // size
                        G = it * p["groups"] + (p["group0"] + g)
                        if name.startswith("up"):
                            if late(name, it, s):
                                act_root(act, NORMED.index(name))
                            f, h = int(name[2]), int(name[3])
                            F = f * FT + h * HALVES[0] + (HALVES[h] - 1 if name.endswith("t") else it * 2 + g)
                            act.wait_ge(sem("gate_scaled"), F + 1)
                            act.activation(work[:, 1, :], work[:, 0, :], ACT.Silu).then_inc(gate_ready, 1)
                            act.wait_ge(sem("prod_ready"), F + 1)
                            m = HALVES[int(name[3])] - 1 if name.endswith("t") else it * 2 + g
                            act.activation(hidh[:, bass.ds(m, 1), :], prodt[:, 1:2, :],
                                           ACT.Copy).then_inc(hid_hi, 1)
                        if name == "branch" and g % 3 == 0:
                            act.wait_ge(sem("gates_landed"), it * 32 + 16 * (g // 3 + 1))
                            gg = gates[:, g // 3, :, :]
                            act.activation(gg, gg, ACT.Sigmoid).then_inc(gate_ready, 1)
                        if name == "branch" and g % 3 == 2:
                            act.wait_ge(sem("gated"), it * 4 + 2 * (g // 3 + 1))
                            pair = bass.ds((it * 2 + g // 3) * 2, 2)
                            act.activation(xh[:, pair, :], merged[:, pair, :], ACT.Copy).then_inc(sem("merged_hi"), 1)

                turns(act, p, body, name == LAST)

            def weave(units):
                for j, k in woven_units("act", units):
                    name, it, s = WOVEN_SLOTS[j]
                    p, q = PLAN[name], s % RING
                    if k == 0:
                        split(ahead(p, s, it))
                    if k < 3 or s % 4 < 3:
                        continue
                    g = it * p["groups"] + s // 4
                    G = p["group0"] + g
                    n = G - PLAN["inA"]["group0"]
                    act.wait_ge(multiplied[q], use(p, s, it) + 2)
                    if n:
                        act.wait_ge(sem("kept_stored"), 16 * n)
                    else:
                        act.wait_ge(sem("consts"), 2)
                    if name == "inA":
                        act.activation(kept[:, :, GAP:SEQW], ps[:, 6:8, 0:TP], ACT.Copy)
                        act.activation(kept[:, :, SEQW:PW].rearrange("p c (b t) -> p c b t", t=GAP + TS)[:, :, :, GAP:],
                                       ps[:, 6:8, TP:NT].rearrange("p c (b t) -> p c b t", t=TS),
                                       ACT.Copy).then_inc(acc_empty, 1)
                        dst, src = projA[:, 2 * g:2 * g + 2, :], kept[:, :, :]
                    else:
                        act.activation(kept[:, :, 0:NT], ps[:, 6:8, 0:NT], ACT.Copy).then_inc(acc_empty, 1)
                        m = n - GROUPS_A
                        dst = (projB[:, 2 * m:2 * m + 2, :] if name != "gate" else
                               gatesD[:, g // 8, g % 8 * 2 * NT:(g % 8 * 2 + 2) * NT].rearrange("p (c t) -> p c t", c=2))
                        src = kept[:, :, 0:NT]
                    act.wait_ge(acc_empty, G + 1)
                    act.dma_start(dst, src).then_inc(sem("kept_stored"), 16)

            act_setup(act)
            for s in range(AHEAD):
                split((s, 0))
            act_norm(act, 0)
            for name in ORDER:
                if name == "low":
                    act_norm(act, 1)
                if name == "up10":
                    act_norm(act, 2)
                if name not in WOVEN:
                    phase(name)
                if name == "inC":
                    act_mixC(act, weave)
                    act_mixA(act, weave)
                    act_mixB(act, weave)
                    weave(WOVEN_REST)
            act_norm(act, 3)

        def act_split(act, src, dst, n, done):
            for k in range(n):
                act.activation(dst[:, k, :], src[:, k, :], ACT.Copy).then_inc(done, 1)

        def act_setup(act):
            pass

        def act_norm(act, n):
            groups = (2, PLAN["low"]["group0"], PLAN["up10"]["group0"],
                      PLAN[LAST]["group0"] + 8)[n]
            act.wait_ge(acc_empty, groups)
            if n == 0:
                act.wait_ge(sem("x_copied"), 12)

            def high(k):
                act.wait_ge(sem("normed_ready"), n * KD + k + 1)
                act.activation(xh[:, k, :], normed[:, k % 2, :], ACT.Copy).then_inc(sem("xn_hi"), 1)

            if n in (0, 2):
                for k in range(KD):
                    high(k)
                for k in range(2):
                    act_square(act, n, k)
                return
            for k in range(KD):
                act_square(act, n, k)
            act_root(act, n)
            if n == 1:
                for k in range(KD):
                    high(k)

        def act_square(act, n, k):
            if n or k > 1:
                act.wait_ge(sem("sq_used"), n * KD + k - 1)
            act.activation(sq[:, k % 2, :], x[:, k, :], ACT.Square).then_inc(sem("sq_ready"), 1)

        def act_root(act, n):
            if n in (0, 2):
                for k in range(2, KD):
                    act_square(act, n, k)
            act.wait_ge(sem("ms_ready"), n + 1)
            act.activation(rstd[:, :], rstd[:, :], ACT.Sqrt).then_inc(sem("root_ready"), 1)

        def dve_program(dve):
            def split(place):
                q, u = place
                dve.wait_ge(hi_ready[q], u + 1)
                dve.tensor_tensor(lo[:, q, :], raw[:, q, :], hi[:, q, :].bitcast(F32),
                                  SUB).then_inc(lo_ready[q], 1)

            def phase(name):
                p = PLAN[name]
                size = {"up": 4, "do": p["n"], "br": 2}.get(name[0:2], 4)

                def body(it):
                    for s in range(p["n"]):
                        q = s % RING
                        if not (name == LAST and it == 1 and s + AHEAD >= p["n"]):
                            split(ahead(p, s, it))
                        if (s + 1) % size:
                            continue
                        g = s // size
                        G = it * p["groups"] + (p["group0"] + g)
                        if name.startswith("up"):
                            f, h = int(name[2]), int(name[3])
                            m = HALVES[h] - 1 if name.endswith("t") else it * 2 + g
                            F = f * FT + h * HALVES[0] + m
                            if late(name, it, s):
                                dve_root(dve, NORMED.index(name))
                            dve.wait_ge(multiplied[q], use(p, s, it) + 2)
                            dve.tensor_tensor(work[:, 0, :], ps[:, g % 2 * 2, 0:NT], rstd[:, :],
                                              MUL).then_inc(sem("gate_scaled"), 1)
                            dve.tensor_tensor(prodt[:, 0, :], ps[:, g % 2 * 2 + 1, 0:NT], rstd[:, :],
                                              MUL).then_inc(acc_empty, 1)
                            dve.wait_ge(acc_empty, G + 1)
                            dve.wait_ge(gate_ready, F + (KD // 2 * f + 1))
                            dve.tensor_tensor(prodt[:, 1, :], work[:, 1, :], prodt[:, 0, :],
                                              MUL).then_inc(sem("prod_ready"), 1)
                            dve.wait_ge(hid_hi, F + 1)
                            dve.tensor_tensor(hidl[:, bass.ds(m, 1), :], prodt[:, 1:2, :],
                                              hidh[:, bass.ds(m, 1), :].bitcast(F32),
                                              SUB).then_inc(hid_lo, 1)
                        elif name.startswith("down"):
                            dve.wait_ge(multiplied[q], use(p, s, it) + 2)
                            for j in range(4):
                                xx = x[:, bass.ds(it * 8 + 2 * j, 2), :]
                                dve.scalar_tensor_tensor(xx, ps[:, 2 * j:2 * j + 2, 0:NT], 0.5, xx,
                                                         MUL, ADD).then_inc(acc_empty, 1)
                        elif name == "out":
                            dve.wait_ge(multiplied[q], use(p, s, it) + 2)
                            xx = x[:, bass.ds((it * 2 + g) * 2, 2), :]
                            dve.tensor_tensor(xx, ps[:, g % 2 * 2:g % 2 * 2 + 2, 0:NT], xx,
                                              ADD).then_inc(acc_empty, 1)
                        elif name == "low":
                            dve.wait_ge(multiplied[q], use(p, s, it) + 2)
                            dve.tensor_copy(low[:, :, :], ps[:, 0:2, 0:NT]).then_inc(acc_empty, 1)
                        elif name.startswith("in"):
                            m = (it * 2 + g) * 2
                            dve.wait_ge(multiplied[q], use(p, s, it) + 2)
                            b = g % 2 * 2
                            dve.tensor_copy(proj[:, bass.ds(m, 2), GAP:SEQW], ps[:, b:b + 2, 0:TP])
                            for c in range(2):
                                cp = dve.tensor_copy(
                                    proj[:, bass.ds(m + c, 1), SEQW:PW].rearrange(
                                        "p o (b t) -> p (o b) t", t=GAP + TS)[:, :, GAP:],
                                    ps[:, b + c, TP:NT].rearrange("p (b t) -> p b t", t=TS))
                            cp.then_inc(acc_empty, 1)
                        elif name == "branch":
                            n, m = g % 3, (it * 2 + g // 3) * 2
                            dve.wait_ge(multiplied[q], use(p, s, it) + 2)
                            if n == 0:
                                dve.wait_ge(gate_ready, it * 2 + (FT + g // 3 + 1))
                            br = ps[:, g % 2 * 2:g % 2 * 2 + 2, 0:NT]
                            gg = gates[:, g // 3, BRANCHES[n], :].rearrange("p (c t) -> p c t", c=2)
                            if n == 0:
                                dve.tensor_tensor(merged[:, bass.ds(m, 2), :], gg, br,
                                                  MUL).then_inc(acc_empty, 1)
                            else:
                                dve.tensor_tensor(gated[:, :, :], gg, br,
                                                  MUL).then_inc(acc_empty, 1)
                                dve.wait_ge(acc_empty, G + 1)
                                mm = merged[:, bass.ds(m, 2), :]
                                dve.tensor_tensor(mm, mm, gated[:, :, :], ADD).then_inc(sem("gated"), 1)
                                dve.wait_ge(sem("gated"), it * 4 + (2 * (g // 3) + n))
                            if n == 2:
                                dve.wait_ge(sem("merged_hi"), it * 2 + (g // 3 + 1))
                                pair = bass.ds(m, 2)
                                dve.tensor_tensor(xl[:, pair, :], merged[:, pair, :], xh[:, pair, :].bitcast(F32),
                                                  SUB).then_inc(sem("merged_ready"), 1)

                turns(dve, p, body, name == LAST)

            def weave(units):
                for j, k in woven_units("dve", units):
                    name, it, s = WOVEN_SLOTS[j]
                    if k == 3:
                        split(ahead(PLAN[name], s, it))

            dve_setup(dve)
            for s in range(AHEAD):
                split((s, 0))
            dve_norm(dve, 0)
            for name in ORDER:
                if name == "low":
                    dve_norm(dve, 1)
                if name == "up10":
                    dve_norm(dve, 2)
                if name not in WOVEN:
                    phase(name)
                if name == "inC":
                    dve_mixC(dve, weave)
                    dve_mixA(dve, weave)
                    dve_mixB(dve, weave)
                    weave(WOVEN_REST)
            dve_norm(dve, 3)
            for kq in range(4):
                for b, (t0, n, _) in enumerate(BLOCKS):
                    r = 3 * kq + b
                    dve.wait_ge(sem("final_turned"), r + 1)
                    dve.tensor_copy(xrow[0:n, b, kq * 512:(kq + 1) * 512],
                                    ps[0:n, r % 4, :]).then_inc(sem("rows_out"), 1)

        def dve_setup(dve):
            for q in range(RING):
                dve.nop().then_inc(lo_ready[q], 1)
            dve.wait_ge(sem("par_turned"), 1)
            dve.tensor_copy(par1[:, :], ps[:, 0, 0:P]).then_inc(acc_empty, 1)
            dve.tensor_copy(par2[:, :], ps[:, 1, 0:75]).then_inc(acc_empty, 1)
            for b, (t0, n, _) in enumerate(BLOCKS):
                for kq in range(4):
                    r = 4 * b + kq
                    dve.wait_ge(sem("x_turned"), r + 1)
                    dve.tensor_copy(x[:, 4 * kq:4 * kq + 4, t0:t0 + n],
                                    ps[:, 2 + r % 4, :].rearrange("p (k t) -> p k t", k=4)[:, :, 0:n]
                                    ).then_inc(sem("x_copied"), 1)

        def dve_norm(dve, n):
            if n in (1, 3):
                dve_root(dve, n)
            elif n:
                dve.wait_ge(acc_empty, PLAN["up10"]["group0"])
            else:
                dve.wait_ge(sem("x_copied"), 12)
            gain = (R_FF1, R_MIX, R_FF2, R_FIN)[n]
            for k in range(KD):
                gk = par1[:, gain + k:gain + k + 1]
                if n == 3:
                    dve.scalar_tensor_tensor(x[:, k, :], x[:, k, :], gk,
                                             rstd[:, :], MUL, MUL).then_inc(sem("final_ready"), 1)
                    continue
                if k > 1:
                    dve.wait_ge(sem("xn_ready"), n * KD + k - 1)
                if n == 1:
                    dve.scalar_tensor_tensor(normed[:, k % 2, :], x[:, k, :], gk,
                                             rstd[:, :], MUL, MUL).then_inc(sem("normed_ready"), 1)
                else:
                    dve.tensor_scalar(normed[:, k % 2, :], x[:, k, :], gk, None,
                                      MUL).then_inc(sem("normed_ready"), 1)
                if k:
                    xn_low(dve, n, k - 1)
            if n < 3:
                xn_low(dve, n, KD - 1)

        def dve_root(dve, n):
            dve.wait_ge(sem("sq_used"), KD * (n + 1))
            dve.tensor_scalar(rstd[:, :], ps[:, 7, 0:NT], 1.0 / D, EPS, MUL, ADD).then_inc(sem("ms_ready"), 1)
            dve.wait_ge(sem("root_ready"), n + 1)
            dve.reciprocal(rstd[:, :], rstd[:, :]).then_inc(sem("rstd_ready"), 1)
            dve.wait_ge(sem("rstd_ready"), n + 1)

        def xn_low(dve, n, k):
            dve.wait_ge(sem("xn_hi"), n * KD + k + 1)
            dve.tensor_tensor(xl[:, k, :], normed[:, k % 2, :], xh[:, k, :].bitcast(F32),
                              SUB).then_inc(sem("xn_ready"), 1)

        class Steps:
            def __init__(self, eng, name):
                self.eng, self.name, self.n, self.done, self.needed = eng, name, 0, {}, {}

            def link(self, ins):
                self.n += 1
                ins.then_inc(sem(self.name), 1)
                self.eng.wait_ge(sem(self.name), self.n)

            def mark(self, ins, step):
                self.done[step] = self.done.get(step, 0) + 1
                ins.then_inc(sem(step), 1)
                if self.name != "pe_chain":
                    self.eng.wait_ge(sem(step), self.done[step])

            def need(self, step, by=1):
                self.needed[step] = self.needed.get(step, 0) + by
                self.eng.wait_ge(sem(step), self.needed[step])

        steps = {}

        def on(eng, name):
            if name not in steps:
                steps[name] = Steps(eng, name)
            return steps[name]

        y_c = y_at + YC * NT * 4
        y_a = y_at + YA * NT * 4
        proj = Map(arena0, y_c)("proj", [P, 24, PW])
        NEG = -math.exp(-0.5)

        def kind(b):
            t0, n, c = BLOCKS[b]
            return mk[b // 2], n, c, n // c, t0, (0, 4 * (CP + 1), 8 * (CP + 1))[b]

        mapC = Map(arena0 + 20 * PW * 4, y_c)
        csC = mapC("csC", [P, BT, CW])
        kkC = mapC("kkC", [P, BT, NT])
        bbC = mapC("bbC", [P, BT, NT])
        startC = mapC.at

        def recur_tiles(m, n, tag, ft, last):
            t = {}
            for k in ("m16", "off", "mt", "m2", "m2t", "tt"):
                t[k] = m(f"{k}{tag}", [P, 6, n])
            for k in last:
                t[k] = m(f"{k}{tag}", [P, 6, n])
            return t

        def maps_C(n, tag):
            m = Map(startC, y_c)
            t = recur_tiles(m, n, tag, 3, ("nt", "qb", "qk"))
            if n == P:
                f = Map(startC + 3 * 6 * n * 4, y_c)
            else:
                f = m
            for k in ("ri", "ki", "bi", "ai"):
                t[k] = f(k + tag, [P, 3, n])
            f2 = Map(startC + 5 * 6 * n * 4, y_c) if n == P else m
            t["dm"] = f2("dm" + tag, [P, 3, n])
            for k in ("kl", "bl", "rr", "aa"):
                t[k] = m(k + tag, [P, 3, n])
            for k in ("klT", "blT", "aT", "vT"):
                t[k] = m(k + tag, [P, 3, P])
            if n == P:
                f = Map(startC, y_c)
            for k in ("w", "zb", "nv", "z"):
                t[k] = (f if n == P else m)(k + tag, [P, 3, P])
            t["pl"] = m("pl" + tag, [P, 3, 8])
            if n == P:
                t["s"] = m("sC", [P, 2, 3, P])
                t["so"] = f("soC", [P, 3, 64])
                t["sw"] = Map(startC + 3 * 6 * n * 4, y_c)("swC", [P, 3, P])
            else:
                t["sd"] = m("sdC", [P, NSEQ, P])
                t["s0"] = m("s0C", [P, NSEQ, P])
                t["um"] = m("umC", [32, NSEQ, P])
                t["vm"] = m("vmC", [32, NSEQ, P])
                t["zT"] = m("zTC", [P, 32])
                t["so8"] = m("so8C", [P, NSEQ, 64])
            return t

        preC = Map(startC, y_c)
        wloraC = preC("wloraC", [P, BW])
        gupC = Map(y_c - BW * 4 - 64, y_c)("gupC", [P, BW])
        srowC = preC("srowC", [9, N_C])
        slastC = preC("slastC", [P, 20, 9])
        shA = preC("shA", [P, 2, PW])
        shB = preC("shB", [P, 2, PW])
        sgw = preC("sgw", [P, 2, NT])
        padC = preC("padC", [P, CW])
        sqC = Map(startC, y_c)("sqC", [P, BT, NT])
        tC = [maps_C(P, "Cp"), maps_C(32, "Cs")]
        finC = Map(startC, y_c)
        sqF = finC("sqF", [P, BT, NT])
        rsF = finC("rsF", [P, BT, NT])

        psf = ps[:, :, :].rearrange("p a b -> p (a b)")

        def region(r, n, m, rows=None):
            rows = slice(0, n) if rows is None else rows
            return psf[rows, r * 1024:(r + 1) * 1024].rearrange("p (h t) -> p h t", t=P)[:, 0:6, 0:m]

        def cell(r, q, n, m):
            return ps[0:n, 2 * r + q // 4, q % 4 * P:q % 4 * P + m]

        def parity(r, par, n, m):
            return ps[0:n, 2 * r + par, :].rearrange("p (h t) -> p h t", t=P)[:, 0:3, 0:m]

        def bc(ap, axis, size):
            ap = ap.unsqueeze(axis)
            shape = list(ap.shape)
            shape[axis] = size
            return ap.to_broadcast(shape)

        SOLVE = {P: (2, 3, 3, 3, 2, 2, 2), 32: (1, 1, 1)}

        def pe_solve(pe, t, n, weave):
            e = on(pe, "pe_chain")
            units = iter(SOLVE[n])
            I = ident[0:n, 0:n]
            for q in range(6):
                mm = pe.transpose(cell(2, q, n, n), t["m16"][0:n, q, :], I)
            e.mark(mm, "so_mt")
            weave(next(units))
            e.need("so_mt_kept")

            def square(a, at, second=True):
                for q in range(6):
                    mm = pe.matmul(cell(0, q, n, n), t[at][0:n, q, :], t[a][0:n, q, :], start=True, stop=True)
                if second:
                    for q in range(6):
                        mm = pe.matmul(cell(1, q, n, n), t[a][0:n, q, :], t[at][0:n, q, :], start=True, stop=True)
                return mm

            def extend(a):
                for q in range(6):
                    mm = pe.matmul(cell(2, q, n, n), t[a][0:n, q, :], t["tt"][0:n, q, :], start=True, stop=True)
                return mm

            e.mark(square("m16", "mt", n == P), "so_sq")
            weave(next(units))
            e.need("so_sq_kept")
            if n < P:
                e.mark(extend("m2"), "so_ex")
                weave(next(units))
                e.need("so_ex_kept")
                return
            square("m2", "m2t")
            e.mark(extend("m2"), "so_sq")
            weave(next(units))
            e.need("so_sq_kept")
            square("m16", "mt", False)
            e.mark(extend("m16"), "so_sq")
            weave(next(units))
            e.need("so_sq_kept")
            e.mark(extend("m2"), "so_ex")
            weave(next(units))
            e.need("so_ex_kept")
            for q in range(6):
                pe.transpose(cell(0, q, n, n), t["tt"][0:n, q, :], I)
                mm = pe.matmul(cell(1, q, n, n), t["off"][0:n, q, :], t["tt"][0:n, q, :], start=True, stop=True)
            e.mark(mm, "so_sq")
            weave(next(units))
            e.need("so_sq_kept")
            for q in range(6):
                mm = pe.matmul(cell(2, q, n, n), t["m2t"][0:n, q, :], t["m2"][0:n, q, :], start=True, stop=True)
            e.mark(mm, "so_ex")
            weave(next(units))
            e.need("so_ex_kept")

        def dve_solve(dve, t, n, weave):
            e = on(dve, "dve_chain")
            units = iter(SOLVE[n])
            T = lambda k: t[k][0:n, :, :]
            e.link(dve.tensor_copy(T("mt"), region(2, n, n)))
            e.mark(dve.tensor_tensor(T("tt"), T("mt"), bc(ident[0:n, 0:n], 1, 6), ADD), "so_mt_kept")
            weave(next(units))
            e.need("so_sq")
            if n < P:
                e.mark(dve.tensor_copy(T("m2"), region(0, n, n)), "so_sq_kept")
                weave(next(units))
                e.need("so_ex")
                e.mark(dve.tensor_tensor(T("tt"), region(2, n, n), T("tt"), ADD), "so_ex_kept")
                weave(next(units))
                return
            e.link(dve.tensor_copy(T("m2"), region(0, n, n)))
            e.mark(dve.tensor_copy(T("m2t"), region(1, n, n)), "so_sq_kept")
            weave(next(units))
            e.need("so_sq")
            e.link(dve.tensor_copy(T("m16"), region(0, n, n)))
            e.link(dve.tensor_copy(T("mt"), region(1, n, n)))
            e.mark(dve.tensor_tensor(T("tt"), region(2, n, n), T("tt"), ADD), "so_sq_kept")
            weave(next(units))
            e.need("so_sq")
            e.link(dve.tensor_copy(T("m2"), region(0, n, n)))
            e.mark(dve.tensor_tensor(T("tt"), region(2, n, n), T("tt"), ADD), "so_sq_kept")
            weave(next(units))
            e.need("so_ex")
            e.mark(dve.tensor_tensor(T("tt"), region(2, n, n), T("tt"), ADD), "so_ex_kept")
            weave(next(units))
            e.need("so_sq")
            e.link(dve.tensor_copy(T("m2t"), region(0, n, n)))
            e.mark(dve.tensor_copy(T("m2"), region(1, n, n)), "so_sq_kept")
            weave(next(units))
            e.need("so_ex")
            e.mark(dve.tensor_tensor(T("tt"), region(2, n, n), T("tt"), ADD), "so_ex_kept")
            weave(next(units))

        U = dict(feat=6, hist=16, shift=60, rec=6, bfeat=4, lora=6, kk=8, prod=8, tok=2,
                 wz=2, z=1, scz=0, sco=2, s0t=1, ssz=1, sso=3, s8t=1, fin=4,
                 conv=4, head=8, gc=4, aprod=6, az=4, ascz=2, asco=3, assz=0, asso=2,
                 bgk=12, fin2=15, hn=12, afin=8, bfin=10, bprod=3, bsco=1, bsso=4)

        def pool_mixers(pool):
            e = on(pool, "pool_chain2")
            pool.wait_ge(acc_empty, PLAN["inC"]["group0"])
            pool.dma_start(wloraC[0:64, :], i["rwkv_w_up"][0]).then_inc(sem("lora_landed"), 16)
            pool.dma_start(wloraC[64:128, :], i["rwkv_a_up"][0]).then_inc(sem("lora_landed"), 16)
            pool.dma_start(srowC[0:8, :], i["state_rwkv_shift"][0].rearrange("b o n -> (b o) n")).then_inc(sem("lora_landed"), 16)
            e.need("shift_rows")
            pool.dma_start(o["shift_p"][0, 0], srowC[0:1, :]).then_inc(sem("out_stored"), 16)
            pool.dma_start(o["shift_s"][0].rearrange("b o n -> (b o) n"), srowC[1:9, :]).then_inc(sem("out_stored"), 16)
            pool.wait_ge(sem("out_stored"), 32)
            pool.nop().then_inc(sem("shift_stored"), 1)
            stored = 2
            ts = tC[1]
            for g in range(2):
                e.need("C_states")
                for par in range(2):
                    pool.dma_start(o["rwkv_p"][0, 0].rearrange("(p r) v k -> r v p k", r=2)[par][:, 3 * g:3 * g + 3, :],
                                   tC[0]["so"][64 * par:64 * par + 64, :, :]).then_inc(sem("out_stored"), 16)
                stored += 2
                pool.wait_ge(sem("out_stored"), 16 * stored)
                pool.nop().then_inc(sem("C_states_stored"), 1)
            e.need("C_sd_clear")
            def load_sd(p):
                for par in range(2):
                    pool.dma_start(ts["sd"][64 * par:64 * par + 64, :, 64 * par:64 * par + 64],
                                   i["state_rwkv"][0, :, 2 * p + par].rearrange("b v k -> v b k")).then_inc(sem("C_sd"), 16)

            load_sd(0)
            for p in range(BT):
                e.need("C_sd_used")
                if p < BT - 1:
                    load_sd(p + 1)
                e.need("C_so8")
                for par in range(2):
                    pool.dma_start(o["rwkv_s"][0, :, 2 * p + par].rearrange("b v k -> v b k"),
                                   ts["so8"][64 * par:64 * par + 64, :, :]).then_inc(sem("out_stored"), 16)
                stored += 2
                pool.wait_ge(sem("out_stored"), 16 * stored)
                pool.nop().then_inc(sem("C_so8_stored"), 1)
            e.need("C_recurred")
            pool.dma_start(gupC[:, :], i["rwkv_g_up"][0]).then_inc(sem("gup_landed"), 16)
            stored = pool_A(pool, e, stored)
            stored = pool_B(pool, e, stored)

        def pe_mixC(pe, weave):
            e = on(pe, "pe_chain")
            pe.wait_ge(acc_empty, PLAN["inA"]["group0"])
            pe.wait_ge(sem("lora_landed"), 48)
            for m in range(20):
                mm = pe.transpose(ps[:, 0, 8 * m:8 * m + 8], srowC[0:8, m * P:(m + 1) * P], ident[0:8, 0:8])
            e.mark(mm, "shift_turned")
            e.need("shift_last")
            for m in range(20):
                mm = pe.transpose(ps[0:9, 1 + m // 4, m % 4 * P:m % 4 * P + P], slastC[:, m, :], ident[:, :])
            e.mark(mm, "last_turned")
            weave(U["shift"])
            e.need("lora_act")
            e.need("shift_rows")
            for p in range(BT):
                if p > 1:
                    e.need("lora_sig")
                b = 2 * (p % 2)
                pe.matmul(ps[:, b, 0:NT], wloraC[0:64, p * P:(p + 1) * P], proj[0:64, 18, 0:NT], start=True, stop=True)
                mm = pe.matmul(ps[:, b + 1, 0:NT], wloraC[64:128, p * P:(p + 1) * P], proj[64:128, 18, 0:NT], start=True, stop=True)
                e.mark(mm, "lora_mm")
                weave(U["lora"])
            e.need("lora_sig", 2)
            e.need("hn_sq")
            for p in range(BT):
                mm = pe.matmul(ps[:, p, 0:NT], ones64[:, :], sqC[:, p, :], start=True, stop=True)
            e.mark(mm, "hn_sum")
            weave(U["kk"])
            e.need("kk_done")
            for b in range(3):
                m, n, c, nch, t0, _ = kind(b)
                t = tC[b // 2]
                for g in range(2):
                    p0 = 3 * g
                    weave(U["feat"])
                    e.need("feat")
                    for r, (l, rh) in enumerate((("ai", "bi"), ("ki", "ai"), ("bi", "ri"))):
                        for par in range(2):
                            h = slice(64 * par, 64 * par + 64)
                            for p in range(3):
                                mm = pe.matmul(ps[0:n, 2 * r + par, p * P:p * P + n], t[l][h, p, :], t[rh][h, p, :], start=True, stop=True)
                    e.mark(mm, "C_prod")
                    weave(U["prod"])
                    e.need("mats")
                    for par in range(2):
                        h = slice(64 * par, 64 * par + 64)
                        for p in range(3):
                            pe.matmul(ps[0:n, par, p * P:p * P + n], t["ki"][h, p, :], t["ri"][h, p, :], start=True, stop=True)
                    for k, src in enumerate(("kl", "bl", "aa", None)):
                        for p in range(3):
                            a = t[src][:, p, :] if src else proj[:, 12 + p0 + p, t0:t0 + n]
                            mm = pe.transpose(ps[0:n, 2 + k, p * P:(p + 1) * P], a, ident[:, :])
                    e.mark(mm, "C_tok")
                    weave(U["tok"])
                    e.need("C_tok_kept")
                    pe_solve(pe, t, n, weave)
                    for p in range(3):
                        for par in range(2):
                            q, h = 3 * par + p, slice(64 * par, 64 * par + 64)
                            pe.matmul(ps[h, 0, p * P:p * P + n], t["aT"][0:n, p, h], t["tt"][0:n, q, :], start=True, stop=True)
                            mm = pe.matmul(ps[0:n, 2, p * P + 64 * par:p * P + 64 * par + 64], t["nt"][0:n, q, :], t["vT"][0:n, p, h], start=True, stop=True)
                    e.mark(mm, "wz")
                    weave(U["wz"])
                    e.need("wz_kept")
                    for p in range(3):
                        for par in range(2):
                            q, h = 3 * par + p, slice(64 * par, 64 * par + 64)
                            mm = pe.matmul(ps[0:n, 4, p * P + 64 * par:p * P + 64 * par + 64], t["tt"][0:n, q, :], t["nv"][0:n, p, h], start=True, stop=True)
                    e.mark(mm, "C_z")
                    weave(U["z"])
                    e.need("C_z_kept")
                    if n == P:
                        for j in range(nch):
                            u = slice(CP * j, CP * j + CP)
                            for p in range(3):
                                mm = pe.matmul(ps[u, 0, p * P:(p + 1) * P], t["w"][:, p, u], t["s"][:, g, p, :], start=True, stop=True)
                            e.mark(mm, "sc_z")
                            weave(U["scz"])
                            e.need("sc_z_kept")
                            for p in range(3):
                                oc = slice(p * CP, (p + 1) * CP)
                                pe.matmul(ps[:, 2, oc], t["s"][:, g, p, :], t["rr"][:, p, u], start=True, stop=False, skip_group_check=True)
                                for par in range(2):
                                    q, h = 3 * par + p, slice(64 * par, 64 * par + 64)
                                    pe.matmul(ps[h, 2, oc], t["z"][u, p, h], t["qb"][u, q, u], start=False, stop=False, skip_group_check=True)
                                    pe.matmul(ps[h, 2, oc], t["vT"][u, p, h], t["qk"][u, q, u], start=False, stop=True, skip_group_check=True)
                                pe.matmul(ps[:, 4, p * P:(p + 1) * P], t["blT"][u, p, :], t["z"][u, p, :], start=True, stop=False)
                                mm = pe.matmul(ps[:, 4, p * P:(p + 1) * P], t["klT"][u, p, :], t["vT"][u, p, :], start=False, stop=True)
                            e.mark(mm, "sc_os")
                            weave(U["sco"])
                            e.need("sc_s_kept")
                            e.need("sc_o_kept")
                        if b == 1:
                            for p in range(3):
                                mm = pe.transpose(ps[:, 0, p * P:(p + 1) * P], t["s"][:, g, p, :], ident[:, :])
                            e.mark(mm, "C_s_turned")
                            e.need("C_states")
                    else:
                        for p in range(3):
                            e.eng.wait_ge(sem("C_sd"), 32 * (p0 + p + 1))
                            for k in range(NSEQ):
                                mm = pe.transpose(ps[:, k // 4, k % 4 * P:k % 4 * P + P], t["sd"][:, k, :], ident[:, :])
                            e.mark(mm, "C_s0t")
                            weave(U["s0t"])
                            e.need("C_s0_kept")
                            for k in range(NSEQ):
                                u = slice(TS * k, TS * k + TS)
                                pe.matmul(ps[:, 2, u], t["s0"][:, k, :], t["w"][:, p, u], start=True, stop=True)
                                mm = pe.matmul(ps[:, 3, u], t["s0"][:, k, :], t["rr"][:, p, u], start=True, stop=True)
                            e.mark(mm, "ss_z")
                            weave(U["ssz"])
                            e.need("ss_zT_kept")
                            e.mark(pe.transpose(ps[0:32, 4, 0:P], t["zT"][:, :], ident[:, :]), "ss_zt")
                            e.need("ss_z_kept")
                            for par in range(2):
                                q, h = 3 * par + p, slice(64 * par, 64 * par + 64)
                                pe.matmul(ps[h, 5, 0:32], t["z"][0:32, p, h], t["qb"][0:32, q, :], start=True, stop=False, skip_group_check=True)
                                pe.matmul(ps[h, 5, 0:32], t["vT"][0:32, p, h], t["qk"][0:32, q, :], start=False, stop=True, skip_group_check=True)
                            for k in range(2):
                                four = slice(4 * k, 4 * k + 4)
                                out = ps[:, k, :].rearrange("p (b v) -> p b v", v=P)
                                pe.matmul(out, t["blT"][0:32, p, :], t["um"][:, four, :], start=True, stop=False)
                                mm = pe.matmul(out, t["klT"][0:32, p, :], t["vm"][:, four, :], start=False, stop=True)
                            e.mark(mm, "ss_os")
                            weave(U["sso"])
                            e.need("ss_s_kept")
                            for k in range(NSEQ):
                                mm = pe.transpose(ps[:, k // 4, k % 4 * P:k % 4 * P + P], t["s0"][:, k, :], ident[:, :])
                            e.mark(mm, "C_s8t")
                            weave(U["s8t"])
                            e.need("C_so8")
            weave(U["rec"])
            e.need("C_recurred")
            for p in range(BT):
                mm = pe.matmul(ps[:, p, 0:NT], ones64[:, :], ybuf[:, YC + p, :], start=True, stop=True)
            e.mark(mm, "hn_sum")
            weave(U["fin"])
            e.need("hn_sq")
            for p in range(BT):
                mm = pe.matmul(ps[:, p, 0:NT], ones64[:, :], sqF[:, p, :], start=True, stop=True)
            e.mark(mm, "hn_sum")
            weave(U["fin2"])
            e.need("hn_sq")
            for p in range(BT):
                mm = pe.matmul(ps[:, p, 0:NT], ones64[:, :], sqF[:, p, :], start=True, stop=True)
            e.mark(mm, "hn_sum")
            weave(U["fin"])
            e.need("gn_bonus_used")
            pe.wait_ge(sem("gup_landed"), 16)
            for p in range(BT):
                mm = pe.matmul(ps[:, p, 0:NT], gupC[:, p * P:(p + 1) * P], proj[:, 19, 0:NT], start=True, stop=True)
            e.mark(mm, "hn_sum")
            weave(U["fin"])

        def chunks(ap, c):
            return ap.rearrange("p h (j t) -> p h j t", t=c)

        def cums(cs, p0, b, tiles=3):
            _, n, c, nch, _, c0 = kind(b)
            v = cs[:, p0:p0 + tiles, c0:c0 + nch * (c + 1)].rearrange("p h (j t) -> p h j t", t=c + 1)
            rep = lambda k: v[:, :, :, k:k + 1].to_broadcast([P, tiles, nch, c])
            return v[:, :, :, 1:], v[:, :, :, 0:c], rep(c // 2), rep(c), v[:, :, :, c]

        def act_mixC(act, weave):
            e = on(act, "act_chain")
            e.need("last_turned")
            e.mark(act.activation(srowC[0:9, :], psf[0:9, 512:512 + N_C], ACT.Copy), "shift_rows")
            for k in range(20):
                m = (18, 19)[k] if k < 2 else k - 2
                e.need("shifted")
                e.link(act.activation(proj[:, m, 0:TP], shB[:, k % 2, 0:TP], ACT.Copy))
                e.mark(act.activation(proj[:, m, TP:NT].rearrange("p (b t) -> p b t", t=TS),
                                      shB[:, k % 2, TP:TP + NSEQ * 7].rearrange("p (b t) -> p b t", t=7)[:, :, GAP:],
                                      ACT.Copy), "compact")
                weave(U["shift"] // 20)
            e.link(act.activation(proj[0:64, 18, 0:NT], proj[0:64, 18, 0:NT], ACT.Tanh))
            e.mark(act.activation(proj[:, 19, 0:NT], proj[:, 19, 0:NT], ACT.Sigmoid), "lora_act")
            for p in range(BT):
                b = 2 * (p % 2)
                e.need("lora_mm")
                if p > 1:
                    e.need("sgw_used")
                act.activation(sgw[:, p % 2, :], ps[:, b, 0:NT], ACT.Sigmoid, bias=par1[:, R_W0 + p:R_W0 + p + 1])
                e.mark(act.activation(bbC[:, p, :], ps[:, b + 1, 0:NT], ACT.Sigmoid, bias=par1[:, R_A0 + p:R_A0 + p + 1]), "lora_sig")
                weave(U["lora"])
            e.need("fin_eps")
            e.link(act.activation(sqC[:, :, :], sqC[:, :, :], ACT.Ln))
            e.mark(act.activation(sqC[:, :, :], sqC[:, :, :], ACT.Exp, scale=-0.5), "fin_rs")
            weave(U["kk"])
            for b in range(3):
                m, n, c, nch, t0, _ = kind(b)
                t = tC[b // 2]
                for g in range(2):
                    inc, exc, _, _, last = cums(csC, 3 * g, b)
                    e.need("diff")
                    act.activation(t["ri"][:, :, :], t["dm"][:, :, :], ACT.Exp)
                    act.activation(t["ki"][:, :, :], t["dm"][:, :, :], ACT.Exp, scale=-1.0)
                    e.mark(act.activation(t["ai"][:, :, :], t["ai"][:, :, :], ACT.Exp), "C_exps")
                    act.activation(t["kl"][:, :, :], t["kl"][:, :, :], ACT.Exp)
                    act.activation(chunks(t["rr"][:, :, :], c), inc, ACT.Exp)
                    act.activation(chunks(t["aa"][:, :, :], c), exc, ACT.Exp)
                    e.mark(act.activation(t["pl"][:, :, 0:nch], last, ACT.Exp), "C_exps")
                    weave(U["feat"] + U["prod"])
                    e.need("C_tok")
                    for k, dst in enumerate(("klT", "blT", "aT", "vT")):
                        cp = act.activation(t[dst][0:n, :, :], ps[0:n, 2 + k, 0:3 * P].rearrange("p (h t) -> p h t", t=P), ACT.Copy)
                    e.mark(cp, "C_tok_kept")
                    weave(U["tok"] + sum(SOLVE[n]) + U["wz"] + U["z"])
                    if n == P:
                        for j in range(nch):
                            weave(U["scz"])
                            e.need("sc_os")
                            e.mark(act.activation(ybuf[:, YC + 3 * g:YC + 3 * g + 3, t0 + CP * j:t0 + CP * j + CP],
                                                  ps[:, 2, 0:3 * CP].rearrange("p (h t) -> p h t", t=CP), ACT.Copy), "sc_o_kept")
                            weave(U["sco"])
                    else:
                        for p in range(3):
                            weave(U["s0t"])
                            e.need("ss_z")
                            e.mark(act.activation(ybuf[:, YC + 3 * g + p, t0:t0 + n], ps[:, 3, 0:32], ACT.Copy), "ss_o_kept")
                            weave(U["ssz"] + U["sso"] + U["s8t"])
            weave(U["rec"] + U["fin"])
            act_norm_tail(e, act, "C", sqF)
            weave(U["fin2"] + 2 * U["fin"])

        def act_norm_tail(e, act, tag, sq_):
            e.need("fin_eps")
            e.link(act.activation(sq_[:, :, :], sq_[:, :, :], ACT.Ln))
            e.mark(act.activation(sq_[:, :, :], sq_[:, :, :], ACT.Exp, scale=-0.5), "fin_rs")

        def dve_mixC(dve, weave):
            e = on(dve, "dve_chain")
            dve.wait_ge(acc_empty, PLAN["inA"]["group0"])
            e.link(dve.memset(proj[:, 0:20, GAP - 1:GAP], 0.0))
            for k in range(GAP - 1):
                e.link(dve.memset(proj[:, 0:20, SEQW:PW].rearrange("p m (b t) -> p m b t", t=7)[:, :, :, k], 0.0))
            e.need("shift_turned")
            e.link(dve.tensor_copy(proj[:, 0:20, SEQW:PW].rearrange("p m (b t) -> p m b t", t=7)[:, :, :, GAP - 1],
                                   ps[:, 0, 0:160].rearrange("p (m b) -> p m b", b=8)))
            e.link(dve.tensor_copy(slastC[:, :, 0:1], proj[:, 0:20, SEQW - 1:SEQW]))
            e.mark(dve.tensor_copy(slastC[:, :, 1:9], proj[:, 0:20, SEQW:PW].rearrange("p m (b t) -> p m b t", t=7)[:, :, :, 6]), "shift_last")
            for k in range(20):
                m = (18, 19)[k] if k < 2 else k - 2
                if k > 1:
                    e.need("compact")
                W = PW - GAP
                e.link(dve.tensor_tensor(shA[:, k % 2, 0:W], proj[:, m, GAP - 1:PW - 1], proj[:, m, GAP:PW], SUB))
                e.mark(dve.scalar_tensor_tensor(shB[:, k % 2, 0:W], shA[:, k % 2, 0:W], par1[:, R_MU + m:R_MU + m + 1],
                                                proj[:, m, GAP:PW], MUL, ADD), "shifted")
                weave(U["shift"] // 20)
            e.need("compact", 2)
            e.link(dve.memset(padC[:, :], 0.0))
            lead = (TP // CP) * (CP + 1)
            for p in range(BT):
                e.need("lora_sig")
                for a, c, lo_, hi_, s0, s1 in ((0, CP, 0, lead, 0, TP), (0, CS, lead, CW, TP, NT)):
                    ins = dve.tensor_scalar(padC[:, lo_:hi_].rearrange("p (j t) -> p j t", t=c + 1)[:, :, 1:],
                                            sgw[:, p % 2, s0:s1].rearrange("p (j t) -> p j t", t=c), NEG, None, MUL)
                    if s0:
                        e.mark(ins, "sgw_used")
                    else:
                        e.link(ins)
                e.link(dve.tensor_tensor_scan(csC[:, p, :], notlead[:, :], padC[:, :], 0.0, MUL, ADD))
                k_ = proj[:, 6 + p, 0:NT]
                e.link(dve.tensor_scalar(kkC[:, p, :], k_, par1[:, R_KK + p:R_KK + p + 1], None, MUL))
                e.link(dve.tensor_scalar(shA[:, 0, 0:NT], bbC[:, p, :], 1.0, par1[:, R_KA + p:R_KA + p + 1], SUB, MUL))
                e.link(dve.scalar_tensor_tensor(k_, shA[:, 0, 0:NT], 1.0, k_, ADD, MUL))
                weave(U["lora"])
            dve.wait_ge(sem("shift_stored"), 1)
            e.mark(dve.tensor_tensor(sqC[:, :, :], kkC[:, :, :], kkC[:, :, :], MUL), "hn_sq")
            e.need("hn_sum")
            e.mark(dve.tensor_scalar(sqC[:, :, :], ps[:, 0:6, 0:NT], 1e-6, None, ADD), "fin_eps")
            e.need("fin_rs")
            e.link(dve.tensor_tensor(kkC[:, :, :], kkC[:, :, :], sqC[:, :, :], MUL))
            e.mark(dve.tensor_tensor(bbC[:, :, :], bbC[:, :, :], kkC[:, :, :], MUL), "kk_done")
            weave(U["kk"])
            e.link(dve.memset(tC[0]["s"][:, :, :, :], 0.0))
            for b in range(3):
                m, n, c, nch, t0, _ = kind(b)
                t = tC[b // 2]
                if b == 2:
                    dve.wait_ge(sem("C_states_stored"), 2)
                    e.mark(dve.memset(t["sd"][:, :, :], 0.0), "C_sd_clear")
                for g in range(2):
                    p0 = 3 * g
                    inc, exc, mid, end, _ = cums(csC, p0, b)
                    C = lambda k: chunks(t[k][:, :, :], c)
                    A = lambda k: t[k][:, :, :]
                    e.link(dve.tensor_tensor(C("dm"), inc, mid, SUB))
                    e.link(dve.tensor_tensor(C("ai"), exc, mid, SUB))
                    e.mark(dve.tensor_tensor(C("kl"), end, inc, SUB), "diff")
                    e.need("C_exps")
                    r_, k_ = proj[:, p0:p0 + 3, t0:t0 + n], proj[:, 6 + p0:9 + p0, t0:t0 + n]
                    kk_, bb_ = kkC[:, p0:p0 + 3, t0:t0 + n], bbC[:, p0:p0 + 3, t0:t0 + n]
                    e.link(dve.tensor_tensor(A("ri"), r_, A("ri"), MUL))
                    e.link(dve.tensor_tensor(A("bi"), bb_, A("ki"), MUL))
                    e.link(dve.tensor_tensor(A("ki"), k_, A("ki"), MUL))
                    e.mark(dve.scalar_tensor_tensor(A("ai"), kk_, -1.0, A("ai"), MUL, MUL), "feat")
                    e.need("C_exps")
                    e.link(dve.tensor_tensor(A("bl"), bb_, A("kl"), MUL))
                    e.link(dve.tensor_tensor(A("kl"), k_, A("kl"), MUL))
                    e.link(dve.tensor_tensor(A("rr"), r_, A("rr"), MUL))
                    e.link(dve.scalar_tensor_tensor(A("aa"), kk_, -1.0, A("aa"), MUL, MUL))
                    weave(U["feat"] + U["prod"])
                    e.need("C_prod")
                    for par in range(2):
                        q = slice(3 * par, 3 * par + 3)
                        mb = lambda k: bc(m[k][:, :], 1, 3)
                        e.link(dve.tensor_tensor(t["m16"][0:n, q, :], parity(0, par, n, n), mb("l16"), MUL))
                        if n == P:
                            e.link(dve.tensor_tensor(t["off"][0:n, q, :], parity(0, par, n, n), mb("off"), MUL))
                        e.link(dve.tensor_tensor(t["nt"][0:n, q, :], parity(1, par, n, n), mb("us"), MUL))
                        ins = dve.tensor_tensor(t["qb"][0:n, q, :], parity(2, par, n, n), mb("ui"), MUL)
                        if par:
                            e.mark(ins, "mats")
                        else:
                            e.link(ins)
                    weave(U["tok"])
                    e.need("C_tok")
                    for par in range(2):
                        e.link(dve.tensor_tensor(t["qk"][0:n, 3 * par:3 * par + 3, :], parity(0, par, n, n), mb("ui"), MUL))
                    e.need("so_mt")
                    dve_solve(dve, t, n, weave)
                    e.need("wz")
                    e.link(dve.tensor_copy(t["w"][:, :, 0:n], ps[:, 0, :].rearrange("p (h t) -> p h t", t=P)[:, 0:3, 0:n]))
                    e.mark(dve.tensor_copy(t["nv"][0:n, :, :], ps[0:n, 2, 0:3 * P].rearrange("p (h t) -> p h t", t=P)), "wz_kept")
                    weave(U["wz"])
                    e.need("C_z")
                    e.mark(dve.tensor_copy(t["zb"][0:n, :, :], ps[0:n, 4, 0:3 * P].rearrange("p (h t) -> p h t", t=P)), "C_z_kept")
                    weave(U["z"])
                    if n == P:
                        for j in range(nch):
                            u = slice(CP * j, CP * j + CP)
                            e.need("sc_z")
                            e.mark(dve.tensor_tensor(t["z"][u, :, :], ps[u, 0, 0:3 * P].rearrange("p (h t) -> p h t", t=P),
                                                     t["zb"][u, :, :], ADD), "sc_z_kept")
                            for par in range(2):
                                h = slice(64 * par, 64 * par + 64)
                                e.link(dve.tensor_tensor(t["sw"][h, :, h], t["s"][h, g, :, h],
                                                         t["pl"][h, :, j:j + 1].to_broadcast([64, 3, 64]), MUL))
                            weave(U["scz"])
                            e.need("sc_os")
                            for par in range(2):
                                h = slice(64 * par, 64 * par + 64)
                                s = t["s"][h, g, :, h]
                                ins = dve.tensor_tensor(s, ps[h, 4, 0:3 * P].rearrange("p (h t) -> p h t", t=P)[:, :, h], t["sw"][h, :, h], ADD)
                                if par:
                                    e.mark(ins, "sc_s_kept")
                                else:
                                    e.link(ins)
                            weave(U["sco"])
                        if b == 1:
                            e.need("C_s_turned")
                            if g:
                                dve.wait_ge(sem("C_states_stored"), 1)
                            for par in range(2):
                                h = slice(64 * par, 64 * par + 64)
                                ins = dve.tensor_copy(t["so"][h, :, :], ps[h, 0, 0:3 * P].rearrange("p (h t) -> p h t", t=P)[:, :, h])
                                if par:
                                    e.mark(ins, "C_states")
                                else:
                                    e.link(ins)
                            dve.wait_ge(sem("C_states_stored"), g + 1)
                    else:
                        for p in range(3):
                            e.need("C_s0t")
                            e.mark(dve.tensor_copy(t["s0"][:, :, :], psf[:, 0:1024].rearrange("p (b v) -> p b v", v=P)), "C_s0_kept")
                            weave(U["s0t"])
                            dve.nop().then_inc(sem("C_sd_used"), 1)
                            e.need("ss_z")
                            e.mark(dve.tensor_copy(t["zT"][:, :], ps[:, 2, 0:32]), "ss_zT_kept")
                            e.need("ss_zt")
                            e.link(dve.tensor_tensor(t["z"][0:32, p, :], ps[0:32, 4, 0:P], t["zb"][0:32, p, :], ADD))
                            sm = bc(seqmask[:, :], 2, P)
                            e.link(dve.tensor_tensor(t["um"][:, :, :], bc(t["z"][0:32, p, :], 1, NSEQ), sm, MUL))
                            e.mark(dve.tensor_tensor(t["vm"][:, :, :], bc(t["vT"][0:32, p, :], 1, NSEQ), sm, MUL), "ss_z_kept")
                            weave(U["ssz"] + U["sso"])
                            e.need("ss_os")
                            e.link(dve.tensor_tensor(t["s0"][:, :, :], t["s0"][:, :, :], bc(t["pl"][:, p, :], 2, P), MUL))
                            e.mark(dve.tensor_tensor(t["s0"][:, :, :], psf[:, 0:1024].rearrange("p (b v) -> p b v", v=P),
                                                     t["s0"][:, :, :], ADD), "ss_s_kept")
                            e.need("ss_o_kept")
                            yy = ybuf[:, YC + p0 + p, t0:t0 + n]
                            e.link(dve.tensor_tensor(yy, ps[:, 5, 0:32], yy, ADD))
                            e.need("C_s8t")
                            if p0 + p:
                                dve.wait_ge(sem("C_so8_stored"), p0 + p)
                            for par in range(2):
                                h = slice(64 * par, 64 * par + 64)
                                ins = dve.tensor_copy(t["so8"][h, :, :], psf[h, 0:1024].rearrange("p (b v) -> p b v", v=P)[:, :, h])
                                if par:
                                    e.mark(ins, "C_so8")
                                else:
                                    e.link(ins)
                            weave(U["s8t"])
            weave(U["rec"])
            dve.wait_ge(sem("C_so8_stored"), 6)
            dve.nop().then_inc(sem("C_recurred"), 1)
            Y = ybuf[:, YC:YC + 6, :]
            PS6 = ps[:, 0:6, 0:NT]
            weave(U["fin"])
            e.need("hn_sum")
            e.link(dve.scalar_tensor_tensor(Y, PS6, -1.0 / 64, Y, MUL, ADD))
            e.mark(dve.tensor_tensor(sqF[:, :, :], Y, Y, MUL), "hn_sq")
            e.need("hn_sum")
            e.mark(dve.tensor_scalar(sqF[:, :, :], PS6, 1.0 / 64, GN_EPS, MUL, ADD), "fin_eps")
            e.need("fin_rs")
            e.link(dve.tensor_tensor(Y, Y, sqF[:, :, :], MUL))
            weave(U["fin2"])
            for p in range(BT):
                e.link(dve.tensor_scalar(Y[:, p, :], Y[:, p, :], par1[:, R_LNW + p:R_LNW + p + 1], par1[:, R_LNB + p:R_LNB + p + 1], MUL, ADD))
                ins = dve.scalar_tensor_tensor(sqF[:, p, :], proj[:, p, 0:NT], par1[:, R_RK + p:R_RK + p + 1], proj[:, 6 + p, 0:NT], MUL, MUL)
                if p < 5:
                    e.link(ins)
                else:
                    e.mark(ins, "hn_sq")
            weave(U["fin"])
            e.need("hn_sum")
            e.mark(dve.tensor_tensor(sqF[:, :, :], PS6, proj[:, 12:18, 0:NT], MUL), "gn_bonus_used")
            e.link(dve.tensor_tensor(Y, Y, sqF[:, :, :], ADD))
            weave(U["fin"])
            e.need("hn_sum")
            e.link(dve.tensor_tensor(Y, PS6, Y, MUL))
            dve.nop().then_inc(sem("mixer_done"), 1)

        startA = arena0 + 24 * PW * 4
        preA = Map(startA, y_a)
        rowsA = preA("rowsA", [27, 2304])
        lastA = preA("lastA", [P, 18, 27])
        cvA = preA("cvA", [P, 2, PW])
        sqA = preA("sqA", [P, BT, NT])

        def maps_A(n, tag):
            m = Map(startA, y_a)
            t = recur_tiles(m, n, tag, 6, ("dt",))
            al = Map(startA, y_a)
            for k in ("w", "zb", "z"):
                t[k] = (al if n == P else m)(k + tag, [P, 6, P])
            for k in ("gb", "dd"):
                t[k] = (al if n == P else m)(k + tag, [P, 6, P])
            t["eg"] = (al if n == P else m)("eg" + tag, [P, 6, n])
            for k in ("kb", "kd", "vb"):
                t[k] = m(k + tag, [P, 6, P])
            for k in ("ba", "ex"):
                t[k] = m(k + tag, [P, 2, 6])
            for k in ("be", "nb", "g", "gc", "gd"):
                t[k] = m(k + tag, [P, 6])
            t["pl"] = m("pl" + tag, [P, 6, 8])
            if n == P:
                t["s"] = m("sA", [P, 6, P])
                t["sw"] = Map(startA + 3 * 6 * n * 4, y_a)("swA", [P, 6, P])
            else:
                for k in range(2):
                    t["s0", k] = m(f"s0A{k}", [P, NSEQ, P])
                t["um"] = m("umA", [32, NSEQ, P])
                t["zT"] = m("zTA", [P, 32])
            return t

        tA = [maps_A(P, "Ap"), maps_A(32, "As")]
        finA = Map(startA, y_a)
        sqG = finA("sqG", [P, BT, NT])
        zgG = finA("zgG", [P, BT, NT])

        def pool_A(pool, e, stored):
            pool.wait_ge(sem("mixer_done"), 1)
            pool.dma_start(rowsA[0:24, :], i["state_gdn_conv"][0].rearrange("b j n -> (b j) n")).then_inc(sem("a_landed"), 16)
            pool.wait_ge(sem("kept_stored"), 16 * GROUPS_A)
            for k in range(4):
                pool.dma_start(proj[:, 6 * k:6 * k + 6, :], projA[:, 6 * k:6 * k + 6, :]).then_inc(sem("projA_landed"), 16)
            pool.dma_start(gkupB[:, :], i["gla_gk_up"][0]).then_inc(sem("gk_landed"), 16)
            for k, name in ((0, "a_log"), (1, "dt_bias")):
                pool.dma_start(smA[:, k, :], i[name][0].partition_broadcast(P)).then_inc(sem("a_landed"), 16)
            e.need("A_rows")
            pool.dma_start(o["conv_p"][0, 0], rowsA[0:3, :]).then_inc(sem("out_stored"), 16)
            pool.dma_start(o["conv_s"][0].rearrange("b j n -> (b j) n"), rowsA[3:27, :]).then_inc(sem("out_stored"), 16)
            stored += 2
            pool.wait_ge(sem("out_stored"), 16 * stored)
            pool.nop().then_inc(sem("A_rows_stored"), 1)
            e.need("state_whole")
            pool.dma_start(o["gdn_p"][0, 0].rearrange("h k v -> k h v"), tA[0]["s"][:, :, :]).then_inc(sem("out_stored"), 16)
            stored += 1
            pool.wait_ge(sem("out_stored"), 16 * stored)
            pool.nop().then_inc(sem("state_stored"), 1)
            return sample_states(pool, e, stored, tA[1], 6, "A",
                                 lambda h: i["state_gdn"][0, :, h].rearrange("b k v -> k b v"),
                                 lambda h: o["gdn_s"][0, :, h].rearrange("b k v -> k b v"))

        def sample_states(pool, e, stored, t, count, tag, src, dst):
            def load(h):
                pool.dma_start(t["s0", h % 2][:, :, :], src(h)).then_inc(sem(f"{tag}_s0_{h % 2}"), 16)

            load(0)
            load(1)
            for h in range(count):
                e.need("s_new")
                pool.dma_start(dst(h), t["s0", h % 2][:, :, :]).then_inc(sem("out_stored"), 16)
                stored += 1
                pool.wait_ge(sem("out_stored"), 16 * stored)
                if h + 2 < count:
                    load(h + 2)
            pool.nop().then_inc(sem("s_stored"), 1)
            return stored

        def pe_mixA(pe, weave):
            e = on(pe, "pe_chain")
            weave(U["hist"])
            pe.wait_ge(sem("a_landed"), 48)
            for m in range(18):
                mm = pe.transpose(ps[:, 0, 24 * m:24 * m + 24], rowsA[0:24, m * P:(m + 1) * P], ident[0:24, 0:24])
            e.mark(mm, "A_hist")
            e.need("A_last")
            for m in range(18):
                mm = pe.transpose(ps[0:27, 1 + m // 4, m % 4 * P:m % 4 * P + P], lastA[:, m, :], ident[:, :])
            e.mark(mm, "A_last_turned")
            weave(18 * U["conv"])
            weave(U["hn"])
            e.need("A_rows")
            for half in range(2):
                e.need("hn_sq")
                for h in range(6):
                    mm = pe.matmul(ps[:, h, 0:NT], ones[:, :], sqA[:, h, :], start=True, stop=True)
                e.mark(mm, "hn_sum")
                weave(U["head"])
            e.need("A_normed")
            for b in range(3):
                m, n, c, nch, t0, _ = kind(b)
                t = tA[b // 2]
                cols = slice(t0, t0 + n)
                e.mark(pe.transpose(ps[0:n, 0, 0:12], low[0:12, 0, cols], ident[0:12, 0:12]), "A_ba")
                e.need("A_g")
                pe.matmul(ps[0:n, 1, 0:6], m["ui"][:, :], t["g"][0:n, :], start=True, stop=True)
                pe.matmul(ps[0:n, 1, 8:14], m["same"][:, :], t["g"][0:n, :], start=True, stop=True)
                for h in range(6):
                    mm = pe.matmul(cell(1, h, P, n), t["gb"][0:n, h, :], m["ui"][:, :], start=True, stop=True)
                e.mark(mm, "A_gc")
                weave(U["gc"])
                e.need("A_exps")
                for h in range(6):
                    q_, k_ = proj[:, h, cols], proj[:, 6 + h, cols]
                    pe.matmul(cell(0, h, n, n), k_, k_, start=True, stop=True)
                    pe.matmul(cell(1, h, n, n), k_, q_, start=True, stop=True)
                    mm = pe.transpose(cell(2, h, n, P), k_, ident[:, :])
                e.mark(mm, "A_prod")
                weave(U["aprod"])
                e.need("mats")
                for h in range(6):
                    pe.transpose(cell(0, h, n, P), proj[:, 12 + h, cols], ident[:, :])
                pe_solve(pe, t, n, weave)
                for h in range(6):
                    pe.matmul(cell(0, h, P, n), t["kb"][0:n, h, :], t["tt"][0:n, h, :], start=True, stop=True)
                    mm = pe.matmul(cell(1, h, n, P), t["tt"][0:n, h, :], t["vb"][0:n, h, :], start=True, stop=True)
                e.mark(mm, "wz")
                weave(U["az"])
                e.need("wz_kept")
                if n == P:
                    for j in range(nch):
                        u = slice(CP * j, CP * j + CP)
                        for h in range(6):
                            mm = pe.matmul(ps[u, h // 4, h % 4 * P:h % 4 * P + P], t["w"][:, h, u], t["s"][:, h, :], start=True, stop=True)
                        e.mark(mm, "sc_z")
                        weave(U["ascz"])
                        e.need("sc_z_kept")
                        for h in range(6):
                            oc = slice(h * CP, (h + 1) * CP)
                            pe.matmul(ps[:, 4, oc], t["s"][:, h, :], proj[:, h, t0 + CP * j:t0 + CP * j + CP], start=True, stop=False)
                            pe.matmul(ps[:, 4, oc], t["z"][u, h, :], t["dt"][u, h, u], start=False, stop=True)
                            mm = pe.matmul(cell(1, h, P, P), t["kd"][u, h, :], t["z"][u, h, :], start=True, stop=True)
                        e.mark(mm, "sc_os")
                        weave(U["asco"])
                        e.need("sc_s_kept")
                        e.need("sc_o_kept")
                else:
                    for h in range(6):
                        pe.wait_ge(sem(f"A_s0_{h % 2}"), 16 * (h // 2 + 1))
                        s0 = t["s0", h % 2]
                        for k in range(NSEQ):
                            u = slice(TS * k, TS * k + TS)
                            pe.matmul(ps[:, 2, u], s0[:, k, :], t["w"][:, h, u], start=True, stop=True)
                            mm = pe.matmul(ps[:, 3, u], s0[:, k, :], proj[:, h, t0 + TS * k:t0 + TS * k + TS], start=True, stop=True)
                        e.mark(mm, "ss_z")
                        weave(U["assz"])
                        e.need("ss_zT_kept")
                        e.mark(pe.transpose(ps[0:32, 4, 0:P], t["zT"][:, :], ident[:, :]), "ss_zt")
                        e.need("ss_z_kept")
                        pe.matmul(ps[:, 5, 0:32], t["z"][0:32, h, :], t["dt"][0:32, h, :], start=True, stop=True)
                        for k in range(2):
                            mm = pe.matmul(ps[:, k, :].rearrange("p (b v) -> p b v", v=P), t["kd"][0:32, h, :],
                                           t["um"][:, 4 * k:4 * k + 4, :], start=True, stop=True)
                        e.mark(mm, "ss_os")
                        weave(U["asso"])
                        e.need("ss_s_kept")
            weave(U["afin"])
            pe_head_norm(e, pe, "A", sqG)
            weave(U["afin"])

        def pe_head_norm(e, pe, tag, sq_):
            e.need("hn_sq")
            for h in range(6):
                mm = pe.matmul(ps[:, h, 0:NT], ones[:, :], sq_[:, h, :], start=True, stop=True)
            e.mark(mm, "hn_sum")

        def act_mixA(act, weave):
            e = on(act, "act_chain")
            weave(U["hist"])
            act.wait_ge(sem("a_landed"), 48)
            e.link(act.activation(smA[:, 0, :], smA[:, 0, :], ACT.Exp))
            e.need("A_last_turned")
            e.mark(act.activation(rowsA[0:27, :], psf[0:27, 512:512 + 2304], ACT.Copy), "A_rows")
            for m in range(18):
                e.need("A_conv")
                e.link(act.activation(proj[:, m, 0:TP], cvA[:, m % 2, 0:TP], ACT.Silu))
                e.mark(act.activation(proj[:, m, TP:NT].rearrange("p (b t) -> p b t", t=TS),
                                      cvA[:, m % 2, SEQW:PW].rearrange("p (b t) -> p b t", t=7)[:, :, 0:TS],
                                      ACT.Silu), "A_silu")
                weave(U["conv"])
            weave(U["hn"])
            for half in range(2):
                e.need("fin_eps")
                e.link(act.activation(sqA[:, :, :], sqA[:, :, :], ACT.Ln))
                e.mark(act.activation(sqA[:, :, :], sqA[:, :, :], ACT.Exp, scale=-0.5), "fin_rs")
                weave(U["head"])
            for b in range(3):
                m, n, c, nch, t0, _ = kind(b)
                t = tA[b // 2]
                e.need("A_ba_kept")
                e.link(act.activation(t["ex"][0:n, :, :], t["ex"][0:n, :, :], ACT.Exp, scale=-1.0))
                e.mark(act.activation(t["be"][0:n, :], t["ex"][0:n, 1, :], ACT.Ln, bias=ones[0:n, 0:1]), "A_ln")
                e.need("A_dd")
                act.activation(t["eg"][:, :, :], region(1, n, n, slice(0, P)), ACT.Exp)
                act.activation(t["pl"][:, :, 0:nch], region(1, n, n, slice(0, P)).rearrange("p h (j t) -> p h j t", t=c)[:, :, :, c - 1], ACT.Exp)
                act.activation(t["dt"][0:n, :, :], t["dt"][0:n, :, :], ACT.Exp)
                act.activation(t["dd"][0:n, :, 0:n], t["dd"][0:n, :, 0:n], ACT.Exp, scale=-1.0)
                act.activation(t["gc"][0:n, :], t["gc"][0:n, :], ACT.Exp)
                e.mark(act.activation(t["gd"][0:n, :], t["gd"][0:n, :], ACT.Exp), "A_exps")
                weave(U["gc"] + U["aprod"] + sum(SOLVE[n]) + U["az"])
                if n == P:
                    for j in range(nch):
                        weave(U["ascz"])
                        e.need("sc_os")
                        e.mark(act.activation(ybuf[:, YA:YA + 6, t0 + CP * j:t0 + CP * j + CP],
                                              ps[:, 4, 0:6 * CP].rearrange("p (h t) -> p h t", t=CP), ACT.Copy), "sc_o_kept")
                        weave(U["asco"])
                else:
                    for h in range(6):
                        e.need("ss_z")
                        e.mark(act.activation(ybuf[:, YA + h, t0:t0 + n], ps[:, 3, 0:32], ACT.Copy), "ss_o_kept")
                        weave(U["assz"] + U["asso"])
            weave(U["afin"])
            e.need("A_fin")
            e.link(act.activation(zgG[:, :, 0:TP], proj[:, 18:24, GAP:SEQW], ACT.Silu))
            for h in range(6):
                e.link(act.activation(zgG[:, h, TP:NT].rearrange("p (b t) -> p b t", t=TS),
                                      proj[:, 18 + h, SEQW:PW].rearrange("p (b t) -> p b t", t=7)[:, :, GAP:], ACT.Silu))
            act_norm_tail(e, act, "A", sqG)
            weave(U["afin"])

        def dve_mixA(dve, weave):
            e = on(dve, "dve_chain")
            weave(U["hist"])
            e.need("A_hist")
            dve.wait_ge(sem("projA_landed"), 64)
            for m in range(18):
                e.link(dve.tensor_copy(proj[:, m, SEQW:PW].rearrange("p (b t) -> p b t", t=7)[:, :, 0:GAP],
                                       ps[:, 0, 24 * m:24 * m + 24].rearrange("p (b t) -> p b t", t=GAP)))
            e.link(dve.tensor_copy(lastA[:, :, 0:GAP], proj[:, 0:18, TP:SEQW]))
            for m in range(18):
                ins = dve.tensor_copy(lastA[:, m, GAP:27].rearrange("p (b t) -> p b t", t=GAP),
                                      proj[:, m, SEQW:PW].rearrange("p (b t) -> p b t", t=7)[:, :, TS:])
                if m < 17:
                    e.link(ins)
                else:
                    e.mark(ins, "A_last")
            W = PW - GAP
            for m in range(18):
                if m > 1:
                    e.need("A_silu")
                cv = cvA[:, m % 2, 0:W]
                tap = lambda j: par2[:, j * 18 + m:j * 18 + m + 1]
                e.link(dve.tensor_scalar(cv, proj[:, m, 0:W], tap(0), None, MUL))
                for j in (1, 2):
                    e.link(dve.scalar_tensor_tensor(cv, proj[:, m, j:j + W], tap(j), cv, MUL, ADD))
                e.mark(dve.scalar_tensor_tensor(cv, proj[:, m, 3:3 + W], tap(3), cv, MUL, ADD), "A_conv")
                weave(U["conv"])
            weave(U["hn"])
            e.need("A_silu", 2)
            for half in range(2):
                v = proj[:, 6 * half:6 * half + 6, 0:NT]
                e.mark(dve.tensor_tensor(sqA[:, :, :], v, v, MUL), "hn_sq")
                e.need("hn_sum")
                e.mark(dve.tensor_scalar(sqA[:, :, :], ps[:, 0:6, 0:NT], 1e-6, None, ADD), "fin_eps")
                e.need("fin_rs")
                if half:
                    e.mark(dve.tensor_tensor(v, v, sqA[:, :, :], MUL), "A_normed")
                else:
                    e.link(dve.tensor_tensor(v, v, sqA[:, :, :], MUL))
                    e.link(dve.tensor_scalar(v, v, 128 ** -0.5, None, MUL))
                weave(U["head"])
            dve.wait_ge(sem("A_rows_stored"), 1)
            e.link(dve.tensor_scalar(smA[:, 0, :], smA[:, 0, :], -1.0, None, MUL))
            e.link(dve.memset(tA[0]["s"][:, :, :], 0.0))
            for b in range(3):
                m, n, c, nch, t0, _ = kind(b)
                t = tA[b // 2]
                if b == 2:
                    dve.nop().then_inc(sem("state_whole"), 1)
                    dve.wait_ge(sem("state_stored"), 1)
                R = lambda k: t[k][0:n, :]
                T = lambda k: t[k][0:n, :, 0:n]
                e.need("A_ba")
                e.link(dve.tensor_copy(t["ba"][0:n, :, :], ps[0:n, 0, 0:12].rearrange("p (a h) -> p a h", a=2)))
                e.link(dve.tensor_tensor(t["ba"][0:n, 1, :], t["ba"][0:n, 1, :], smA[0:n, 1, :], ADD))
                e.link(dve.tensor_copy(t["ex"][0:n, 0, :], t["ba"][0:n, 0, :]))
                e.mark(dve.scalar_tensor_tensor(t["ex"][0:n, 1, :], t["ba"][0:n, 1, :], -1.0, t["ba"][0:n, 1, :], MUL, ALU.max), "A_ba_kept")
                e.need("A_ln")
                e.link(dve.scalar_tensor_tensor(R("g"), t["ba"][0:n, 1, :], 0.0, R("be"), ALU.max, ADD))
                e.link(dve.tensor_tensor(R("g"), R("g"), smA[0:n, 0, :], MUL))
                e.mark(dve.tensor_copy(t["gb"][0:n, :, :], bc(R("g"), 2, P)), "A_g")
                e.link(dve.tensor_scalar(t["ex"][0:n, 0, :], t["ex"][0:n, 0, :], 1.0, None, ADD))
                e.link(dve.reciprocal(R("be"), t["ex"][0:n, 0, :]))
                e.link(dve.tensor_scalar(R("nb"), R("be"), -1.0, None, MUL))
                e.need("A_gc")
                e.link(dve.tensor_copy(R("gc"), ps[0:n, 1, 0:6]))
                e.link(dve.tensor_tensor(R("gd"), ps[0:n, 1, 8:14], R("gc"), SUB))
                e.link(dve.tensor_tensor(T("dd"), region(1, n, n), bc(R("gc"), 2, n), SUB))
                e.link(dve.tensor_scalar(T("dt"), T("dd"), 0.0, None, ALU.min))
                e.mark(dve.tensor_scalar(T("dd"), T("dd"), 0.0, None, ALU.max), "A_dd")
                weave(U["gc"])
                e.need("A_exps")
                e.link(dve.tensor_tensor(T("dt"), T("dt"), bc(m["ui"][:, :], 1, 6), MUL))
                e.link(dve.tensor_tensor(T("dd"), T("dd"), bc(R("nb"), 2, n), MUL))
                e.link(dve.tensor_tensor(T("m16"), T("dd"), bc(m["l16"][:, :], 1, 6), MUL))
                if n == P:
                    e.link(dve.tensor_tensor(T("off"), T("dd"), bc(m["off"][:, :], 1, 6), MUL))
                e.link(dve.tensor_tensor(R("nb"), R("nb"), R("gc"), MUL))
                e.need("A_prod")
                e.link(dve.tensor_tensor(T("m16"), region(0, n, n), T("m16"), MUL))
                if n == P:
                    e.link(dve.tensor_tensor(T("off"), region(0, n, n), T("off"), MUL))
                e.link(dve.tensor_tensor(T("dt"), region(1, n, n), T("dt"), MUL))
                e.link(dve.tensor_tensor(t["kb"][0:n, :, :], region(2, n, P), bc(R("nb"), 2, P), MUL))
                e.link(dve.tensor_tensor(t["kd"][0:n, :, :], region(2, n, P), bc(R("gd"), 2, P), MUL))
                q_ = proj[:, 0:6, t0:t0 + n]
                e.mark(dve.tensor_tensor(q_, q_, t["eg"][:, :, :], MUL), "mats")
                weave(U["aprod"])
                e.need("so_mt")
                e.link(dve.tensor_tensor(t["vb"][0:n, :, :], region(0, n, P), bc(R("be"), 2, P), MUL))
                dve_solve(dve, t, n, weave)
                e.need("wz")
                e.link(dve.tensor_copy(t["w"][:, :, 0:n], region(0, n, n, slice(0, P))))
                e.mark(dve.tensor_copy(t["zb"][0:n, :, :], region(1, n, P)), "wz_kept")
                weave(U["az"])
                if n == P:
                    for j in range(nch):
                        u = slice(CP * j, CP * j + CP)
                        e.need("sc_z")
                        e.mark(dve.tensor_tensor(t["z"][u, :, :], region(0, n, P, u), t["zb"][u, :, :], ADD), "sc_z_kept")
                        s, sw = t["s"][:, :, :], t["sw"][:, :, :]
                        e.link(dve.tensor_tensor(sw, s, t["pl"][:, :, j:j + 1].to_broadcast([P, 6, P]), MUL))
                        weave(U["ascz"])
                        e.need("sc_os")
                        e.mark(dve.tensor_tensor(s, region(1, P, P), sw, ADD), "sc_s_kept")
                        weave(U["asco"])
                else:
                    for h in range(6):
                        e.need("ss_z")
                        e.mark(dve.tensor_copy(t["zT"][:, :], ps[:, 2, 0:32]), "ss_zT_kept")
                        e.need("ss_zt")
                        e.link(dve.tensor_tensor(t["z"][0:32, h, :], ps[0:32, 4, 0:P], t["zb"][0:32, h, :], ADD))
                        e.mark(dve.tensor_tensor(t["um"][:, :, :], bc(t["z"][0:32, h, :], 1, NSEQ), bc(seqmask[:, :], 2, P), MUL), "ss_z_kept")
                        weave(U["assz"] + U["asso"])
                        e.need("ss_os")
                        s0 = t["s0", h % 2][:, :, :]
                        e.link(dve.tensor_tensor(s0, s0, bc(t["pl"][:, h, :], 2, P), MUL))
                        e.mark(dve.tensor_tensor(s0, psf[:, 0:1024].rearrange("p (b v) -> p b v", v=P), s0, ADD), "s_new")
                        e.need("ss_o_kept")
                        yy = ybuf[:, YA + h, t0:t0 + n]
                        e.mark(dve.tensor_tensor(yy, ps[:, 5, 0:32], yy, ADD), "ss_s_kept")
            weave(U["afin"])
            dve.wait_ge(sem("s_stored"), 1)
            dve.nop().then_inc(sem("A_fin"), 1)
            dve_head_norm(e, dve, "A", sqG, zgG[:, :, :], YA, R_GDN)
            weave(U["afin"])
            dve.nop().then_inc(sem("mixer_done"), 1)

        def dve_head_norm(e, dve, tag, sq_, gate, y0, gain, meanwhile=None):
            Y = ybuf[:, y0:y0 + 6, :]
            e.mark(dve.tensor_tensor(sq_[:, :, :], Y, Y, MUL), "hn_sq")
            e.need("hn_sum")
            e.mark(dve.tensor_scalar(sq_[:, :, :], ps[:, 0:6, 0:NT], 1.0 / P, EPS, MUL, ADD), "fin_eps")
            if meanwhile:
                meanwhile(0, 2 * BT)
            e.need("fin_rs")
            e.link(dve.scalar_tensor_tensor(Y, Y, par1[:, gain:gain + 1], sq_[:, :, :], MUL, MUL))
            e.link(dve.tensor_tensor(Y, Y, gate, MUL))

        startB = arena0 + 18 * PW * 4
        mapB = Map(startB, y_at)
        csB = mapB("csB", [P, 3, CW])
        startB = mapB.at
        preB = Map(startB, y_at)
        gkupB = Map(y_at - 2048, y_at)("gkupB", [RANK, 384])
        gxB = preB("gxB", [P, 3, NT])
        glB = preB("glB", [P, 3, NT])
        padB = preB("padB", [P, CW])

        def maps_B(n, tag):
            m = Map(startB, y_at)
            t = {"qk": m("qk" + tag, [P, 6, n])}
            for k in ("dm", "ri", "ki", "kl", "rr"):
                t[k] = m(k + tag, [P, 3, n])
            t["klT"] = m("klT" + tag, [P, 3, P])
            t["vT"] = m("vT" + tag, [P, 6, P])
            t["pl"] = m("pl" + tag, [P, 3, 8])
            if n == P:
                t["s"] = m("sB", [P, 3, P])
                t["sw"] = m("swB", [P, 3, P])
            else:
                for k in range(2):
                    t["s0", k] = m(f"s0B{k}", [P, NSEQ, P])
                t["vm"] = m("vmB", [32, 2, NSEQ, P])
            return t

        tB = [maps_B(P, "Bp"), maps_B(32, "Bs")]
        sqB = Map(startB, y_at)("sqB", [P, BT, NT])

        def pool_B(pool, e, stored):
            pool.wait_ge(sem("mixer_done"), 2)
            pool.wait_ge(sem("kept_stored"), 16 * (GROUPS_A + GROUPS_B))
            for k in range(3):
                pool.dma_start(proj[:, 6 * k:6 * k + 6, 0:NT], projB[:, 6 * k:6 * k + 6, :]).then_inc(sem("projB_landed"), 16)
            e.need("state_whole")
            for par in range(2):
                pool.dma_start(o["gla_p"][0, 0].rearrange("(p r) k v -> r k p v", r=2)[par],
                               tB[0]["s"][64 * par:64 * par + 64, :, :]).then_inc(sem("out_stored"), 16)
            stored += 2
            pool.wait_ge(sem("out_stored"), 16 * stored)
            pool.nop().then_inc(sem("state_stored"), 2)
            rows = lambda x, p: x[0].rearrange("b h k v -> (h k) b v")[p * P:(p + 1) * P]
            return sample_states(pool, e, stored, tB[1], 3, "B",
                                 lambda p: rows(i["state_gla"], p), lambda p: rows(o["gla_s"], p))

        def pe_mixB(pe, weave):
            e = on(pe, "pe_chain")
            pe.wait_ge(sem("gk_landed"), 16)
            pe.wait_ge(sem("mixer_done"), 2)
            for p in range(3):
                mm = pe.matmul(ps[:, p, 0:NT], gkupB[:, p * P:(p + 1) * P], low[0:RANK, 1, :], start=True, stop=True)
            e.mark(mm, "B_gk")
            weave(U["bgk"])
            e.need("B_gx")
            for b in range(3):
                m, n, c, nch, t0, _ = kind(b)
                t = tB[b // 2]
                weave(U["bfeat"])
                e.need("feat")
                for par in range(2):
                    h = slice(64 * par, 64 * par + 64)
                    for p in range(3):
                        pe.matmul(ps[0:n, par, p * P:p * P + n], t["ki"][h, p, :], t["ri"][h, p, :], start=True, stop=True)
                for p in range(3):
                    mm = pe.transpose(ps[0:n, 2, p * P:(p + 1) * P], t["kl"][:, p, :], ident[:, :])
                for h in range(6):
                    mm = pe.transpose(cell(2, h, n, P), proj[:, 6 + h, t0:t0 + n], ident[:, :])
                e.mark(mm, "B_prod")
                weave(U["bprod"])
                e.need("mats")
                e.need("B_tok_kept")
                if n == P:
                    for j in range(nch):
                        u = slice(CP * j, CP * j + CP)
                        for par in range(2):
                            h = slice(64 * par, 64 * par + 64)
                            for p in range(3):
                                q, oc = 3 * par + p, slice(p * CP, (p + 1) * CP)
                                pe.matmul(ps[:, par, oc], t["s"][h, p, :], t["rr"][h, p, u], start=True, stop=False)
                                pe.matmul(ps[:, par, oc], t["vT"][u, 2 * p + par, :], t["qk"][u, q, u], start=False, stop=True)
                                mm = pe.matmul(ps[h, 3, p * P:(p + 1) * P], t["klT"][u, p, h], t["vT"][u, 2 * p + par, :], start=True, stop=True)
                        e.mark(mm, "sc_os")
                        weave(U["bsco"])
                        e.need("sc_s_kept")
                        e.need("sc_o_kept")
                else:
                    for p in range(3):
                        pe.wait_ge(sem(f"B_s0_{p % 2}"), 16 * (p // 2 + 1))
                        s0 = t["s0", p % 2]
                        for par in range(2):
                            h, q = slice(64 * par, 64 * par + 64), 3 * par + p
                            for k in range(NSEQ):
                                u = slice(TS * k, TS * k + TS)
                                pe.matmul(ps[:, par, u], s0[h, k, :], t["rr"][h, p, u], start=True, stop=True)
                            pe.matmul(ps[:, 2 + par, 0:32], t["vT"][0:32, 2 * p + par, :], t["qk"][0:32, q, :], start=True, stop=True)
                        e.need("B_vm")
                        for par in range(2):
                            h = slice(64 * par, 64 * par + 64)
                            for k in range(2):
                                mm = pe.matmul(ps[h, 4 + k, :].rearrange("p (b v) -> p b v", v=P), t["klT"][0:32, p, h],
                                               t["vm"][:, par, 4 * k:4 * k + 4, :], start=True, stop=True)
                        e.mark(mm, "B_ss_os")
                        weave(U["bsso"])
                        e.need("ss_s_kept")
            weave(U["bfin"])
            pe_head_norm(e, pe, "B", sqB)
            weave(U["bfin"])

        def act_mixB(act, weave):
            e = on(act, "act_chain")
            e.need("B_gx")
            e.link(act.activation(glB[:, :, :], glB[:, :, :], ACT.Exp, scale=-1.0))
            e.mark(act.activation(glB[:, :, :], glB[:, :, :], ACT.Ln, bias=ones[:, 0:1]), "B_gl")
            weave(U["bgk"])
            for b in range(3):
                m, n, c, nch, t0, _ = kind(b)
                t = tB[b // 2]
                inc, _, _, _, last = cums(csB, 0, b)
                e.need("diff")
                act.activation(t["ri"][:, :, :], t["dm"][:, :, :], ACT.Exp)
                act.activation(t["ki"][:, :, :], t["dm"][:, :, :], ACT.Exp, scale=-1.0)
                act.activation(t["kl"][:, :, :], t["kl"][:, :, :], ACT.Exp)
                act.activation(chunks(t["rr"][:, :, :], c), inc, ACT.Exp)
                e.mark(act.activation(t["pl"][:, :, 0:nch], last, ACT.Exp), "B_exps")
                weave(U["bfeat"])
                e.need("B_prod")
                act.activation(t["klT"][0:n, :, :], ps[0:n, 2, 0:3 * P].rearrange("p (h t) -> p h t", t=P), ACT.Copy)
                e.mark(act.activation(t["vT"][0:n, :, :], region(2, n, P), ACT.Copy), "B_tok_kept")
                weave(U["bprod"])
                if n == P:
                    for j in range(nch):
                        e.need("sc_os")
                        for par in range(2):
                            ins = act.activation(ybuf[:, YB + par:YB + 6:2, t0 + CP * j:t0 + CP * j + CP],
                                                 ps[:, par, 0:3 * CP].rearrange("p (h t) -> p h t", t=CP), ACT.Copy)
                        e.mark(ins, "sc_o_kept")
                        weave(U["bsco"])
                else:
                    for p in range(3):
                        e.need("B_ss_os")
                        for par in range(2):
                            ins = act.activation(ybuf[:, YB + 2 * p + par, t0:t0 + n], ps[:, par, 0:32], ACT.Copy)
                        e.mark(ins, "B_ss_o")
                        weave(U["bsso"])
            weave(U["bfin"])
            e.need("B_fin")
            e.link(act.activation(proj[:, 12:18, 0:NT], proj[:, 12:18, 0:NT], ACT.Silu))
            split_y(act, Y_ORDER[0:2 * BT])
            act_norm_tail(e, act, "B", sqB)
            weave(U["bfin"])
            act.wait_ge(sem("B_whole"), 1)
            split_y(act, Y_ORDER[2 * BT:])

        Y_ORDER = [y + k for y in Y_OF for k in range(BT)]

        def split_y(act, tiles):
            for k in tiles:
                act.activation(yh[:, k, :], ybuf[:, k, :], ACT.Copy).then_inc(sem("y_hi"), 1)

        def dve_mixB(dve, weave):
            e = on(dve, "dve_chain")
            e.need("B_gk")
            for p in range(3):
                e.link(dve.tensor_scalar(gxB[:, p, :], ps[:, p, 0:NT], par2[:, R_BIAS + p:R_BIAS + p + 1], None, ADD))
            e.mark(dve.scalar_tensor_tensor(glB[:, :, :], gxB[:, :, :], -1.0, gxB[:, :, :], MUL, ALU.max), "B_gx")
            weave(U["bgk"])
            e.need("B_gl")
            e.link(dve.scalar_tensor_tensor(gxB[:, :, :], gxB[:, :, :], 0.0, glB[:, :, :], ALU.min, SUB))
            e.link(dve.memset(padB[:, :], 0.0))
            lead = (TP // CP) * (CP + 1)
            for p in range(3):
                for c, lo_, hi_, s0, s1 in ((CP, 0, lead, 0, TP), (CS, lead, CW, TP, NT)):
                    e.link(dve.tensor_scalar(padB[:, lo_:hi_].rearrange("p (j t) -> p j t", t=c + 1)[:, :, 1:],
                                             gxB[:, p, s0:s1].rearrange("p (j t) -> p j t", t=c), 1.0 / 16, None, MUL))
                e.link(dve.tensor_tensor_scan(csB[:, p, :], notlead[:, :], padB[:, :], 0.0, MUL, ADD))
            e.link(dve.memset(tB[0]["s"][:, :, :], 0.0))
            for b in range(3):
                m, n, c, nch, t0, _ = kind(b)
                t = tB[b // 2]
                if b == 2:
                    dve.nop().then_inc(sem("state_whole"), 1)
                    dve.wait_ge(sem("state_stored"), 2)
                if b == 0:
                    dve.wait_ge(sem("projB_landed"), 48)
                inc, _, mid, end, _ = cums(csB, 0, b)
                C = lambda k: chunks(t[k][:, :, :], c)
                A = lambda k: t[k][:, :, :]
                e.link(dve.tensor_tensor(C("dm"), inc, mid, SUB))
                e.mark(dve.tensor_tensor(C("kl"), end, inc, SUB), "diff")
                e.need("B_exps")
                q_, k_ = proj[:, 0:3, t0:t0 + n], proj[:, 3:6, t0:t0 + n]
                e.link(dve.scalar_tensor_tensor(A("ri"), q_, 64 ** -0.5, A("ri"), MUL, MUL))
                e.link(dve.scalar_tensor_tensor(A("rr"), q_, 64 ** -0.5, A("rr"), MUL, MUL))
                e.link(dve.tensor_tensor(A("ki"), k_, A("ki"), MUL))
                e.mark(dve.tensor_tensor(A("kl"), k_, A("kl"), MUL), "feat")
                weave(U["bfeat"])
                e.need("B_prod")
                for par in range(2):
                    ins = dve.tensor_tensor(t["qk"][0:n, 3 * par:3 * par + 3, :], parity(0, par, n, n), bc(m["ui"][:, :], 1, 3), MUL)
                    if par:
                        e.mark(ins, "mats")
                    else:
                        e.link(ins)
                weave(U["bprod"])
                e.need("B_tok_kept")
                if n == P:
                    for j in range(nch):
                        s, sw = t["s"][:, :, :], t["sw"][:, :, :]
                        e.link(dve.tensor_tensor(sw, s, t["pl"][:, :, j:j + 1].to_broadcast([P, 3, P]), MUL))
                        e.need("sc_os")
                        e.mark(dve.tensor_tensor(s, ps[:, 3, 0:3 * P].rearrange("p (h t) -> p h t", t=P), sw, ADD), "sc_s_kept")
                        weave(U["bsco"])
                else:
                    for p in range(3):
                        for par in range(2):
                            ins = dve.tensor_tensor(t["vm"][:, par, :, :], bc(t["vT"][0:32, 2 * p + par, :], 1, NSEQ), bc(seqmask[:, :], 2, P), MUL)
                            if par:
                                e.mark(ins, "B_vm")
                            else:
                                e.link(ins)
                        weave(U["bsso"])
                        e.need("B_ss_os")
                        s0 = t["s0", p % 2][:, :, :]
                        e.link(dve.tensor_tensor(s0, s0, bc(t["pl"][:, p, :], 2, P), MUL))
                        e.mark(dve.tensor_tensor(s0, psf[:, 2048:3072].rearrange("p (b v) -> p b v", v=P), s0, ADD), "s_new")
                        e.need("B_ss_o")
                        for par in range(2):
                            yy = ybuf[:, YB + 2 * p + par, t0:t0 + n]
                            ins = dve.tensor_tensor(yy, ps[:, 2 + par, 0:32], yy, ADD)
                            if par:
                                e.mark(ins, "ss_s_kept")
                            else:
                                e.link(ins)
            weave(U["bfin"])
            dve.wait_ge(sem("s_stored"), 2)
            dve.nop().then_inc(sem("B_fin"), 1)
            def rest(k0, k1):
                for k in range(k0, k1):
                    y = Y_ORDER[k]
                    dve.wait_ge(sem("y_hi"), k + 1)
                    dve.tensor_tensor(yl[:, y, :], ybuf[:, y, :], yh[:, y, :].bitcast(F32), SUB).then_inc(sem("y_ready"), 1)

            dve_head_norm(e, dve, "B", sqB, proj[:, 12:18, 0:NT], YB, R_GLA, rest)
            weave(U["bfin"])
            dve.nop().then_inc(sem("B_whole"), 1)
            rest(2 * BT, 3 * BT)
            dve.wait_ge(sem("y_ready"), 3 * BT)


        vectors = [("norm_ff1", R_FF1, 16), ("norm_mix", R_MIX, 16), ("norm_ff2", R_FF2, 16),
                   ("norm_final", R_FIN, 16), ("rwkv_mu", R_MU, 20), ("rwkv_w0", R_W0, 6),
                   ("rwkv_a0", R_A0, 6), ("rwkv_k_k", R_KK, 6), ("rwkv_k_a", R_KA, 6),
                   ("rwkv_r_k", R_RK, 6), ("rwkv_ln_w", R_LNW, 6), ("rwkv_ln_b", R_LNB, 6),
                   ("gdn_norm", R_GDN, 1), ("gla_norm", R_GLA, 1)]
        PROWS = len(vectors) + 2

        def pool_program(pool):
            made = [0]

            def chain(ins):
                made[0] += 1
                ins.then_inc(sem("pool_chain"), 1)
                pool.wait_ge(sem("pool_chain"), made[0])

            def keep(t, conds, fill=0.0):
                for cond, b0, pattern, mult in conds:
                    chain(pool.affine_select(out=t, in_=t, compare_op=cond, fill=fill, base=b0,
                                             pattern=pattern, channel_multiplier=mult))

            GE = ALU.is_ge
            for name, r, n in vectors:
                v = i[name]
                if len(v.shape) == 2:
                    v = v[0]
                pool.dma_start(prow[r:r + n, 0, :], v.rearrange("(a b) -> a b", b=P)).then_inc(sem("prow_landed"), 16)
            pool.dma_start(prow[0:72, 1, :], i["conv_a"][0].rearrange("j (a b) -> (j a) b", b=P)).then_inc(sem("prow_landed"), 16)
            pool.dma_start(prow[R_BIAS:R_BIAS + 3, 1, :], i["gla_gk_bias"][0].rearrange("(a b) -> a b", b=P)).then_inc(sem("prow_landed"), 16)
            chain(pool.memset(ones[:, :], 1.0))
            chain(pool.memset(ident[:, :], 0.0))
            keep(ident[:, :], [(ALU.not_equal, 0, [[-1, P]], 1)], fill=1.0)
            pool.nop().then_inc(sem("consts"), 1)
            chain(pool.memset(ones64[:, :], 1.0))
            keep(ones64[:, :], [(GE, 0, [[-64, 2], [0, 64]], 1), (GE, 63, [[64, 2], [0, 64]], -1)])
            for m, w, c in ((mk[0], P, CP), (mk[1], 32, CS)):
                for k in m:
                    chain(pool.memset(m[k][:, :], 1.0))
                v = {k: m[k][:, :] for k in m}
                after = (GE, 0, [[-c, w // c], [0, c]], 1)
                before = (GE, c - 1, [[c, w // c], [0, c]], -1)
                keep(v["ui"], [(GE, 0, [[1, w]], -1), after])
                keep(v["us"], [(GE, -1, [[1, w]], -1), after])
                keep(v["same"], [after, before])
                h = min(c, 16)
                keep(v["l16"], [(GE, -1, [[-1, w]], 1), (GE, h - 1, [[h, w // h], [0, h]], -1)])
                keep(v["off"], [(GE, -1, [[-1, w]], 1), before])
                chain(pool.tensor_tensor(v["off"], v["off"], v["l16"], SUB))
            chain(pool.memset(seqmask[:, :], 1.0))
            keep(seqmask[:, :], [(GE, 0, [[-TS, NSEQ]], 1), (GE, TS - 1, [[TS, NSEQ]], -1)])
            chain(pool.memset(notlead[:, :], 1.0))
            lead = (TP // CP) * (CP + 1)
            chain(pool.memset(notlead[:, 0:lead].rearrange("p (c t) -> p c t", t=CP + 1)[:, :, 0:1], 0.0))
            chain(pool.memset(notlead[:, lead:CW].rearrange("p (c t) -> p c t", t=CS + 1)[:, :, 0:1], 0.0))
            chain(pool.memset(kept[:, :, :], 0.0))
            pool.nop().then_inc(sem("consts"), 1)
            pool_mixers(pool)

        block = ctx.enter_context(nc.Block())

        @block.sync
        def _(sp):
            sp_program(sp)

        @block.gpsimd
        def _(pool):
            pool_program(pool)

        @block.scalar
        def _(act):
            act_program(act)

        @block.vector
        def _(dve):
            dve_program(dve)

        @block.tensor
        def _(pe):
            pe_program(pe)


INS = ["x_prompt", "x_sample", "state_gdn", "state_gdn_conv", "state_gla", "state_rwkv", "state_rwkv_shift",
       "w_in", "conv_a", "a_log", "dt_bias", "gdn_norm", "gla_gk_up", "gla_gk_bias", "gla_norm",
       "rwkv_mu", "rwkv_w0", "rwkv_w_up", "rwkv_a0", "rwkv_a_up", "rwkv_g_up", "rwkv_k_k", "rwkv_k_a",
       "rwkv_r_k", "rwkv_ln_w", "rwkv_ln_b", "w_branch", "w_out", "norm_ff1", "w_ff1_up", "w_ff1_down",
       "norm_mix", "norm_ff2", "w_ff2_up", "w_ff2_down", "norm_final"]
OUTS = [("y_prompt", (1, TP, D)), ("y_sample", (NSEQ, TS, D)),
        ("gdn_p", (1, 1, 6, 128, 128)), ("gdn_s", (1, NSEQ, 6, 128, 128)),
        ("conv_p", (1, 1, 3, 2304)), ("conv_s", (1, NSEQ, 3, 2304)),
        ("gla_p", (1, 1, 6, 64, 128)), ("gla_s", (1, NSEQ, 6, 64, 128)),
        ("rwkv_p", (1, 1, 12, 64, 64)), ("rwkv_s", (1, NSEQ, 12, 64, 64)),
        ("shift_p", (1, 1, 1, N_C)), ("shift_s", (1, NSEQ, 1, N_C))]


def kernel(**inputs):
    import numpy as np
    import concourse.bacc as bacc
    from concourse.bass_utils import run_bass_kernel_spmd

    nc = bacc.Bacc("TRN2", target_bir_lowering=False, num_devices=1)
    arrays, ins, outs = {}, {}, {}
    for name in INS:
        a = np.ascontiguousarray(inputs[name])
        arrays[f"in_{name}"] = a
        ins[name] = nc.dram_tensor(f"in_{name}", a.shape, mybir.dt.from_np(a.dtype), kind="ExternalInput").ap()
    for name, shape in OUTS:
        outs[name] = nc.dram_tensor(f"out_{name}", shape, F32, kind="ExternalOutput").ap()
    build(nc, ins, outs)
    r = run_bass_kernel_spmd(nc, [arrays], core_ids=[0])
    return tuple(r.results[0][f"out_{name}"] for name, _ in OUTS)
```
